# Optimizing a Trainium2 kernel written in Bass

```python
import jax, jax.numpy as jnp
from jax import lax
import numpy as np
import math

D_MODEL = 1024
BATCH = 1
SEQ = 512
DEPTH = 1

HEAD_DIM = 64
D_MIX = D_MODEL
D_CONV = D_MIX // 2
D_ATTN = D_MIX - D_CONV
N_HEADS = D_ATTN // HEAD_DIM
CONV_WIDTH = 3
DILATED_BRANCHES = ((128, 1), (512, 4), (2048, 16))
BLOCK = 128
D_FF = ((-(-8 * D_MODEL // 3) + 255) // 256) * 256
D_IN = 3 * D_CONV + 3 * D_ATTN
EPS = 1e-6


def rms_norm(x, g):
    xf = x.astype(jnp.float32)
    y = xf * lax.rsqrt(jnp.mean(xf * xf, axis=-1, keepdims=True) + EPS)
    return (y * g.astype(jnp.float32)).astype(x.dtype)

def short_conv(u, w):
    return lax.conv_general_dilated(
        u, w[:, None, :].astype(u.dtype), window_strides=(1,),
        padding=[(CONV_WIDTH - 1, 0)], dimension_numbers=("NWC", "WIO", "NWC"),
        feature_group_count=u.shape[-1])

def dilated_branch(q, k, v, window, dil):
    B, S, H, dh = q.shape
    M = S // dil
    L = window // dil
    nb = -(-M // BLOCK)
    Mp = nb * BLOCK
    pad = Mp - M

    def to_sub(t):
        return t.reshape(B, M, dil, H, dh).transpose(0, 2, 1, 3, 4).reshape(B * dil, M, H, dh)

    qs, ks, vs = to_sub(q), to_sub(k), to_sub(v)
    Bd = B * dil
    qb = jnp.pad(qs, ((0, 0), (0, pad), (0, 0), (0, 0))).reshape(Bd, nb, BLOCK, H, dh)

    def band(t):
        tp = jnp.pad(t, ((0, 0), (BLOCK, pad), (0, 0), (0, 0)))
        prev = tp[:, :Mp].reshape(Bd, nb, BLOCK, H, dh)
        cur = tp[:, BLOCK:].reshape(Bd, nb, BLOCK, H, dh)
        return jnp.concatenate([prev, cur], axis=2)

    kw, vw = band(ks), band(vs)
    s = jnp.einsum("bnqhd,bnkhd->bnhqk", qb, kw, preferred_element_type=jnp.float32)

    i = jnp.arange(BLOCK)[:, None]
    j = jnp.arange(2 * BLOCK)[None, :]
    dist = BLOCK + i - j
    kpos = (jnp.arange(nb)[:, None, None] - 1) * BLOCK + j[None]
    valid = ((dist >= 0) & (dist <= L))[None] & (kpos >= 0)
    s = jnp.where(valid[None, :, None], s, -jnp.inf)

    m = jnp.max(s, axis=-1, keepdims=True)
    e = jnp.exp(s - m)
    den = jnp.sum(e, axis=-1, keepdims=True)
    p = e / den
    lse = (m + jnp.log(den))[..., 0]
    o = jnp.einsum("bnhqk,bnkhd->bnqhd", p.astype(vw.dtype), vw)

    o = o.reshape(Bd, Mp, H, dh)[:, :M]
    lse = lse.transpose(0, 1, 3, 2).reshape(Bd, Mp, H)[:, :M]
    o = o.reshape(B, dil, M, H, dh).transpose(0, 2, 1, 3, 4).reshape(B, S, H, dh)
    lse = lse.reshape(B, dil, M, H).transpose(0, 2, 1, 3).reshape(B, S, H)
    return o, lse

def dilated_mixture(q, k, v):
    outs, lses = [], []
    for window, dil in DILATED_BRANCHES:
        o, lse = dilated_branch(q, k, v, window, dil)
        outs.append(o)
        lses.append(lse)
    w = jax.nn.softmax(jnp.stack(lses, axis=0), axis=0)
    o = jnp.sum(w[..., None] * jnp.stack(outs, axis=0).astype(jnp.float32), axis=0)
    return o.astype(q.dtype)

def first_inputs(seed: int = 0) -> dict:
    key = jax.random.key(seed)
    ks = jax.random.split(key, 13)
    f32 = jnp.float32

    def gain(k_, n):
        return 1.0 + 0.05 * jax.random.normal(k_, (DEPTH, n), f32)

    return {
        "x": jax.random.normal(ks[0], (BATCH, SEQ, D_MODEL), f32),
        "g_mix": gain(ks[1], D_MODEL),
        "w_in": jax.random.normal(ks[2], (DEPTH, D_MODEL, D_IN), f32) * D_MODEL ** -0.5,
        "conv_w": jax.random.normal(ks[3], (DEPTH, CONV_WIDTH, D_CONV), f32) * CONV_WIDTH ** -0.5,
        "g_q": gain(ks[4], HEAD_DIM),
        "g_k": gain(ks[5], HEAD_DIM),
        "g_conv_out": gain(ks[6], D_CONV),
        "g_attn_out": gain(ks[7], D_ATTN),
        "w_out": jax.random.normal(ks[8], (DEPTH, D_MIX, D_MODEL), f32) * D_MIX ** -0.5,
        "g_ffn": gain(ks[9], D_MODEL),
        "w_gate": jax.random.normal(ks[10], (DEPTH, D_MODEL, D_FF), f32) * D_MODEL ** -0.5,
        "w_up": jax.random.normal(ks[11], (DEPTH, D_MODEL, D_FF), f32) * D_MODEL ** -0.5,
        "w_down": jax.random.normal(ks[12], (DEPTH, D_FF, D_MODEL), f32) * D_FF ** -0.5,
    }

def first_block(x, g_mix, w_in, conv_w, g_q, g_k, g_conv_out, g_attn_out, w_out,
              g_ffn, w_gate, w_up, w_down):
    B, S, _ = x.shape
    splits = [D_CONV, 2 * D_CONV, 3 * D_CONV, 3 * D_CONV + D_ATTN, 3 * D_CONV + 2 * D_ATTN]
    for l in range(DEPTH):
        h = rms_norm(x, g_mix[l])
        z = h @ w_in[l]
        u, gb, gc, q, k, v = jnp.split(z, splits, axis=-1)

        y_conv = gb * short_conv(gc * u, conv_w[l])

        q = rms_norm(q.reshape(B, S, N_HEADS, HEAD_DIM), g_q[l]) * (HEAD_DIM ** -0.5)
        k = rms_norm(k.reshape(B, S, N_HEADS, HEAD_DIM), g_k[l])
        v = v.reshape(B, S, N_HEADS, HEAD_DIM)
        y_attn = dilated_mixture(q, k, v).reshape(B, S, D_ATTN)

        mix = jnp.concatenate([rms_norm(y_conv, g_conv_out[l]),
                               rms_norm(y_attn, g_attn_out[l])], axis=-1)
        x = x + mix @ w_out[l]

        h = rms_norm(x, g_ffn[l])
        x = x + (jax.nn.silu(h @ w_gate[l]) * (h @ w_up[l])) @ w_down[l]
    return x


SSM_WIDTH = D_MODEL // 2
SSM_GROUP = 16
SSM_GROUPS = SSM_WIDTH // SSM_GROUP
SSM_STATE = 64
SSM_CHUNK_MAX = 512
DT_MIN = 1e-3
DT_MAX = 1e-1
ATTN_HEADS = 8
ATTN_WIDTH = ATTN_HEADS * HEAD_DIM
IDX_HEADS = 8
IDX_DIM = 64
IDX_SCALE = (IDX_HEADS * IDX_DIM) ** -0.5
TOPK_MAX = 256
Q_BLOCK = 128
RMS_EPS = 1e-6

IN_WIDTHS = (
    SSM_WIDTH,
    SSM_WIDTH,
    ATTN_WIDTH,
    HEAD_DIM,
    HEAD_DIM,
    ATTN_WIDTH,
    IDX_HEADS * IDX_DIM,
    IDX_DIM,
    IDX_HEADS,
    D_MODEL,
    D_MODEL,
)
IN_COLS = sum(IN_WIDTHS)
IN_SPLITS = tuple(int(s) for s in np.cumsum(IN_WIDTHS)[:-1])


def rms_norm_2(x, g):
    x32 = x.astype(jnp.float32)
    y = x32 * lax.rsqrt(jnp.mean(x32 * x32, axis=-1, keepdims=True) + RMS_EPS)
    return (y * g.astype(jnp.float32)).astype(x.dtype)

def _complex_affine_combine(e1, e2):
    a1r, a1i, b1r, b1i = e1
    a2r, a2i, b2r, b2i = e2
    return (a1r * a2r - a1i * a2i,
            a1r * a2i + a1i * a2r,
            a2r * b1r - a2i * b1i + b2r,
            a2r * b1i + a2i * b1r + b2i)

def s5_mixer(u, a_re, a_im, b_re, b_im, c_re, c_im, d_skip, log_dt):
    bsz, seq_len, _ = u.shape
    f32 = jnp.float32
    ar, ai = a_re.astype(f32), a_im.astype(f32)
    dt = jnp.exp(log_dt.astype(f32))[:, None]
    mag = jnp.exp(ar * dt)
    abar_r, abar_i = mag * jnp.cos(ai * dt), mag * jnp.sin(ai * dt)
    den = ar * ar + ai * ai
    nr = abar_r - 1.0
    cr = (nr * ar + abar_i * ai) / den
    ci = (abar_i * ar - nr * ai) / den
    br, bi = b_re.astype(f32), b_im.astype(f32)
    bb_r = cr[..., None] * br - ci[..., None] * bi
    bb_i = cr[..., None] * bi + ci[..., None] * br
    cre, cim = c_re.astype(f32), c_im.astype(f32)

    chunk = math.gcd(seq_len, SSM_CHUNK_MAX)
    n_chunks = seq_len // chunk
    ug = u.astype(f32).reshape(bsz, n_chunks, chunk, SSM_GROUPS, SSM_GROUP)
    ug = ug.transpose(1, 0, 2, 3, 4)

    def chunk_step(h0, u_c):
        h0r, h0i = h0
        bu_r = jnp.einsum('btgp,gnp->btgn', u_c, bb_r)
        bu_i = jnp.einsum('btgp,gnp->btgn', u_c, bb_i)
        a_r = jnp.broadcast_to(abar_r, bu_r.shape)
        a_i = jnp.broadcast_to(abar_i, bu_i.shape)
        cum_r, cum_i, hl_r, hl_i = lax.associative_scan(
            _complex_affine_combine, (a_r, a_i, bu_r, bu_i), axis=1)
        h_r = hl_r + cum_r * h0r[:, None] - cum_i * h0i[:, None]
        h_i = hl_i + cum_r * h0i[:, None] + cum_i * h0r[:, None]
        y = (jnp.einsum('btgn,gpn->btgp', h_r, cre)
             - jnp.einsum('btgn,gpn->btgp', h_i, cim))
        return (h_r[:, -1], h_i[:, -1]), y

    h_init = (jnp.zeros((bsz, SSM_GROUPS, SSM_STATE), f32),
              jnp.zeros((bsz, SSM_GROUPS, SSM_STATE), f32))
    _, y = lax.scan(chunk_step, h_init, ug)
    y = y.transpose(1, 0, 2, 3, 4).reshape(bsz, seq_len, SSM_WIDTH)
    y = y + d_skip.astype(f32) * u.astype(f32)
    return y.astype(u.dtype)

def dsa_mixer(q, k, v, q_idx, k_idx, w_idx):
    bsz, seq_len = q.shape[0], q.shape[1]
    f32 = jnp.float32
    top_k = min(TOPK_MAX, seq_len // 4)
    n_blocks = seq_len // Q_BLOCK
    key_pos = jnp.arange(seq_len)
    k_idx32 = k_idx.astype(f32)
    attn_scale = HEAD_DIM ** -0.5

    def to_blocks(t):
        return t.reshape((bsz, n_blocks, Q_BLOCK) + t.shape[2:]).swapaxes(0, 1)

    def block(args):
        blk, qb, qib, wb = args
        q_pos = blk * Q_BLOCK + jnp.arange(Q_BLOCK)
        causal = key_pos[None, :] <= q_pos[:, None]
        s = jax.nn.relu(jnp.einsum('bqhd,bkd->bqhk', qib.astype(f32), k_idx32)) * IDX_SCALE
        score = jnp.einsum('bqh,bqhk->bqk', wb.astype(f32), s)
        score = jnp.where(causal[None], score, -jnp.inf)
        _, sel = lax.top_k(score, top_k)
        valid = sel <= q_pos[None, :, None]
        k_sel = jax.vmap(lambda kk, ii: kk[ii])(k, sel)
        v_sel = jax.vmap(lambda vv, ii: vv[ii])(v, sel)
        logits = jnp.einsum('bqhd,bqkd->bqhk', qb.astype(f32), k_sel.astype(f32)) * attn_scale
        logits = jnp.where(valid[:, :, None, :], logits, -jnp.inf)
        p = jax.nn.softmax(logits, axis=-1)
        o = jnp.einsum('bqhk,bqkd->bqhd', p, v_sel.astype(f32))
        return o.astype(qb.dtype)

    out = lax.map(block, (jnp.arange(n_blocks), to_blocks(q), to_blocks(q_idx), to_blocks(w_idx)))
    return out.swapaxes(0, 1).reshape(bsz, seq_len, ATTN_WIDTH)

def hybrid_layer(x, c, norm_g, w_mod, b_mod, w_in, a_re, a_im, b_re, b_im, c_re, c_im,
                 d_skip, log_dt, w_glu, b_glu, w_a_o, w_b_o, w_out):
    bsz, seq_len, _ = x.shape
    mod = jax.nn.silu(c) @ w_mod + b_mod
    shift, scale, gate = jnp.split(mod, 3, axis=-1)
    h = rms_norm_2(x, norm_g) * (1 + scale[:, None]) + shift[:, None]
    proj = h @ w_in
    xa, za, q, k, v, zb, qi, ki, wi, ga, gb = jnp.split(proj, IN_SPLITS, axis=-1)

    ya = jax.nn.gelu(s5_mixer(xa, a_re, a_im, b_re, b_im, c_re, c_im, d_skip, log_dt))
    g = ya @ w_glu + b_glu
    ya = g[..., :SSM_WIDTH] * jax.nn.sigmoid(g[..., SSM_WIDTH:])
    ya = (ya * jax.nn.silu(za)) @ w_a_o

    yb = dsa_mixer(q.reshape(bsz, seq_len, ATTN_HEADS, HEAD_DIM), k, v,
                   qi.reshape(bsz, seq_len, IDX_HEADS, IDX_DIM), ki, wi)
    yb = (yb * jax.nn.silu(zb)) @ w_b_o

    merged = jax.nn.sigmoid(ga) * ya + jax.nn.sigmoid(gb) * yb
    return x + gate[:, None] * (merged @ w_out)

def second_inputs(seed: int = 0) -> dict:
    key = jax.random.key(seed)
    ks = jax.random.split(key, 20)
    f32 = jnp.float32
    G, N, P = SSM_GROUPS, SSM_STATE, SSM_GROUP

    def nrm(k, shape, std):
        return jax.random.normal(k, shape, f32) * std

    n_idx = jnp.arange(N, dtype=f32)
    return {
        "x": nrm(ks[0], (BATCH, SEQ, D_MODEL), 1.0),
        "c": nrm(ks[1], (BATCH, D_MODEL), 1.0),
        "norm_g": 1.0 + nrm(ks[2], (DEPTH, D_MODEL), 0.02),
        "w_mod": nrm(ks[3], (DEPTH, D_MODEL, 3 * D_MODEL), 0.5 * D_MODEL ** -0.5),
        "b_mod": nrm(ks[4], (DEPTH, 3 * D_MODEL), 0.01),
        "w_in": nrm(ks[5], (DEPTH, D_MODEL, IN_COLS), D_MODEL ** -0.5),
        "a_re": -0.5 + nrm(ks[6], (DEPTH, G, N), 0.01),
        "a_im": math.pi * n_idx + nrm(ks[7], (DEPTH, G, N), 0.01),
        "b_re": nrm(ks[8], (DEPTH, G, N, P), (2 * P) ** -0.5),
        "b_im": nrm(ks[9], (DEPTH, G, N, P), (2 * P) ** -0.5),
        "c_re": nrm(ks[10], (DEPTH, G, P, N), N ** -0.5),
        "c_im": nrm(ks[11], (DEPTH, G, P, N), N ** -0.5),
        "d_skip": nrm(ks[12], (DEPTH, SSM_WIDTH), 1.0),
        "log_dt": jax.random.uniform(ks[13], (DEPTH, G), f32,
                                     minval=math.log(DT_MIN), maxval=math.log(DT_MAX)),
        "w_glu": nrm(ks[14], (DEPTH, SSM_WIDTH, 2 * SSM_WIDTH), SSM_WIDTH ** -0.5),
        "b_glu": nrm(ks[15], (DEPTH, 2 * SSM_WIDTH), 0.01),
        "w_a_o": nrm(ks[16], (DEPTH, SSM_WIDTH, D_MODEL), SSM_WIDTH ** -0.5),
        "w_b_o": nrm(ks[17], (DEPTH, ATTN_WIDTH, D_MODEL), ATTN_WIDTH ** -0.5),
        "w_out": nrm(ks[18], (DEPTH, D_MODEL, D_MODEL), D_MODEL ** -0.5),
        "final_g": 1.0 + nrm(ks[19], (D_MODEL,), 0.02),
    }

def second_block(x, c, norm_g, w_mod, b_mod, w_in, a_re, a_im, b_re, b_im, c_re, c_im,
              d_skip, log_dt, w_glu, b_glu, w_a_o, w_b_o, w_out, final_g):
    for l in range(DEPTH):
        x = hybrid_layer(x, c, norm_g[l], w_mod[l], b_mod[l], w_in[l], a_re[l], a_im[l],
                         b_re[l], b_im[l], c_re[l], c_im[l], d_skip[l], log_dt[l],
                         w_glu[l], b_glu[l], w_a_o[l], w_b_o[l], w_out[l])
    return rms_norm_2(x, final_g)


def setup_inputs(seed=0):
    out = dict(first_inputs(seed))
    for name, value in second_inputs(seed + 1).items():
        if name != "x":
            out[name + "_2"] = value
    return out


def reference(
    x, g_mix, w_in, conv_w, g_q, g_k, g_conv_out, g_attn_out, w_out, g_ffn, w_gate, w_up,
    w_down, c_2, norm_g_2, w_mod_2, b_mod_2, w_in_2, a_re_2, a_im_2, b_re_2, b_im_2, c_re_2,
    c_im_2, d_skip_2, log_dt_2, w_glu_2, b_glu_2, w_a_o_2, w_b_o_2, w_out_2, final_g_2,
):
    x = first_block(
        x, g_mix, w_in, conv_w, g_q, g_k, g_conv_out, g_attn_out, w_out, g_ffn, w_gate, w_up,
        w_down,
    )
    return second_block(
        x, c_2, norm_g_2, w_mod_2, b_mod_2, w_in_2, a_re_2, a_im_2, b_re_2, b_im_2, c_re_2,
        c_im_2, d_skip_2, log_dt_2, w_glu_2, b_glu_2, w_a_o_2, w_b_o_2, w_out_2, final_g_2,
    )


_drawn_inputs = setup_inputs


def setup_inputs(seed=0):
    import zlib

    import numpy as np

    out = dict(_drawn_inputs(seed))
    spreads = {}
    factors = {'norm_g_2': 8.0,
     'b_mod_2': 8.0,
     'a_re_2': 64.0,
     'a_im_2': 64.0,
     'b_re_2': 64.0,
     'b_im_2': 64.0,
     'c_re_2': 64.0,
     'c_im_2': 64.0,
     'log_dt_2': 64.0,
     'b_glu_2': 57.596}
    for name, (base, spread) in spreads.items():
        noise = np.random.default_rng([zlib.crc32(name.encode()), seed]).standard_normal(out[name].shape)
        drawn = base * np.exp(spread * noise) if base else spread * noise
        out[name] = __import__('jax').numpy.asarray(drawn.astype(out[name].dtype))
    for name, factor in factors.items():
        out[name] = (out[name] * factor).astype(out[name].dtype)
    return out
```

```python
import concourse.bass as bass
from concourse import mybir
from contextlib import ExitStack
import numpy as np

F32 = mybir.dt.float32
F32R = mybir.dt.float32r
I32 = mybir.dt.int32
ALU = mybir.AluOpType
ACT = mybir.ActivationFunctionType
AX = mybir.AxisListType

P = 128
S = 512
TB = S // P
D = 1024
KD = D // P
HALF = D // 2
KH = HALF // P
HD = 64
NPAIR = 4
FF = ((-(-8 * D // 3) + 255) // 256) * 256
KF = FF // P
EPS = 1e-6
NEG = -1e30
GONE = -3e38
TOPK = min(256, S // 4)
ROUNDS = TOPK // 8
IDX_SCALE = float((8 * 64) ** -0.5)
G2, NST, GP = 32, 64, 16
NCH = G2 * NST // P
LEVELS = 9
MIX_STEPS, S5_STEPS = 9, 68

Z_U, Z_GB, Z_GC, Z_Q, Z_K, Z_V = (j * HALF for j in range(6))
Y_XA, Y_ZA, Y_Q, Y_K, Y_ZB, Y_QI, Y_KI, Y_WI = 0, 512, 1024, 1536, 1664, 2176, 2688, 2752
Y_GA, Y_GB = 2760, 3784
NKI = Y_GA - Y_KI

N_MIX = 0
N_WO = N_MIX + 24
N_FF = N_WO + KD
N_DN = N_FF + 2 * KF
N_KV = N_DN + KF
N_IX = N_KV + 2
N_S5 = N_IX + 2 * NPAIR
N_AT = N_S5 + 24
N_AB = N_AT + 8
N_O2 = N_AB + 8
N_END = N_O2 + KD

CB = [0, 128, 384, 768, 1280]
OFF = [0, 512, 896, 1152, 1280]

V_GMIX, V_CONV, V_GCONV, V_GATT, V_GFFN, V_C, V_NG, V_BMOD, V_BGLU, V_DSK, V_FG, V_GQ, V_GK = \
    0, 8, 20, 24, 28, 36, 44, 52, 76, 84, 88, 96, 97
NV1 = 98
W_ARE, W_AIM, W_LDT = 0, 16, 32
NV2 = 48

C_ID, C_DG, C_BD, C_M1, C_END = 0, 128, 256, 384, 896


def constants():
    i = np.arange(P)[:, None]
    d = i - np.arange(S)[None, :] + (S - P)
    c = ((d >= 0) & (d <= 128)) * 1 + ((d >= 0) & (d % 4 == 0)) + ((d >= 0) & (d % 16 == 0))
    m1 = np.where(c > 0, np.log(np.maximum(c, 1)), NEG)
    j = np.arange(P)[None, :]
    dg = np.where(j <= i, 0.0, 1.0)
    bd = (i // HD == j // HD) * 1.0
    return np.concatenate([np.eye(P), dg, bd, m1], 1).astype(np.float32)


def gfree_count(n):
    return n // 2 - (KF // 2 if n >= N_KV else 0)


class Steps:

    def __init__(self, eng, sem):
        self.eng, self.sem, self.base, self.k, self.i, self.per = eng, sem, 0, 0, None, 0

    def mark(self, ins):
        ins.then_inc(self.sem, 1)
        self.k += 1
        return self.k

    def need(self, k=None):
        k = self.k if k is None else k
        self.eng.wait_ge(self.sem, self.base + k if self.i is None else self.i * self.per + (self.base + k))

    def enter(self, i, per):
        self.base, self.k, self.i, self.per = self.base + self.k, 0, i, per

    def leave(self, times):
        assert self.k == self.per, ("steps in the loop's body", self.k)
        self.base, self.k, self.i = self.base + self.per * times, 0, None


def program(nc, io):
    (x, g_mix, w_in, conv_w, g_q, g_k, g_conv_out, g_attn_out, w_out, g_ffn, w_gate, w_up, w_down,
     c_2, norm_g_2, w_mod_2, b_mod_2, w_in_2, a_re_2, a_im_2, b_re_2, b_im_2, c_re_2, c_im_2,
     d_skip_2, log_dt_2, w_glu_2, b_glu_2, w_a_o_2, w_b_o_2, w_out_2, final_g_2, consts) = io[:-1]
    out = io[-1]
    e_dram = nc.dram_tensor("rotations", [NCH, P, 2, S], F32, kind="Internal").ap()

    with ExitStack() as ctx:
        base = (nc.sbuf_base + 63) // 64 * 64
        top = [base]

        def at(name, shape, dt=F32, off=None):
            size = 4 * int(np.prod(shape[1:]))
            if off is None:
                off = top[0]
                top[0] += (size + 31) // 32 * 32
            return nc.alloc_sbuf_tensor_at(name, shape, dt, offset=off)

        def sem(name):
            return ctx.enter_context(nc.semaphore(name))

        PB = [ctx.enter_context(nc.psum_tensor(f"bank{b}", [P, S], F32)) for b in range(8)]
        SB, TBANK, OB = (PB[4], PB[5]), (PB[6], PB[2]), PB[7]

        xT = at("xT", [P, KD, S])
        hH, hL = at("hH", [P, KD, S], F32R), at("hL", [P, KD, S], F32R)
        raw = [at(f"raw{s}", [P, 1024]) for s in range(2)]
        wH = [at(f"wH{s}", [P, 1024], F32R) for s in range(2)]
        wL = [at(f"wL{s}", [P, 1024], F32R) for s in range(2)]
        cst = at("cst", [P, C_M1])
        vec, svec = at("vec", [P, NV1]), at("svec", [P, NV2])
        ones = at("ones", [P, P])
        epst = at("epst", [P, 1])
        csil, mod, gs = at("csil", [P, KD]), at("mod", [P, 3 * KD]), at("gs", [P, KD])
        mx, nmx, rs, rinv = (at(n, [P, 8]) for n in ("mx", "nmx", "rs", "rinv"))
        sm = at("sm", [P, 24])
        sp = at("sp", [P, 20, NCH])
        spi = at("spi", [P, NCH], I32)
        hbg, ldt = at("hbg", [P, KH]), at("ldt", [P, 2])
        m8 = at("m8", [P, 3, 8])
        ident, diag, bdones = cst[:, C_ID:C_DG], cst[:, C_DG:C_BD], cst[:, C_BD:C_M1]
        A0 = top[0]
        aH, aL = at("aH", [P, KF, S], F32R, A0), at("aL", [P, KF, S], F32R, A0 + 4 * KF * S)
        x_tok, xn_tok = at("x_tok", [P, TB, D], F32, A0), at("xn_tok", [P, TB, D], F32, A0 + 16384)
        row1, row2 = at("row1", [P, P], F32, A0 + 32768), at("row2", [P, P], F32, A0 + 33280)
        names = ["qraw", "kraw", "vT", "u_s", "sqq", "sqk", "rq", "rk", "cv", "yc", "sqc", "yo", "sqa"]
        (qraw, kraw, vT, u_s, sqq, sqk, rq, rk, cv, yc, sqc, yo, sqa) = (
            at(n, [P, S], F32, A0 + 2048 * j) for j, n in enumerate(names))
        cuP = at("cuP", [P, S + 2], F32, A0 + 2048 * 13)
        mixH, mixL = at("mixH", [P, KD, S], F32R, A0 + 32768), at("mixL", [P, KD, S], F32R, A0 + 49152)
        macc = at("macc", [P, 3 * D], F32, A0 + 65536)
        mraw = [at(f"mraw{s}", [P, D], F32, A0 + 77824 + 4096 * s) for s in range(2)]
        ssc, ssa = at("ssc", [P, S], F32, A0 + 86016), at("ssa", [P, S], F32, A0 + 88064)
        rc, ra = at("rc", [P, S], F32, A0), at("ra", [P, S], F32, A0 + 2048)
        nt1, nt2 = at("nt1", [P, S], F32, A0 + 4096), at("nt2", [P, S], F32, A0 + 6144)
        wo1, wo2 = at("wo1", [P, S], F32, A0 + 8192), at("wo2", [P, S], F32, A0 + 10240)
        tga, tgb = at("tga", [P, KD, S], F32, A0), at("tgb", [P, KD, S], F32, A0 + 16384)
        szb, sza = at("szb", [P, KH, S], F32, A0 + 32768), at("sza", [P, KH, S], F32, A0 + 40960)
        ebuf = [at(f"ebuf{s}", [P, 2, S], F32, A0 + 49152 + 4096 * s) for s in range(2)]
        S0 = A0 + 57344
        braw = at("braw", [P, 2, NCH, GP], F32, S0)
        bdg = at("bdg", [P, 2, NCH, 2 * GP], F32, S0 + 2048)
        bbT = at("bbT", [P, 2, KH, P], F32, S0 + 6144)
        craw = at("craw", [P, 2, KH, NST], F32, S0 + 10240)
        cTt = at("cTt", [P, 2, NCH, 2 * GP], F32, S0 + 12288)
        yaH, yaL = at("yaH", [P, KH, S], F32R, A0 + 73728), at("yaL", [P, KH, S], F32R, A0 + 81920)
        y2H, y2L = at("y2H", [P, KH, S], F32R, A0 + 49152), at("y2L", [P, KH, S], F32R, A0 + 57344)
        ybH = at("ybH", [P, KH, S], F32R, A0 + 65536)
        out_tok = at("out_tok", [P, TB, D], F32, A0)
        B0 = A0 + 90112
        L = at("L", [P, 2, CB[4]], F32, B0)
        pT = at("pT", [P, 2, CB[4]], F32, B0 + 10240)
        qn, kn = at("qn", [P, S], F32, B0 + 20480), at("kn", [P, S], F32, B0 + 22528)
        vtok = at("vtok", [P, TB, P], F32, B0 + 24576)
        score, work = at("score", [P, CB[4]], F32, B0 + 26624), at("work", [P, CB[4]], F32, B0 + 31744)
        relu_b = [at(f"relu{s}", [P, S], F32, B0 + 36864 + 2048 * s) for s in range(2)]
        ybL = at("ybL", [P, KH, S], F32R, B0 + 31744)
        r1, gt, ut, sg, a32, sqx = (at(n, [P, S], F32, B0 + 26624 + 2048 * j) for j, n in
                                    enumerate(("r1", "gt", "ut", "sg", "a32", "sqx")))
        ss1 = at("ss1", [P, S], F32, B0 + 38912)
        eb = at("eb", [P, 2, 2, S], F32, B0)
        et = [at(f"et{j}", [P, 2, S // 2], F32, B0 + 8192 + 2048 * j) for j in range(4)]
        bbS, dgS = at("bbS", [P, 2, P], F32, B0 + 24576), at("dgS", [P, P], F32, B0 + 25600)
        cpS = at("cpS", [P, 4, 2, P], F32, B0 + 36864)
        thg = at("thg", [P, S], F32, B0 + 24576)
        k2, yg = at("k2", [P, S], F32, B0 + 40960), at("yg", [P, S], F32, B0 + 40960)
        t1, t2, t3, t4, gr, gi, hr0, hr1, hi0, hi1 = (
            at(n, [P, S], F32, B0 + 2048 * j) for j, n in
            enumerate(("t1", "t2", "t3", "t4", "gr", "gi", "hr0", "hr1", "hi0", "hi1")))
        kvraw, kiraw = at("kvraw", [P, S], F32, B0), at("kiraw", [P, S], F32, B0 + 2048)
        xaS = at("xaS", [P, S], F32, B0 + 20480)
        mask1 = at("mask1", [P, S], F32, B0 + 40960)
        pw = at("pw", [P, 2, LEVELS, NCH], F32, B0 + 43008)
        vt2 = at("vt2", [P, TB, HD], F32, B0 + 43008)
        wtok = at("wtok", [P, TB, 8], F32, B0 + 44032)
        assert B0 + 44160 <= nc.sbuf_usable_end

        x_in, cst_in, mask_in, glu_full, vec_in, s5_in, out_done = (
            sem(n) for n in ("x_in", "cst_in", "mask_in", "glu_full", "vec_in", "s5_in", "out_done"))
        w_full = [sem(f"w_full{s}") for s in range(2)]
        hi_done, lo_done = sem("hi_done"), sem("lo_done")
        slot_used = sem("slot_used")
        gfree = [sem(f"gfree{s}") for s in range(2)]
        m_full = [sem(f"m_full{s}") for s in range(2)]
        m_used = sem("m_used")
        vstep, astep, pstep = sem("vstep"), sem("astep"), sem("pstep")
        pe_pre, pre_done, init_v, init_a = (sem(n) for n in ("pe_pre", "pre_done", "init_v", "init_a"))
        ss0, r0d, xn_done, hin_done, vec_rdy, s5_cv = (
            sem(n) for n in ("ss0", "r0d", "xn_done", "hin_done", "vec_rdy", "s5_cv"))
        ss_mm, ss_rd, rs_rdy, qn_rdy = (sem(n) for n in ("ss_mm", "ss_rd", "rs_rdy", "qn_rdy"))
        vtr, vt_done, ych = sem("vtr"), sem("vt_done"), sem("ych")
        sc_ready, sc_free, nm, ex, pn = (sem(n) for n in ("sc_ready", "sc_free", "nm", "ex", "pn"))
        tr_mm, t_free, pv, o_free, yo_rdy = (sem(n) for n in ("tr_mm", "t_free", "pv", "o_free", "yo_rdy"))
        ssum, ssm, rr, nt_done = (sem(n) for n in ("ssum", "ssm", "rr", "nt_done"))
        x1_rdy, x1h, x1l = sem("x1_rdy"), sem("x1h"), sem("x1l")
        sg_rdy, a32_rdy, ah_rdy, a_done, dn_done = (sem(n) for n in ("sg_rdy", "a32_rdy", "ah_rdy", "a_done", "dn_done"))
        mod_mm, pw_rdy, e_out = sem("mod_mm"), sem("pw_rdy"), sem("e_out")
        sq2_rdy, h2f, h2h, h2_done = (sem(n) for n in ("sq2_rdy", "h2f", "h2h", "h2_done"))
        trig_a, trig_r = sem("trig_a"), sem("trig_r")
        kdup, bd_rdy, s5_tr, s5_ev, s5w = (sem(n) for n in ("kdup", "bd_rdy", "s5_tr", "s5_ev", "s5w"))
        kv_tr, kv_ev, ix_ready, relu_rdy, r_used = (sem(n) for n in ("kv_tr", "kv_ev", "ix_ready", "relu_rdy", "r_used"))
        bu_done, bu_free, h_rdy, y_mm, y_free, yg_rdy, ya_h, ya_done = (
            sem(n) for n in ("bu_done", "bu_free", "h_rdy", "y_mm", "y_free", "yg_rdy", "ya_h", "ya_done"))
        e_full = [sem(f"e_full{s}") for s in range(2)]
        e_used = sem("e_used")
        th_rdy, y2h, y2_done, ybh, yb_done = (
            sem(n) for n in ("th_rdy", "y2h", "y2_done", "ybh", "yb_done"))
        mg_rdy, mgh, mg_done = sem("mg_rdy"), sem("mgh"), sem("mg_done")
        x3_rdy, xf_rdy, xf_tr, ot_done, fin = (sem(n) for n in ("x3_rdy", "xf_rdy", "xf_tr", "ot_done", "fin"))

        def wait(eng, s, v):
            if not (isinstance(v, int) and v <= 0):
                eng.wait_ge(s, v)

        class Slot:

            def __init__(self, first, j=0, per=0, i=0):
                c = first + j
                self.par = c % 2
                self.n = c + per * i if isinstance(i, int) else i * per + c
                self.half = c // 2 + per // 2 * i if isinstance(i, int) else i * (per // 2) + c // 2
                self.gf = self.half - (KF // 2 if c >= N_KV else 0)

            def next(self, k=2):
                s = Slot(0)
                s.par, s.n, s.half, s.gf = self.par, self.n + k, self.half + k // 2, self.gf + k // 2
                return s

        def settled(eng):
            eng.nop(nofuse=True)

        def freed(eng, s):
            eng.wait_ge(gfree[s.par], s.gf + 1)

        def blk(t, k):
            return t[:, k * P:(k + 1) * P]

        block = ctx.enter_context(nc.Block())

        @block.sync
        def _(sp_):
            for t in range(TB):
                sp_.dma_start(x_tok[:, t, :], x[0, t * P:(t + 1) * P, :]).then_inc(x_in, 16)

            def cols(w, c, n=P):
                return w[0].rearrange("(k p) c -> p k c", p=P)[:, :, bass.ds(c, n)]

            def load(s, src, width=P, shape=KD):
                wait(sp_, lo_done, s.n - 1)
                dst = raw[s.par][:].rearrange("p (k c) -> p k c", k=shape)[:, :, 0:width]
                sp_.dma_start(dst, src).then_inc(w_full[s.par], 16)

            for j, z in enumerate((Z_Q, Z_K, Z_V)):
                load(Slot(N_MIX, j), cols(w_in, z))

            def mix(i, last):
                for j, z in enumerate((Z_U, Z_GC, Z_GB)):
                    load(Slot(3, j, 6, i), cols(w_in, i * P + z))
                if not last:
                    for j, z in enumerate((Z_Q, Z_K, Z_V)):
                        load(Slot(3, 3 + j, 6, i), cols(w_in, i * P + (z + P)))
            with sp_.Fori(0, NPAIR - 1) as i:
                mix(i, False)
            mix(NPAIR - 1, True)
            with sp_.Fori(0, KD // 2) as i:
                for s in range(2):
                    load(Slot(N_WO, s, 2, i), cols(w_out, i * (2 * P) + s * P))
            with sp_.Fori(0, KF) as i:
                load(Slot(N_FF, 0, 2, i), cols(w_gate, i * P))
                load(Slot(N_FF, 1, 2, i), cols(w_up, i * P))
            with sp_.Fori(0, KF // 2) as i:
                for s in range(2):
                    load(Slot(N_DN, s, 2, i), w_down[0][bass.ds(i * (2 * P) + s * P, P), :]
                         .rearrange("p (k c) -> p k c", k=KD))
            load(Slot(N_KV, 0), cols(w_in_2, Y_K))
            load(Slot(N_KV, 1), cols(w_in_2, Y_KI, NKI), NKI)
            with sp_.Fori(0, NPAIR) as i:
                load(Slot(N_IX, 0, 2, i), cols(w_in_2, i * P + Y_QI))
                load(Slot(N_IX, 1, 2, i), cols(w_in_2, i * P + Y_ZB))
            load(Slot(N_S5), cols(w_in_2, Y_XA))

            def s5(j, last):
                for k in range(2):
                    load(Slot(N_S5 + 1, 2 * k, 6, j), cols(w_in_2, j * (2 * P) + (k * P + Y_GA)))
                    load(Slot(N_S5 + 1, 2 * k + 1, 6, j), cols(w_in_2, j * (2 * P) + (k * P + Y_GB)))
                load(Slot(N_S5 + 1, 4, 6, j), cols(w_in_2, j * P + Y_ZA))
                if not last:
                    load(Slot(N_S5 + 1, 5, 6, j), cols(w_in_2, j * P + (Y_XA + P)))
            with sp_.Fori(0, KH - 1) as j:
                s5(j, False)
            s5(KH - 1, True)
            load(Slot(N_AT), cols(w_in_2, Y_Q))

            def at_(i, last):
                s = Slot(N_AT + 1, 0, 2, i)
                wait(sp_, lo_done, s.n - 1)
                for e in range(2):
                    dst = raw[s.par][:].rearrange("p (k e c) -> p k e c", k=KH, e=2)[:, :, e, :]
                    src = w_glu_2[0].rearrange("(k p) c -> p k c", p=P)[:, :, bass.ds(i * P + e * HALF, P)]
                    sp_.dma_start(dst, src).then_inc(glu_full if e else w_full[s.par], 16)
                if not last:
                    load(Slot(N_AT + 1, 1, 2, i), cols(w_in_2, i * P + (Y_Q + P)))
            with sp_.Fori(0, NPAIR - 1) as i:
                at_(i, False)
            at_(NPAIR - 1, True)
            with sp_.Fori(0, KD // 2) as i:
                load(Slot(N_AB, 0, 2, i), cols(w_a_o_2, i * (2 * P), 2 * P), 2 * P, KH)
                load(Slot(N_AB, 1, 2, i), cols(w_b_o_2, i * (2 * P), 2 * P), 2 * P, KH)
            with sp_.Fori(0, KD // 2) as i:
                for s in range(2):
                    load(Slot(N_O2, s, 2, i), cols(w_out_2, i * (2 * P) + s * P))
            for t in range(TB):
                sp_.wait_ge(fin, t + 1)
                sp_.dma_start(out[0, t * P:(t + 1) * P, :], out_tok[:, t, :]).then_inc(out_done, 16)
            sp_.wait_ge(out_done, 16 * TB)

        @block.gpsimd
        def _(pool):
            g = nc.gpsimd
            pool.dma_start(cst[:], consts[:, 0:C_M1]).then_inc(cst_in, 16)
            pool.dma_start(mask1[:], consts[:, C_M1:C_END]).then_inc(mask_in, 16)
            rows = [(g_mix, V_GMIX, 8), (g_conv_out, V_GCONV, 4), (g_attn_out, V_GATT, 4), (g_ffn, V_GFFN, 8),
                    (c_2, V_C, 8), (norm_g_2, V_NG, 8), (b_mod_2, V_BMOD, 24), (b_glu_2, V_BGLU, 8),
                    (d_skip_2, V_DSK, 4)]
            for v, r, n in rows:
                pool.dma_start(row1[r:r + n, :], v.rearrange("a (n p) -> (a n) p", p=P)).then_inc(vec_in, 16)
            pool.dma_start(row1[V_CONV:V_CONV + 12, :],
                           conv_w.rearrange("a w (n p) -> (a w n) p", p=P)).then_inc(vec_in, 16)
            pool.dma_start(row1[V_FG:V_FG + 8, :], final_g_2.rearrange("(n p) -> n p", p=P)).then_inc(vec_in, 16)
            for r, v in ((V_GQ, g_q), (V_GK, g_k)):
                for e in range(2):
                    pool.dma_start(row1[r:r + 1, e * HD:(e + 1) * HD], v).then_inc(vec_in, 16)
            for r, v in ((W_ARE, a_re_2), (W_AIM, a_im_2)):
                pool.dma_start(row2[r:r + NCH, :], v[0].rearrange("(s g) n -> s (g n)", g=2)).then_inc(vec_in, 16)
            pool.dma_start(ldt[W_LDT:W_LDT + NCH, :], log_dt_2[0].rearrange("(s g) -> s g", g=2)).then_inc(vec_in, 16)

            with pool.Fori(0, NPAIR) as i:
                for m in range(6):
                    pool.wait_ge(m_used, i * 6 + (m + 1))
                    pool.dma_start(mraw[m % 2][:], w_mod_2[0][bass.ds(i * (2 * P) + (m // 3) * P, P),
                                                             (m % 3) * D:(m % 3 + 1) * D]).then_inc(m_full[m % 2], 16)

            pool.wait_ge(pw_rdy, 1)
            pool.wait_ge(pv, 2 * NPAIR)
            st = Steps(pool, pstep)
            with pool.Fori(0, NCH // 2) as i:
                st.enter(i, 1 + 6 * LEVELS)
                wait(pool, e_out, i * 32)
                settled(pool)
                g.memset(eb[:, :, 0, 0:1], 1.0)
                st.mark(g.memset(eb[:, :, 1, 0:1], 0.0))
                for k in range(LEVELS):
                    n = 1 << k
                    st.need()
                    c, s = eb[:, :, 0, 0:n], eb[:, :, 1, 0:n]
                    wc, ws = (pw[:, e, k, bass.ds(i * 2, 2)].unsqueeze(2).broadcast_to([P, 2, n]) for e in range(2))
                    m = [t[:, :, 0:n] for t in et]
                    st.mark(g.tensor_tensor(m[0], c, wc, ALU.mult))
                    st.mark(g.tensor_tensor(m[1], s, ws, ALU.mult))
                    st.mark(g.tensor_tensor(m[2], c, ws, ALU.mult))
                    last = st.mark(g.tensor_tensor(m[3], s, wc, ALU.mult))
                    st.need(last - 2)
                    st.mark(g.tensor_tensor(eb[:, :, 0, n:2 * n], m[0], m[1], ALU.subtract))
                    st.need(last)
                    st.mark(g.tensor_tensor(eb[:, :, 1, n:2 * n], m[2], m[3], ALU.add))
                st.need()
                for c in range(2):
                    pool.dma_start(e_dram[bass.ds(i * 2 + c, 1)].rearrange("a p e t -> (a p) e t"),
                                   eb[:, c]).then_inc(e_out, 16)
                st.leave(NCH // 2)

            pool.wait_ge(slot_used, N_DN + KF)
            for e, (b, c) in enumerate(((b_re_2, c_re_2), (b_im_2, c_im_2))):
                pool.dma_start(braw[:, e], b[0].rearrange("(s g) n p -> (g n) s p", g=2)).then_inc(s5_in, 16)
                pool.dma_start(craw[:, e], c[0].rearrange("(k g) p n -> (g p) k n", g=8)).then_inc(s5_in, 16)
            pool.wait_ge(e_out, 16 * NCH)
            pool.wait_ge(s5_ev, 2)
            pool.wait_ge(s5_cv, 1)
            pool.wait_ge(r_used, 6 * NPAIR + 2)
            m = st.mark(g.memset(cpS[:], 0.0))
            st.need(m)

            def s5(j):
                wait(pool, y_mm, j * 4)
                g.tensor_copy(bbS[:], bbT[:, :, bass.ds(j, 1), :].rearrange("p e j n -> p e (j n)"))
                g.tensor_tensor(dgS[:], ident, vec[:, bass.ds(j + V_DSK, 1)].broadcast_to([P, P]), ALU.mult)
                for c in range(4):
                    ins = g.tensor_copy(cpS[:, c, :, 32 * c:32 * c + 32],
                                        cTt[:, :, bass.ds(j * 4 + c, 1), :].rearrange("p e j n -> p e (j n)"))
                ins.then_inc(s5w, 1)
                for c in range(4):
                    pool.wait_ge(e_used, j * 4 + (c + 1))
                    pool.dma_start(ebuf[c % 2][:], e_dram[bass.ds(j * 4 + c, 1)]
                                   .rearrange("a p e t -> (a p) e t")).then_inc(e_full[c % 2], 16)
            with pool.Fori(0, KH) as j:
                s5(j)

        @block.tensor
        def _(pe):
            mm = nc.tensor.matmul

            def transposes(dst, srcs, idn=ident):
                for t, src in enumerate(srcs):
                    m, kk = src.shape[1], src.shape[0]
                    ins = nc.tensor.transpose(dst[0:m, t * P:t * P + kk], src, idn[0:kk, 0:kk])
                return ins

            def products(s, terms):
                pe.wait_ge(lo_done, s.n + 1)
                for k, rh, rl, o, a, z in terms:
                    mm(o, blk(wH[s.par], k), rh, start=a, stop=False)
                    mm(o, blk(wH[s.par], k), rl, start=False, stop=False)
                    ins = mm(o, blk(wL[s.par], k), rh, start=False, stop=z)
                ins.then_inc(slot_used, 1)

            def project(s, m=P):
                wait(pe, gfree[s.par], s.gf)
                pe.wait_ge(lo_done, s.n + 1)
                o = PB[s.par][0:m, :]
                for k in range(KD):
                    a, b = wH[s.par][:, k * P:k * P + m], wL[s.par][:, k * P:k * P + m]
                    mm(o, a, hH[:, k, :], start=(k == 0), stop=False)
                    mm(o, a, hL[:, k, :], start=False, stop=False)
                    ins = mm(o, b, hH[:, k, :], start=False, stop=(k == KD - 1))
                ins.then_inc(slot_used, 1)

            def scores(a, q, k):
                for hh in range(2):
                    r = slice(HD * hh, HD * hh + HD)
                    for b in range(TB):
                        u = 4 * hh + b
                        pe.wait_ge(sc_free, a * 8 + (u + 1))
                        mm(SB[u % 2][:, 0:P * (b + 1)], q[r, blkc(b)], k[r, 0:P * (b + 1)],
                           start=True, stop=True).then_inc(sc_ready, 1)

            def blkc(b):
                return slice(b * P, (b + 1) * P)

            def attend(a, v, vcol):
                for hh in range(2):
                    pe.wait_ge(pn, a * 2 + (hh + 1))
                    for kb in range(TB):
                        pe.wait_ge(t_free, a * 8 + (4 * hh + kb + 1))
                        transposes(TBANK[kb % 2], [L[:, hh, CB[b] + P * kb:CB[b] + P * kb + P] for b in range(kb, TB)]
                                   ).then_inc(tr_mm, 1)
                wait(pe, o_free, a)
                for hh in range(2):
                    r = slice(HD * hh, HD * hh + HD)
                    pe.wait_ge(t_free, a * 8 + (4 * hh + 4 + 2))
                    for kb in range(TB):
                        ins = mm(OB[r, P * kb:S], v[:, kb, vcol(hh)], pT[:, hh, OFF[kb]:OFF[kb + 1]],
                                 start=(kb == 0), stop=(kb == TB - 1), skip_group_check=True)
                    ins.then_inc(pv, 1)

            pe.wait_ge(cst_in, 16)
            pe.wait_ge(vec_in, 16 * 18)
            pe.wait_ge(r0d, 1)
            nc.tensor.transpose(PB[6][:, 0:NV1], row1[0:NV1, :], ident[0:NV1, 0:NV1]).then_inc(pe_pre, 1)
            nc.tensor.transpose(PB[7][:, 0:NV2], row2[0:NV2, :], ident[0:NV2, 0:NV2]).then_inc(pe_pre, 1)
            for f in range(2 * KD):
                src = xn_tok if f < KD else x_tok
                if f == 0:
                    pe.wait_ge(xn_done, 1)
                wait(pe, pre_done, f - 1)
                transposes(PB[f % 2], [src[:, t, (f % KD) * P:(f % KD) * P + P] for t in range(TB)]).then_inc(pe_pre, 1)
            pe.wait_ge(pre_done, 2 * KD)

            def qkv(first, i):
                for j in range(3):
                    project(Slot(first, j, 6, i))

            def head_sums(a, ks):
                freed(pe, ks)
                wait(pe, vt_done, a)
                for e, sq in enumerate((sqq, sqk)):
                    wait(pe, ss_rd, a * 2 + e)
                    mm(PB[3][:], bdones, sq[:], start=True, stop=True).then_inc(ss_mm, 1)

            def mix(i, last):
                for j in range(3):
                    project(Slot(3, j, 6, i))
                pe.wait_ge(ss_rd, i * 2 + 2)
                freed(pe, Slot(2, 0, 6, i))
                transposes(PB[3], [vT[:, blkc(b)] for b in range(TB)]).then_inc(vtr, 1)
                pe.wait_ge(qn_rdy, i + 1)
                scores(i, qn, kn)
                if not last:
                    qkv(6, i)
                pe.wait_ge(vt_done, i + 1)
                attend(i, vtok, lambda hh: slice(HD * hh, HD * hh + HD))
                if not last:
                    head_sums(i + 1, Slot(7, 0, 6, i))

            qkv(0, 0)
            freed(pe, Slot(0, 2))
            head_sums(0, Slot(1))
            with pe.Fori(0, NPAIR - 1) as i:
                mix(i, False)
            mix(NPAIR - 1, True)

            pe.wait_ge(ssum, 1)
            mm(PB[4][:], ones[:], ssc[:], start=True, stop=True).then_inc(ssm, 1)
            pe.wait_ge(ssum, 2)
            mm(PB[5][:], ones[:], ssa[:], start=True, stop=True).then_inc(ssm, 1)
            for c in range(3 * KD):
                ins = mm(PB[6][:, c:c + 1], macc[:, blkc(c)], ones[:, 0:1], start=True, stop=True)
            ins.then_inc(mod_mm, 1)
            with pe.Fori(0, KD // 2) as i:
                for s in range(2):
                    sl = Slot(N_WO, s, 2, i)
                    pe.wait_ge(gfree[s], sl.gf)
                    products(sl, [(k, mixH[:, k, :], mixL[:, k, :], PB[s if k < KH else 2 + s][:], k % KH == 0,
                                   k % KH == KH - 1) for k in range(KD)])

            pe.wait_ge(x1l, KD)
            pe.wait_ge(ssum, 3)
            mm(PB[4][:], ones[:], ss1[:], start=True, stop=True).then_inc(ssm, 1)
            with pe.Fori(0, KF) as i:
                for s in range(2):
                    project(Slot(N_FF, s, 2, i))
            pe.wait_ge(a_done, KF)

            def down(i, first, last):
                for s in range(2):
                    sl = Slot(N_DN, s, 2, i)
                    pe.wait_ge(lo_done, sl.n + 1)
                    kf = i * 2 + s
                    rh, rl = (t[:, bass.ds(kf, 1), :].rearrange("p k t -> p (k t)") if not isinstance(i, int)
                              else t[:, kf, :] for t in (aH, aL))
                    for d in range(KD):
                        a, z = first and s == 0, last and s == 1
                        mm(PB[d][:], blk(wH[s], d), rh, start=a, stop=False, skip_group_check=True)
                        mm(PB[d][:], blk(wH[s], d), rl, start=False, stop=False, skip_group_check=True)
                        ins = mm(PB[d][:], blk(wL[s], d), rh, start=False, stop=z, skip_group_check=True)
                        if z and d < KD - 1:
                            ins.then_inc(dn_done, 1)
                    ins.then_inc(slot_used, 1)
            down(0, True, False)
            with pe.Fori(1, KF // 2 - 1) as i:
                down(i, False, False)
            down(KF // 2 - 1, False, True)

            pe.wait_ge(ssum, 4)
            mm(PB[4][:], ones[:], ss1[:], start=True, stop=True).then_inc(ssm, 1)
            pe.wait_ge(h2_done, KD)
            project(Slot(N_KV, 0))
            project(Slot(N_KV, 1), NKI)
            pe.wait_ge(bd_rdy, 1)
            for e in range(2):
                transposes(PB[6 + e], [bdg[:, e, 4 * j:4 * j + 4, :].rearrange("p s q -> p (s q)") for j in range(KH)]
                           ).then_inc(s5_tr, 1)
            for e in range(2):
                transposes(PB[4 + e], [craw[:, e, k, :] for k in range(KH)]).then_inc(s5_tr, 1)
            freed(pe, Slot(N_KV, 0))
            transposes(PB[3], [kvraw[:, blkc(b)] for b in range(TB)]).then_inc(kv_tr, 1)
            freed(pe, Slot(N_KV, 1))
            transposes(PB[2], [kiraw[0:NKI, blkc(b)] for b in range(TB)]).then_inc(kv_tr, 1)
            pe.wait_ge(s5_cv, 1)
            pe.wait_ge(kdup, 2)

            with pe.Fori(0, NPAIR) as i:
                project(Slot(N_IX, 0, 2, i))
                project(Slot(N_IX, 1, 2, i))
                freed(pe, Slot(N_IX, 0, 2, i))
                for hh in range(2):
                    r = slice(HD * hh, HD * hh + HD)
                    for b in range(1, TB):
                        u = 3 * hh + b - 1
                        pe.wait_ge(relu_rdy, i * 6 + (u + 1))
                        mm(SB[u % 2][:, 0:P * (b + 1)], qn[r, blkc(b)], k2[r, 0:P * (b + 1)],
                           start=True, stop=True).then_inc(ix_ready, 1)

            project(Slot(N_S5))
            freed(pe, Slot(N_S5))
            pe.wait_ge(kv_ev, 2)
            pe.wait_ge(relu_rdy, 6 * NPAIR + 2)

            def y_out(j, c):
                pe.wait_ge(h_rdy, j * 4 + (c + 1))
                for e, h in enumerate(((hr0, hr1)[c % 2], (hi0, hi1)[c % 2])):
                    ins = mm(OB[:], cpS[:, c, e, :], h[:], start=False, stop=(c == 3 and e == 1), skip_group_check=True)
                ins.then_inc(y_mm, 1)

            def s5(j, last):
                pe.wait_ge(s5w, j + 1)
                wait(pe, y_free, j)
                freed(pe, Slot(N_S5, 0, 6, j))
                mm(OB[:], dgS[:], xaS[:], start=True, stop=False, skip_group_check=True)
                for c in range(4):
                    project(Slot(N_S5 + 1, c, 6, j))
                    pe.wait_ge(bu_free, j * 4 + (c + 1))
                    r = slice(32 * c, 32 * c + 32)
                    for e in range(2):
                        ins = mm((SB if c % 2 == 0 else TBANK)[e][:], bbS[r, e, :], xaS[r, :], start=True, stop=True)
                    ins.then_inc(bu_done, 1)
                    if c:
                        y_out(j, c - 1)
                project(Slot(N_S5 + 1, 4, 6, j))
                y_out(j, 3)
                if not last:
                    project(Slot(N_S5 + 1, 5, 6, j))
            with pe.Fori(0, KH - 1) as j:
                s5(j, False)
            s5(KH - 1, True)

            project(Slot(N_AT))
            freed(pe, Slot(N_AT))
            pe.wait_ge(bu_free, NCH + 2)
            pe.wait_ge(y_free, KH)
            scores(NPAIR, qn, kn)
            pe.wait_ge(ya_done, KH)

            def att(i, last):
                sl = Slot(N_AT + 1, 0, 2, i)
                pe.wait_ge(gfree[1], sl.gf)
                products(sl, [(2 * k + e, yaH[:, k, :], yaL[:, k, :], PB[1 + 2 * e][:], k == 0, k == KH - 1)
                              for e in range(2) for k in range(KH)])
                if not last:
                    project(Slot(N_AT + 1, 1, 2, i))
                attend(i + NPAIR, vt2, lambda hh: slice(0, HD))
                if not last:
                    freed(pe, Slot(N_AT + 1, 1, 2, i))
                    scores(i + (NPAIR + 1), qn, kn)
            with pe.Fori(0, NPAIR - 1) as i:
                att(i, False)
            att(NPAIR - 1, True)

            pe.wait_ge(y2_done, KH)
            pe.wait_ge(yb_done, KH)
            with pe.Fori(0, KD // 2) as i:
                for s, (rh, rl) in enumerate(((y2H, y2L), (ybH, ybL))):
                    sl = Slot(N_AB, s, 2, i)
                    pe.wait_ge(gfree[s], sl.gf)
                    products(sl, [(2 * k + e, rh[:, k, :], rl[:, k, :], PB[s + 2 * e][:], k == 0, k == KH - 1)
                                  for e in range(2) for k in range(KH)])
            pe.wait_ge(mg_done, KD)
            with pe.Fori(0, KD // 2) as i:
                project(Slot(N_O2, 0, 2, i))
                project(Slot(N_O2, 1, 2, i))
                for s in range(2):
                    pe.wait_ge(xf_rdy, i * 2 + (s + 1))
                    wait(pe, ot_done, i * 2)
                    transposes(TBANK[s], [(t3, t4)[s][:, blkc(b)] for b in range(TB)]).then_inc(xf_tr, 1)
            pe.wait_ge(ssum, 5)
            for t in range(TB):
                ins = mm(PB[4][:, t:t + 1], gr[:, blkc(t)], ones[:, 0:1], start=True, stop=True)
            ins.then_inc(ssm, 1)

        @block.scalar
        def _(act):
            A = nc.scalar.activation

            def copy(o, i_, scale=1.0):
                return A(o, i_, ACT.Copy, scale=scale)

            def split_hi(s):
                act.wait_ge(w_full[s.par], s.half * 16 + 16)
                wait(act, slot_used, s.n - 1)
                copy(wH[s.par][:], raw[s.par][:]).then_inc(hi_done, 1)

            def used(s):
                act.wait_ge(slot_used, s.n + 1)

            def rsqrt(o, ps, scale, k, done):
                act.wait_ge(ssm, k)
                A(o, ps, ACT.Ln, bias=epst[:, 0:1], scale=scale).then_inc(astep, 1)
                a_n[0] += 1
                act.wait_ge(astep, a_n[0])
                A(o, o, ACT.Exp, scale=-0.5).then_inc(done, 1)
            a_n = [0]

            act.wait_ge(init_v, 1)
            act.wait_ge(x_in, 16 * TB)
            for t in range(TB):
                ins = A(xn_tok[:, t, :], x_tok[:, t, :], ACT.Square, accum_out=sm[:, t:t + 1])
            ins.then_inc(astep, 1)
            a_n[0] += 1
            act.wait_ge(astep, a_n[0])
            A(sm[:, 4:8], sm[:, 0:4], ACT.Ln, bias=epst[:, 0:1], scale=1.0 / D).then_inc(astep, 1)
            a_n[0] += 1
            act.wait_ge(astep, a_n[0])
            A(sm[:, 8:12], sm[:, 4:8], ACT.Exp, scale=-0.5).then_inc(ss0, 1)
            split_hi(Slot(0))
            split_hi(Slot(1))
            act.wait_ge(vec_rdy, 1)
            for k in range(KD):
                act.wait_ge(pe_pre, 2 + k + 1)
                A(hH[:, k, :], PB[k % 2][:], ACT.Identity, scale=vec[:, V_GMIX + k:V_GMIX + k + 1]).then_inc(hin_done, 1)
            A(csil[:], vec[:, V_C:V_C + KD], ACT.Silu).then_inc(trig_a, 1)
            act.wait_ge(trig_r, 1)
            A(sp[:, 6:8, :], sp[:, 4:6, :], ACT.Sin).then_inc(trig_a, 1)

            def qkv(first, i, a):
                s = [Slot(first, j, 6, i) for j in range(3)]
                wait(act, qn_rdy, a)
                wait(act, ss_mm, a * 2)
                for sl, dst, sq in ((s[0], qraw, sqq), (s[1], kraw, sqk)):
                    used(sl)
                    copy(dst[:], PB[sl.par][:])
                    A(sq[:], PB[sl.par][:], ACT.Square).then_inc(gfree[sl.par], 1)
                    split_hi(sl.next())
                used(s[2])
                wait(act, vtr, a)
                copy(vT[:], PB[s[2].par][:]).then_inc(gfree[s[2].par], 1)
                split_hi(s[2].next())

            def head_rsqrt(a):
                for e, r in enumerate((rq, rk)):
                    act.wait_ge(ss_mm, a * 2 + (e + 1))
                    A(r[:], PB[3][:], ACT.Ln, bias=epst[:, 0:1], scale=1.0 / HD).then_inc(ss_rd, 1)
                    act.wait_ge(ss_rd, a * 2 + (e + 1))
                    A(r[:], r[:], ACT.Exp, scale=-0.5).then_inc(rs_rdy, 1)

            def softmax(a):
                for hh in range(2):
                    act.wait_ge(nm, a * 2 + (hh + 1))
                    for b in range(TB):
                        c = 4 * hh + b
                        l = L[:, hh, CB[b]:CB[b + 1]]
                        ins = A(l, l, ACT.Exp, bias=nmx[:, c:c + 1], accum_out=rs[:, c:c + 1])
                    ins.then_inc(ex, 1)

            def p_evac(a):
                for hh in range(2):
                    for kb in range(TB):
                        act.wait_ge(tr_mm, a * 8 + (4 * hh + kb + 1))
                        n = S - P * kb
                        copy(pT[:, hh, OFF[kb]:OFF[kb + 1]], TBANK[kb % 2][:, 0:n]).then_inc(t_free, 1)

            def mix(i, last):
                head_rsqrt(i)
                u, gc, gb = (Slot(3, j, 6, i) for j in range(3))
                used(u)
                if not (isinstance(i, int) and i == 0):
                    wait(act, ych, i)
                copy(u_s[:], PB[u.par][:]).then_inc(gfree[u.par], 1)
                split_hi(u.next())
                used(gc)
                split_hi(gc.next())
                used(gb)
                split_hi(gb.next())
                freed(act, gb)
                A(sqc[:], yc[:], ACT.Square)
                A(dyn(mixH, i), yc[:], ACT.Identity, scale=vec[:, bass.ds(i + V_GCONV, 1)]).then_inc(ych, 1)
                act.wait_ge(vtr, i + 1)
                copy(vtok[:].rearrange("p b n -> p (b n)"), PB[3][:]).then_inc(vt_done, 1)
                softmax(i)
                if not last:
                    qkv(6, i, i + 1)
                p_evac(i)
                act.wait_ge(pv, i * 2 + 2)
                copy(yo[:], OB[:])
                A(sqa[:], OB[:], ACT.Square)
                A(dyn(mixH, i + KH), OB[:], ACT.Identity, scale=vec[:, bass.ds(i + V_GATT, 1)]).then_inc(o_free, 1)

            def dyn(t, k):
                return t[:, k, :] if isinstance(k, int) else t[:, bass.ds(k, 1), :].rearrange("p k t -> p (k t)")

            act.nop().then_inc(t_free, 1)
            act.nop().then_inc(t_free, 1)
            qkv(0, 0, 0)
            with act.Fori(0, NPAIR - 1) as i:
                mix(i, False)
            mix(NPAIR - 1, True)

            rsqrt(rc[:], PB[4][:], 1.0 / HALF, 1, rr)
            rsqrt(ra[:], PB[5][:], 1.0 / HALF, 2, rr)
            with act.Fori(0, KD // 2) as i:
                for s in range(2):
                    sl, d = Slot(N_WO, s, 2, i), i * 2 + s
                    used(sl)
                    split_hi(sl.next())
                    act.wait_ge(x1_rdy, d + 1)
                    A(sqx[:], dyn(xT, d), ACT.Square)
                    A(dyn(hH, d), dyn(xT, d), ACT.Identity, scale=vec[:, bass.ds(d + V_GFFN, 1)]).then_inc(x1h, 1)

            rsqrt(r1[:], PB[4][:], 1.0 / D, 3, rr)
            with act.Fori(0, KF) as i:
                g_, u_ = Slot(N_FF, 0, 2, i), Slot(N_FF, 1, 2, i)
                used(g_)
                split_hi(g_.next())
                freed(act, g_)
                A(sg[:], gt[:], ACT.Silu).then_inc(sg_rdy, 1)
                used(u_)
                split_hi(u_.next())
                act.wait_ge(a32_rdy, i + 1)
                copy(dyn(aH, i), a32[:]).then_inc(ah_rdy, 1)
            with act.Fori(0, KF // 2) as i:
                for s in range(2):
                    sl = Slot(N_DN, s, 2, i)
                    used(sl)
                    split_hi(sl.next())

            for d in range(KD):
                act.wait_ge(x1_rdy, KD + d + 1)
                A((sqx, a32)[d % 2][:], xT[:, d, :], ACT.Square).then_inc(sq2_rdy, 1)
            rsqrt(r1[:], PB[4][:], 1.0 / D, 4, rr)
            for d in range(KD):
                act.wait_ge(h2f, d + 1)
                A(hH[:, d, :], (sg, a32)[d % 2][:], ACT.Identity, bias=mod[:, d:d + 1]).then_inc(h2h, 1)
            kv, ki = Slot(N_KV, 0), Slot(N_KV, 1)
            used(kv)
            act.wait_ge(e_out, 16 * NCH)
            copy(kvraw[:], PB[0][:]).then_inc(gfree[0], 1)
            split_hi(kv.next())
            used(ki)
            copy(kiraw[0:NKI, :], PB[1][0:NKI, :]).then_inc(gfree[1], 1)
            split_hi(ki.next())
            for e in range(2):
                act.wait_ge(s5_tr, e + 1)
                copy(bbT[:, e].rearrange("p k n -> p (k n)"), PB[6 + e][:]).then_inc(s5_ev, 1)
            act.wait_ge(kv_tr, 1)
            copy(vt2[:], PB[3][:].rearrange("p (b n) -> p b n", b=TB)[:, :, HD:2 * HD]).then_inc(kv_ev, 1)
            act.wait_ge(kv_tr, 2)
            copy(wtok[:], PB[2][:].rearrange("p (b n) -> p b n", b=TB)[:, :, HD:HD + 8]).then_inc(kv_ev, 1)

            act.nop().then_inc(relu_rdy, 1)
            act.nop().then_inc(relu_rdy, 1)
            with act.Fori(0, NPAIR) as i:
                q, z = Slot(N_IX, 0, 2, i), Slot(N_IX, 1, 2, i)
                used(q)
                wait(act, ix_ready, i * 6)
                copy(qn[:], PB[0][:]).then_inc(gfree[0], 1)
                split_hi(q.next())
                used(z)
                A(dyn(szb, i), PB[1][:], ACT.Silu).then_inc(gfree[1], 1)
                split_hi(z.next())
                for hh in range(2):
                    for b in range(1, TB):
                        u = 3 * hh + b - 1
                        act.wait_ge(ix_ready, i * 6 + (u + 1))
                        act.wait_ge(r_used, i * 6 + (u + 1))
                        A(relu_b[u % 2][:, 0:P * (b + 1)], SB[u % 2][:, 0:P * (b + 1)], ACT.Relu,
                          scale=IDX_SCALE).then_inc(relu_rdy, 1)

            xa = Slot(N_S5)
            used(xa)
            copy(xaS[:], PB[xa.par][:]).then_inc(gfree[xa.par], 1)
            split_hi(xa.next())

            def s5(j, last):
                for c in range(4):
                    s = Slot(N_S5 + 1, c, 6, j)
                    used(s)
                    A(dyn((tga, tgb)[c % 2], j * 2 + c // 2), PB[s.par][:], ACT.Tanh, scale=0.5).then_inc(gfree[s.par], 1)
                    split_hi(s.next())
                s = Slot(N_S5 + 1, 4, 6, j)
                used(s)
                A(dyn(sza, j), PB[s.par][:], ACT.Silu).then_inc(gfree[s.par], 1)
                if last:
                    act.wait_ge(glu_full, 16)
                split_hi(s.next())
                act.wait_ge(y_mm, j * 4 + 4)
                wait(act, ya_done, j)
                A(yg[:], OB[:], ACT.Gelu_apprx_tanh).then_inc(y_free, 1)
                act.wait_ge(y_free, j + 1)
                copy(dyn(yaH, j), yg[:]).then_inc(ya_h, 1)
                if not last:
                    s = Slot(N_S5 + 1, 5, 6, j)
                    used(s)
                    copy(xaS[:], PB[s.par][:]).then_inc(gfree[s.par], 1)
                    split_hi(s.next())
            with act.Fori(0, KH - 1) as j:
                s5(j, False)
            s5(KH - 1, True)

            q = Slot(N_AT)
            used(q)
            copy(qn[:], PB[0][:], HD ** -0.5).then_inc(gfree[0], 1)
            split_hi(q.next())

            def att(i, last):
                softmax(i + NPAIR)
                s = Slot(N_AT + 1, 0, 2, i)
                used(s)
                if not last:
                    act.wait_ge(glu_full, i * 16 + 32)
                split_hi(s.next())
                A(thg[:], PB[3][:], ACT.Tanh, bias=hbg[:, bass.ds(i, 1)], scale=0.5).then_inc(th_rdy, 1)
                freed(act, s)
                copy(dyn(y2H, i), dyn(sza, i), 0.5).then_inc(y2h, 1)
                if not last:
                    s = Slot(N_AT + 1, 1, 2, i)
                    used(s)
                    copy(qn[:], PB[0][:], HD ** -0.5).then_inc(gfree[0], 1)
                    split_hi(s.next())
                p_evac(i + NPAIR)
                act.wait_ge(o_free, i + (NPAIR + 1))
                copy(dyn(ybH, i), dyn(szb, i)).then_inc(ybh, 1)
            with act.Fori(0, NPAIR - 1) as i:
                att(i, False)
            att(NPAIR - 1, True)

            with act.Fori(0, KD // 2) as i:
                for s in range(2):
                    sl = Slot(N_AB, s, 2, i)
                    used(sl)
                    split_hi(sl.next())
                for e in range(2):
                    act.wait_ge(mg_rdy, i * 2 + (e + 1))
                    copy(dyn(hH, i * 2 + e), dyn(tga, i * 2 + e), 0.5).then_inc(mgh, 1)

            def out2(i, last):
                for s in range(2):
                    sl, d = Slot(N_O2, s, 2, i), i * 2 + s
                    if not last:
                        used(sl)
                        split_hi(sl.next())
                    act.wait_ge(x3_rdy, d + 1)
                    wait(act, xf_tr, i * 2)
                    A((t1, t2)[s][:], dyn(xT, d), ACT.Square)
                    A((t3, t4)[s][:], dyn(xT, d), ACT.Identity, scale=vec[:, bass.ds(d + V_FG, 1)]).then_inc(xf_rdy, 1)
            with act.Fori(0, KD // 2 - 1) as i:
                out2(i, False)
            out2(KD // 2 - 1, True)
            act.wait_ge(ssm, 5)
            A(sm[:, 12:16], PB[4][:, 0:4], ACT.Ln, bias=epst[:, 0:1], scale=1.0 / D).then_inc(astep, 1)
            a_n[0] += 1
            act.wait_ge(astep, a_n[0])
            A(sm[:, 16:20], sm[:, 12:16], ACT.Exp, scale=-0.5).then_inc(rr, 1)

        @block.vector
        def _(dve):
            v = nc.vector
            TT, TS, STT = v.tensor_tensor, v.tensor_scalar, v.scalar_tensor_tensor
            MU, AD, SU = ALU.mult, ALU.add, ALU.subtract
            st = Steps(dve, vstep)
            mark, need = st.mark, st.need

            def dyn(t, k):
                return t[:, k, :] if isinstance(k, int) else t[:, bass.ds(k, 1), :].rearrange("p k t -> p (k t)")

            def col(t, k):
                return t[:, bass.ds(k, 1)] if not isinstance(k, int) else t[:, k:k + 1]

            def split_lo(s):
                dve.wait_ge(hi_done, s.n + 1)
                TT(wL[s.par][:], raw[s.par][:], wH[s.par][:].bitcast(F32), SU).then_inc(lo_done, 1)

            def used(s):
                dve.wait_ge(slot_used, s.n + 1)

            def newton(r, ss, scale, ta, tb):
                mark(TS(ta, ss, scale, EPS, MU, AD))
                mark(TT(tb, r, r, MU))
                need()
                mark(TT(tb, tb, ta, MU))
                need()
                mark(TS(tb, tb, -0.5, 1.5, MU, AD))
                need()
                return mark(TT(r, r, tb, MU))

            for s in (sc_free, m_used, r_used, bu_free, e_used):
                for _ in range(2):
                    dve.nop().then_inc(s, 1)
            v.memset(epst[:], EPS).then_inc(init_v, 1)
            v.memset(ones[:], 1.0)
            v.memset(macc[:], 0.0)
            v.memset(ssc[:], 0.0)
            m_init = mark(v.memset(ssa[:], 0.0))
            dve.wait_ge(vec_in, 16 * 18)
            for e in range(2):
                ins = v.tensor_copy(row2[32:48, e * HD:(e + 1) * HD], ldt[32:48, e:e + 1].broadcast_to([NCH, HD]))
            ins.then_inc(r0d, 1)
            dve.wait_ge(ss0, 1)
            need(newton(sm[:, 8:12], sm[:, 0:4], 1.0 / D, sm[:, 12:16], sm[:, 16:20]))
            for t in range(TB):
                ins = TS(xn_tok[:, t, :], x_tok[:, t, :], sm[:, 8 + t:9 + t], None, MU)
            ins.then_inc(xn_done, 1)
            dve.wait_ge(pe_pre, 2)
            v.tensor_copy(vec[:], PB[6][:, 0:NV1])
            ins = v.tensor_copy(svec[:], PB[7][:, 0:NV2])
            mark(ins)
            need()
            mark(TS(hbg[:], vec[:, V_BGLU + KH:V_BGLU + 2 * KH], 0.5, None, MU))
            TS(vec[:, V_GQ:V_GQ + 1], vec[:, V_GQ:V_GQ + 1], HD ** -0.5, None, MU).then_inc(vec_rdy, 1)
            split_lo(Slot(0))
            for k in range(KD):
                dve.wait_ge(pe_pre, 2 + k + 1)
                dve.wait_ge(hin_done, k + 1)
                STT(hL[:, k, :], PB[k % 2][:], vec[:, V_GMIX + k:V_GMIX + k + 1], hH[:, k, :].bitcast(F32),
                    MU, SU).then_inc(pre_done, 1)
            for k in range(KD):
                dve.wait_ge(pe_pre, 2 + KD + k + 1)
                v.tensor_copy(xT[:, k, :], PB[k % 2][:]).then_inc(pre_done, 1)
            split_lo(Slot(1))
            mark(v.memset(cuP[:, 0:2], 0.0))

            def par(k):
                return sp[:, k, :]

            def seq(*fs):
                for f in fs:
                    need()
                    mark(f())

            MAGIC, PI, TWO_PI = 12582912.0, 3.1415925, 6.283185307179586
            LN2H, LN2L = 0.693359375, -2.12194440e-4

            def exp(dst, src):
                z, n, r, p = par(8), par(9), par(10), par(11)
                seq(lambda: TS(z, src, -87.0, 88.0, ALU.max, ALU.min),
                    lambda: TS(n, z, 1.4426950408889634, MAGIC, MU, AD),
                    lambda: TS(n, n, MAGIC, None, SU),
                    lambda: STT(r, n, -LN2H, z, MU, AD),
                    lambda: STT(r, n, -LN2L, r, MU, AD),
                    lambda: TS(p, r, 1 / 5040, None, MU))
                for c in (1 / 720, 1 / 120, 1 / 24, 1 / 6, 1 / 2, 1.0):
                    seq(lambda: STT(p, p, c, r, AD, MU))
                seq(lambda: TS(n, n, 127.0, None, AD),
                    lambda: v.tensor_copy(spi[:], n),
                    lambda: TS(spi[:], spi[:], 23, None, ALU.logical_shift_left),
                    lambda: STT(dst, p, 1.0, spi[:].bitcast(F32), AD, MU))

            are, aim = svec[:, 0:NCH], svec[:, NCH:2 * NCH]
            exp(par(0), svec[:, 2 * NCH:3 * NCH])
            seq(lambda: TT(par(12), are, par(0), MU))
            exp(par(1), par(12))
            C1, C2 = 6.28125, 1.93500518798828125e-3
            C3 = TWO_PI - C1 - C2
            th, n, r, t = par(2), par(9), par(4), par(10)
            seq(lambda: TT(th, aim, par(0), MU),
                lambda: TS(n, th, 1 / TWO_PI, MAGIC, MU, AD),
                lambda: TS(n, n, MAGIC, None, SU),
                lambda: STT(th, n, -C1, th, MU, AD),
                lambda: STT(th, n, -C2, th, MU, AD),
                lambda: STT(th, n, -C3, th, MU, AD),
                lambda: TS(r, th, PI, -PI, ALU.min, ALU.max),
                lambda: TS(par(5), th, TWO_PI / 4, None, AD),
                lambda: TS(t, par(5), PI, -TWO_PI, ALU.is_gt, MU),
                lambda: TT(par(5), par(5), t, AD),
                lambda: TS(par(5), par(5), PI, -PI, ALU.min, ALU.max))
            need()
            v.tensor_copy(par(3), par(5)).then_inc(trig_r, 1)
            dve.wait_ge(trig_a, 2)
            sn, cs = par(6), par(7)
            nr, ni, den, rd, crr, cri = (par(k) for k in (12, 13, 14, 8, 15, 16))
            seq(lambda: TT(nr, par(1), cs, MU),
                lambda: TS(nr, nr, -1.0, None, AD),
                lambda: TT(ni, par(1), sn, MU),
                lambda: TT(den, are, are, MU),
                lambda: TT(t, aim, aim, MU),
                lambda: TT(den, den, t, AD),
                lambda: v.reciprocal(rd, den),
                lambda: TT(crr, nr, are, MU),
                lambda: TT(t, ni, aim, MU),
                lambda: TT(crr, crr, t, AD),
                lambda: TT(crr, crr, rd, MU),
                lambda: TT(cri, ni, are, MU),
                lambda: TT(t, nr, aim, MU),
                lambda: TT(cri, cri, t, SU),
                lambda: TT(cri, cri, rd, MU))
            mark(v.tensor_copy(pw[:, 0, 0, :], cs))
            mark(v.tensor_copy(pw[:, 1, 0, :], sn))
            for k in range(LEVELS - 1):
                c, s = pw[:, 0, k, :], pw[:, 1, k, :]
                need()
                mark(TT(par(9), c, s, SU))
                mark(TT(par(10), c, s, AD))
                need()
                mark(STT(pw[:, 1, k + 1, :], c, 2.0, s, MU, MU))
                mark(TT(pw[:, 0, k + 1, :], par(9), par(10), MU))
            need()
            v.tensor_copy(par(17), par(9)).then_inc(pw_rdy, 1)

            def qk_norm(a):
                dve.wait_ge(rs_rdy, a * 2 + 1)
                STT(qn[:], qraw[:], vec[:, V_GQ:V_GQ + 1], rq[:], MU, MU)
                dve.wait_ge(rs_rdy, a * 2 + 2)
                STT(kn[:], kraw[:], vec[:, V_GK:V_GK + 1], rk[:], MU, MU).then_inc(qn_rdy, 1)

            def score_max(a, masks):
                for hh in range(2):
                    for b in range(TB):
                        u, c = 4 * hh + b, 4 * hh + b
                        dve.wait_ge(sc_ready, a * 8 + (u + 1))
                        settled(dve)
                        v.tensor_tensor_reduce(L[:, hh, CB[b]:CB[b + 1]], SB[u % 2][:, 0:P * (b + 1)], masks[b], 1.0,
                                               GONE, AD, ALU.max, mx[:, c:c + 1]).then_inc(sc_free, 1)
                    dve.wait_ge(sc_free, a * 8 + (4 * hh + 4 + 2))
                    TS(nmx[:, 4 * hh:4 * hh + 4], mx[:, 4 * hh:4 * hh + 4], -1.0, None, MU).then_inc(nm, 1)

            def normalise(a):
                for hh in range(2):
                    dve.wait_ge(ex, a * 2 + (hh + 1))
                    mark(v.reciprocal(rinv[:, 4 * hh:4 * hh + 4], rs[:, 4 * hh:4 * hh + 4]))
                    need()
                    for b in range(TB):
                        l = L[:, hh, CB[b]:CB[b + 1]]
                        ins = TS(l, l, rinv[:, 4 * hh + b:4 * hh + b + 1], None, MU)
                    ins.then_inc(pn, 1)

            def mod_rows(i, ms):
                for m in ms:
                    dve.wait_ge(m_full[m % 2], i * 48 + 16 * (m // 2 + 1))
                    wait(dve, m_used, i * 6 + m)
                    o = macc[:, (m % 3) * D:(m % 3 + 1) * D]
                    STT(o, mraw[m % 2][:], col(csil, i * 2 + m // 3), o, MU, AD).then_inc(m_used, 1)

            def mix(i, last):
                qk_norm(i)
                u, gc, gb = (Slot(3, j, 6, i) for j in range(3))
                split_lo(u.next())
                used(gc)
                freed(dve, u)
                mark(TT(cuP[:, 2:S + 2], PB[gc.par][:], u_s[:], MU))
                need()
                TS(cv[:], cuP[:, 2:S + 2], col(vec, i + (V_CONV + 8)), None, MU).then_inc(gfree[gc.par], 1)
                split_lo(gc.next())
                freed(dve, gc)
                mark(STT(cv[:], cuP[:, 1:S + 1], col(vec, i + (V_CONV + 4)), cv[:], MU, AD))
                need()
                mark(STT(cv[:], cuP[:, 0:S], col(vec, i + V_CONV), cv[:], MU, AD))
                used(gb)
                need()
                wait(dve, ych, i)
                TT(yc[:], PB[gb.par][:], cv[:], MU).then_inc(gfree[gb.par], 1)
                split_lo(gb.next())
                dve.wait_ge(ych, i + 1)
                mark(TT(ssc[:], ssc[:], sqc[:], AD))
                mark(STT(dyn(mixL, i), yc[:], col(vec, i + V_GCONV), dyn(mixH, i).bitcast(F32), MU, SU))
                score_max(i, [mask1[:, S - P * (b + 1):S] for b in range(TB)])
                mod_rows(i, range(0, 2))
                normalise(i)
                if not last:
                    split_lo(Slot(3, 3, 6, i).next())
                    mod_rows(i, range(2, 4))
                    split_lo(Slot(3, 4, 6, i).next())
                    mod_rows(i, range(4, 6))
                    split_lo(Slot(3, 5, 6, i).next())
                else:
                    mod_rows(i, range(2, 6))
                dve.wait_ge(o_free, i + 1)
                mark(TT(ssa[:], ssa[:], sqa[:], AD))
                mark(STT(dyn(mixL, i + KH), yo[:], col(vec, i + V_GATT), dyn(mixH, i + KH).bitcast(F32), MU, SU))

            need(m_init)
            dve.wait_ge(trig_a, 1)
            for j in range(3):
                split_lo(Slot(0, j).next())
            with dve.Fori(0, NPAIR - 1) as i:
                st.enter(i, MIX_STEPS)
                mix(i, False)
                st.leave(NPAIR - 1)
            mix(NPAIR - 1, True)
            need()
            v.memset(ss1[:], 0.0).then_inc(ssum, 1)
            v.memset(nt1[:], 0.0).then_inc(ssum, 1)

            dve.wait_ge(mod_mm, 1)
            mark(TT(mod[:], PB[6][:, 0:3 * KD], vec[:, V_BMOD:V_BMOD + 3 * KD], AD))
            need()
            mark(STT(gs[:], mod[:, KD:2 * KD], 1.0, vec[:, V_NG:V_NG + KD], AD, MU))
            dve.wait_ge(rr, 1)
            need(newton(rc[:], PB[4][:], 1.0 / HALF, nt1[:], nt2[:]))
            dve.wait_ge(rr, 2)
            need(newton(ra[:], PB[5][:], 1.0 / HALF, nt1[:], nt2[:]))
            with dve.Fori(0, KD // 2) as i:
                st.enter(i, 8)
                for s in range(2):
                    sl, d = Slot(N_WO, s, 2, i), i * 2 + s
                    used(sl)
                    mark(TT(wo1[:], PB[s][:], rc[:], MU))
                    TT(wo2[:], PB[2 + s][:], ra[:], MU).then_inc(gfree[s], 1)
                    need()
                    mark(TT(dyn(xT, d), dyn(xT, d), wo1[:], AD))
                    freed(dve, sl)
                    need()
                    TT(dyn(xT, d), dyn(xT, d), wo2[:], AD).then_inc(x1_rdy, 1)
                    split_lo(sl.next())
                    dve.wait_ge(x1h, d + 1)
                    mark(TT(ss1[:], ss1[:], sqx[:], AD))
                    STT(dyn(hL, d), dyn(xT, d), col(vec, d + V_GFFN), dyn(hH, d).bitcast(F32), MU, SU).then_inc(x1l, 1)
                    need()
                    mark(v.memset(m8[:, 0, 0:1], 0.0))
                st.leave(KD // 2)
            need()
            v.memset(m8[:, 0, 0:1], 0.0).then_inc(ssum, 1)

            dve.wait_ge(rr, 3)
            need(newton(r1[:], PB[4][:], 1.0 / D, gt[:], ut[:]))
            with dve.Fori(0, KF) as i:
                st.enter(i, 1)
                g_, u_ = Slot(N_FF, 0, 2, i), Slot(N_FF, 1, 2, i)
                used(g_)
                TT(gt[:], PB[0][:], r1[:], MU).then_inc(gfree[0], 1)
                split_lo(g_.next())
                used(u_)
                TT(ut[:], PB[1][:], r1[:], MU).then_inc(gfree[1], 1)
                split_lo(u_.next())
                dve.wait_ge(sg_rdy, i + 1)
                freed(dve, u_)
                TT(a32[:], sg[:], ut[:], MU).then_inc(a32_rdy, 1)
                dve.wait_ge(ah_rdy, i + 1)
                TT(dyn(aL, i), a32[:], dyn(aH, i).bitcast(F32), SU).then_inc(a_done, 1)
                mark(v.memset(m8[:, 0, 0:1], 0.0))
                st.leave(KF)
            with dve.Fori(0, KF // 2) as i:
                for s in range(2):
                    split_lo(Slot(N_DN, s, 2, i).next())

            mark(v.memset(ss1[:], 0.0))

            def ss_add(d):
                dve.wait_ge(sq2_rdy, d + 1)
                need()
                mark(TT(ss1[:], ss1[:], (sqx, a32)[d % 2][:], AD))
            for d in range(KD):
                if d < KD - 1:
                    dve.wait_ge(dn_done, d + 1)
                else:
                    dve.wait_ge(slot_used, N_DN + KF)
                TT(xT[:, d, :], xT[:, d, :], PB[d][:], AD).then_inc(x1_rdy, 1)
                if d:
                    ss_add(d - 1)
            ss_add(KD - 1)
            need()
            v.memset(cTt[:], 0.0).then_inc(ssum, 1)
            mark(v.memset(bdg[:], 0.0))
            dve.wait_ge(rr, 4)
            need(newton(r1[:], PB[4][:], 1.0 / D, gt[:], ut[:]))

            def h2_low(d):
                dve.wait_ge(h2h, d + 1)
                STT(hL[:, d, :], (sg, a32)[d % 2][:], mod[:, d:d + 1], hH[:, d, :].bitcast(F32), AD, SU
                    ).then_inc(h2_done, 1)
            for d in range(KD):
                wait(dve, h2_done, d - 1)
                STT((sg, a32)[d % 2][:], xT[:, d, :], gs[:, d:d + 1], r1[:], MU, MU).then_inc(h2f, 1)
                if d:
                    h2_low(d - 1)
            h2_low(KD - 1)

            dve.wait_ge(s5_in, 64)
            dve.wait_ge(e_out, 16 * NCH)

            def over(k):
                return par(k).unsqueeze(2).broadcast_to([P, NCH, GP])
            tb_ = [t[:, 0:NCH * GP].rearrange("p (s q) -> p s q", q=GP) for t in (t3, t4, gr, gi)]
            mark(TT(tb_[0], braw[:, 0], over(15), MU))
            mark(TT(tb_[1], braw[:, 1], over(16), MU))
            mark(TT(tb_[2], braw[:, 1], over(15), MU))
            mark(TT(tb_[3], braw[:, 0], over(16), MU))
            need()
            for g2 in range(2):
                r = slice(HD * g2, HD * g2 + HD)
                mark(TT(bdg[r, 0, :, GP * g2:GP * g2 + GP], tb_[0][r], tb_[1][r], SU))
                ins = TT(bdg[r, 1, :, GP * g2:GP * g2 + GP], tb_[2][r], tb_[3][r], AD)
            ins.then_inc(bd_rdy, 1)
            for k, (raw_, dst) in enumerate(((kvraw, kn), (kiraw, k2))):
                freed(dve, Slot(N_KV, k))
                v.tensor_copy(dst[0:HD, :], raw_[0:HD, :])
                v.tensor_copy(dst[HD:P, :], raw_[0:HD, :]).then_inc(kdup, 1)
                split_lo(Slot(N_KV, k).next())
            for e in range(2):
                dve.wait_ge(s5_tr, 3 + e)
                for g2 in range(2):
                    src = PB[4 + e][0:HD, :].rearrange("n (s g q) -> n s g q", g=2, q=GP)[:, :, g2, :]
                    ins = TS(cTt[HD * g2:HD * g2 + HD, e, :, GP * g2:GP * g2 + GP], src, (1.0, -1.0)[e], None, MU)
            ins.then_inc(s5_cv, 1)

            m_s = mark(v.memset(score[:], 0.0))
            dve.wait_ge(kv_ev, 2)
            need(m_s)
            with dve.Fori(0, NPAIR) as i:
                q, z = Slot(N_IX, 0, 2, i), Slot(N_IX, 1, 2, i)
                split_lo(q.next())
                split_lo(z.next())
                for hh in range(2):
                    for b in range(1, TB):
                        u = 3 * hh + b - 1
                        dve.wait_ge(relu_rdy, i * 6 + (u + 1 + 2))
                        wait(dve, r_used, i * 6 + u)
                        sc = score[:, CB[b]:CB[b + 1]]
                        STT(sc, relu_b[u % 2][:, 0:P * (b + 1)], wtok[:, b, bass.ds(i * 2 + hh, 1)], sc, MU, AD
                            ).then_inc(r_used, 1)
            dve.wait_ge(r_used, 6 * NPAIR + 2)
            for b in range(1, TB):
                mark(STT(score[:, CB[b + 1] - P:CB[b + 1]], diag, GONE, score[:, CB[b + 1] - P:CB[b + 1]], MU, AD))
            need()
            mark(v.tensor_copy(work[:, P:CB[4]], score[:, P:CB[4]]))

            def top8():
                need()
                settled(dve)
                w = [work[:, CB[b]:CB[b + 1]] for b in range(1, TB)]
                for b in range(3):
                    mark(v.max(m8[:, b, :], w[b]))
                need()
                settled(dve)
                for b in range(3):
                    mark(v.match_replace(w[b], m8[:, b, :], w[b], GONE))

            def s5(j, last):
                for c in range(4):
                    split_lo(Slot(N_S5 + 1, c, 6, j).next())
                    q = j * 4 + c
                    br, bi = (b[:] for b in (SB if c % 2 == 0 else TBANK))
                    co, si = ebuf[c % 2][:, 0, :], ebuf[c % 2][:, 1, :]
                    hr, hi = (hr0, hr1)[c % 2][:], (hi0, hi1)[c % 2][:]
                    dve.wait_ge(bu_done, q + 1)
                    dve.wait_ge(e_full[c % 2], j * 32 + 16 * (c // 2 + 1))
                    mark(TT(t1[:], br, co, MU))
                    a = mark(TT(t2[:], bi, si, MU))
                    mark(TT(t3[:], bi, co, MU))
                    b4 = mark(TT(t4[:], br, si, MU))
                    need(a)
                    a = mark(TT(t1[:], t1[:], t2[:], AD))
                    need(b4)
                    TT(t3[:], t3[:], t4[:], SU).then_inc(bu_free, 1)
                    need(a)
                    mg = par(1)[:, bass.ds(q, 1)] if not isinstance(q, int) else par(1)[:, q:q + 1]
                    mark(v.tensor_tensor_scan(gr[:], mg.broadcast_to([P, S]), t1[:], 0.0, MU, AD))
                    dve.wait_ge(bu_free, q + (1 + 2))
                    mark(v.tensor_tensor_scan(gi[:], mg.broadcast_to([P, S]), t3[:], 0.0, MU, AD))
                    need()
                    mark(TT(t1[:], gr[:], co, MU))
                    mark(TT(t2[:], gi[:], si, MU))
                    mark(TT(t3[:], gr[:], si, MU))
                    TT(t4[:], gi[:], co, MU).then_inc(e_used, 1)
                    need()
                    wait(dve, y_mm, q - 1 if c >= 2 else j * 4)
                    mark(TT(hr, t1[:], t2[:], SU))
                    dve.wait_ge(e_used, q + (1 + 2))
                    TT(hi, t3[:], t4[:], AD).then_inc(h_rdy, 1)
                    top8()
                split_lo(Slot(N_S5 + 1, 4, 6, j).next())
                dve.wait_ge(ya_h, j + 1)
                STT(dyn(yaL, j), yg[:], 1.0, dyn(yaH, j).bitcast(F32), MU, SU).then_inc(ya_done, 1)
                if not last:
                    split_lo(Slot(N_S5 + 1, 5, 6, j).next())

            split_lo(Slot(N_S5).next())
            with dve.Fori(0, KH - 1) as j:
                st.enter(j, S5_STEPS)
                s5(j, False)
                st.leave(KH - 1)
            s5(KH - 1, True)
            need()
            mark(TT(work[:, P:CB[4]], work[:, P:CB[4]], score[:, P:CB[4]], ALU.is_lt))
            need()
            mark(TS(score[:, P:CB[4]], work[:, P:CB[4]], -1.0, -NEG, AD, MU))
            mark(TS(score[:, 0:P], diag, NEG, None, MU))
            need()

            masks = [score[:, CB[b]:CB[b + 1]] for b in range(TB)]
            split_lo(Slot(N_AT).next())
            score_max(NPAIR, masks)

            def att(i, last):
                normalise(i + NPAIR)
                s = Slot(N_AT + 1, 0, 2, i)
                used(s)
                mark(STT(dyn(sza, i), PB[1][:], col(vec, i + V_BGLU), dyn(sza, i), AD, MU))
                split_lo(s.next())
                need()
                dve.wait_ge(th_rdy, i + 1)
                STT(dyn(sza, i), thg[:], 1.0, dyn(sza, i), AD, MU).then_inc(gfree[1], 1)
                dve.wait_ge(y2h, i + 1)
                STT(dyn(y2L, i), dyn(sza, i), 0.5, dyn(y2H, i).bitcast(F32), MU, SU).then_inc(y2_done, 1)
                if not last:
                    split_lo(Slot(N_AT + 1, 1, 2, i).next())
                dve.wait_ge(pv, (i + NPAIR) * 2 + 2)
                TT(dyn(szb, i), OB[:], dyn(szb, i), MU).then_inc(o_free, 1)
                dve.wait_ge(o_free, i + (NPAIR + 1))
                dve.wait_ge(ybh, i + 1)
                STT(dyn(ybL, i), dyn(szb, i), 1.0, dyn(ybH, i).bitcast(F32), MU, SU).then_inc(yb_done, 1)
                if not last:
                    score_max(i + (NPAIR + 1), masks)
            with dve.Fori(0, NPAIR - 1) as i:
                st.enter(i, 3)
                att(i, False)
                st.leave(NPAIR - 1)
            att(NPAIR - 1, True)

            with dve.Fori(0, KD // 2) as i:
                st.enter(i, 3)
                for s, tg in enumerate((tga, tgb)):
                    sl = Slot(N_AB, s, 2, i)
                    used(sl)
                    t0 = mark(STT(dyn(tg, i * 2), dyn(tg, i * 2), 1.0, PB[s][:], AD, MU))
                    STT(dyn(tg, i * 2 + 1), dyn(tg, i * 2 + 1), 1.0, PB[s + 2][:], AD, MU).then_inc(gfree[s], 1)
                    split_lo(sl.next())
                need()
                freed(dve, sl)
                for e in range(2):
                    d = i * 2 + e
                    TT(dyn(tga, d), dyn(tga, d), dyn(tgb, d), AD).then_inc(mg_rdy, 1)
                for e in range(2):
                    d = i * 2 + e
                    dve.wait_ge(mgh, d + 1)
                    STT(dyn(hL, d), dyn(tga, d), 0.5, dyn(hH, d).bitcast(F32), MU, SU).then_inc(mg_done, 1)
                mark(v.memset(m8[:, 0, 0:1], 0.0))
                st.leave(KD // 2)

            mark(v.memset(gr[:], 0.0))
            need()

            def out2(i, last):
                for s in range(2):
                    sl, d = Slot(N_O2, s, 2, i), i * 2 + s
                    used(sl)
                    STT(dyn(xT, d), PB[s][:], col(mod, d + 2 * KD), dyn(xT, d), MU, AD).then_inc(x3_rdy, 1)
                    if last:
                        dve.nop().then_inc(gfree[s], 1)
                    else:
                        dve.wait_ge(x3_rdy, d + 1)
                        v.memset(m8[:, 1, 0:1], 0.0).then_inc(gfree[s], 1)
                        split_lo(sl.next())
                for s in range(2):
                    d = i * 2 + s
                    dve.wait_ge(xf_rdy, d + 1)
                    mark(TT(gr[:], gr[:], (t1, t2)[s][:], AD))
                    dve.wait_ge(xf_tr, d + 1)
                    v.tensor_copy(out_tok[:, :, bass.ds(d * P, P)], TBANK[s][:].rearrange("p (b n) -> p b n", b=TB)
                                  ).then_inc(ot_done, 1)
                    need()
            with dve.Fori(0, KD // 2 - 1) as i:
                st.enter(i, 2)
                out2(i, False)
                st.leave(KD // 2 - 1)
            out2(KD // 2 - 1, True)
            v.memset(m8[:, 0, 0:1], 0.0).then_inc(ssum, 1)
            dve.wait_ge(rr, 5)
            dve.wait_ge(ot_done, KD)
            need(newton(sm[:, 16:20], PB[4][:, 0:4], 1.0 / D, sm[:, 12:16], sm[:, 8:12]))
            for t in range(TB):
                TS(out_tok[:, t, :], out_tok[:, t, :], sm[:, 16 + t:17 + t], None, MU).then_inc(fin, 1)


_INS = ["x", "g_mix", "w_in", "conv_w", "g_q", "g_k", "g_conv_out", "g_attn_out", "w_out", "g_ffn", "w_gate", "w_up",
        "w_down", "c_2", "norm_g_2", "w_mod_2", "b_mod_2", "w_in_2", "a_re_2", "a_im_2", "b_re_2", "b_im_2", "c_re_2",
        "c_im_2", "d_skip_2", "log_dt_2", "w_glu_2", "b_glu_2", "w_a_o_2", "w_b_o_2", "w_out_2", "final_g_2"]


def kernel(**inputs):
    import concourse.bacc as _bacc
    from concourse.bass_utils import run_bass_kernel_spmd as _run

    nc = _bacc.Bacc("TRN2", target_bir_lowering=False, num_devices=1)
    arrays, args = {}, []
    for name in _INS + ["constants"]:
        a = constants() if name == "constants" else np.ascontiguousarray(inputs[name])
        arrays[f"in_{name}_dram"] = a
        args.append(nc.dram_tensor(f"in_{name}_dram", a.shape, mybir.dt.from_np(a.dtype), kind="ExternalInput").ap())
    args.append(nc.dram_tensor("out_0_dram", (1, S, D), F32, kind="ExternalOutput").ap())
    program(nc, args)
    r = _run(nc, [arrays], core_ids=[0])
    return r.results[0]["out_0_dram"]
```

```python
import concourse.bass as bass
from concourse import mybir
from contextlib import ExitStack
import numpy as np

F32 = mybir.dt.float32
F32R = mybir.dt.float32r
I32 = mybir.dt.int32
ALU = mybir.AluOpType
ACT = mybir.ActivationFunctionType
AX = mybir.AxisListType

P = 128
S = 512
TB = S // P
D = 1024
KD = D // P
HALF = D // 2
KH = HALF // P
HD = 64
NPAIR = 4
FF = ((-(-8 * D // 3) + 255) // 256) * 256
KF = FF // P
EPS = 1e-6
NEG = -1e30
GONE = -3e38
TOPK = min(256, S // 4)
ROUNDS = TOPK // 8
IDX_SCALE = float((8 * 64) ** -0.5)
G2, NST, GP = 32, 64, 16
NCH = G2 * NST // P
LEVELS = 9
MIX_STEPS, S5_STEPS = 9, 32

Z_U, Z_GB, Z_GC, Z_Q, Z_K, Z_V = (j * HALF for j in range(6))
Y_XA, Y_ZA, Y_Q, Y_K, Y_ZB, Y_QI, Y_KI, Y_WI = 0, 512, 1024, 1536, 1664, 2176, 2688, 2752
Y_GA, Y_GB = 2760, 3784
NKI = Y_GA - Y_KI

N_MIX = 0
N_WO = N_MIX + 24
N_FF = N_WO + KD
N_DN = N_FF + 2 * KF
N_KV = N_DN + KF
N_IX = N_KV + 2
N_S5 = N_IX + 2 * NPAIR
N_AT = N_S5 + 24
N_AB = N_AT + 8
N_O2 = N_AB + 8
N_END = N_O2 + KD

CB = [0, 128, 384, 768, 1280]
OFF = [0, 512, 896, 1152, 1280]

V_GMIX, V_CONV, V_GCONV, V_GATT, V_GFFN, V_C, V_NG, V_BMOD, V_BGLU, V_DSK, V_FG, V_GQ, V_GK = \
    0, 8, 20, 24, 28, 36, 44, 52, 76, 84, 88, 96, 97
NV1 = 98
W_ARE, W_AIM, W_LDT = 0, 16, 32
NV2 = 48

C_ID, C_DG, C_BD, C_M1, C_END = 0, 128, 256, 384, 896


def constants():
    i = np.arange(P)[:, None]
    d = i - np.arange(S)[None, :] + (S - P)
    c = ((d >= 0) & (d <= 128)) * 1 + ((d >= 0) & (d % 4 == 0)) + ((d >= 0) & (d % 16 == 0))
    m1 = np.where(c > 0, np.log(np.maximum(c, 1)), NEG)
    j = np.arange(P)[None, :]
    dg = np.where(j <= i, 0.0, 1.0)
    bd = (i // HD == j // HD) * 1.0
    return np.concatenate([np.eye(P), dg, bd, m1], 1).astype(np.float32)


def gfree_count(n):
    return n // 2 - (KF // 2 if n >= N_KV else 0)


class Steps:

    def __init__(self, eng, sem):
        self.eng, self.sem, self.base, self.k, self.i, self.per = eng, sem, 0, 0, None, 0

    def mark(self, ins):
        ins.then_inc(self.sem, 1)
        self.k += 1
        return self.k

    def need(self, k=None):
        k = self.k if k is None else k
        self.eng.wait_ge(self.sem, self.base + k if self.i is None else self.i * self.per + (self.base + k))

    def enter(self, i, per):
        self.base, self.k, self.i, self.per = self.base + self.k, 0, i, per

    def leave(self, times):
        assert self.k == self.per, ("steps in the loop's body", self.k)
        self.base, self.k, self.i = self.base + self.per * times, 0, None


def program(nc, io):
    (x, g_mix, w_in, conv_w, g_q, g_k, g_conv_out, g_attn_out, w_out, g_ffn, w_gate, w_up, w_down,
     c_2, norm_g_2, w_mod_2, b_mod_2, w_in_2, a_re_2, a_im_2, b_re_2, b_im_2, c_re_2, c_im_2,
     d_skip_2, log_dt_2, w_glu_2, b_glu_2, w_a_o_2, w_b_o_2, w_out_2, final_g_2, consts) = io[:-1]
    out = io[-1]
    e_dram = nc.dram_tensor("rotations", [NCH, P, 2, S], F32, kind="Internal").ap()

    with ExitStack() as ctx:
        base = (nc.sbuf_base + 63) // 64 * 64
        top = [base]

        def at(name, shape, dt=F32, off=None):
            size = 4 * int(np.prod(shape[1:]))
            if off is None:
                off = top[0]
                top[0] += (size + 31) // 32 * 32
            return nc.alloc_sbuf_tensor_at(name, shape, dt, offset=off)

        def sem(name):
            return ctx.enter_context(nc.semaphore(name))

        PB = [ctx.enter_context(nc.psum_tensor(f"bank{b}", [P, S], F32)) for b in range(8)]
        SB, TBANK, OB = (PB[4], PB[5]), (PB[6], PB[2]), PB[7]

        xT = at("xT", [P, KD, S])
        hH, hL = at("hH", [P, KD, S], F32R), at("hL", [P, KD, S], F32R)
        raw = [at(f"raw{s}", [P, 1024]) for s in range(2)]
        wH = [at(f"wH{s}", [P, 1024], F32R) for s in range(2)]
        wL = [at(f"wL{s}", [P, 1024], F32R) for s in range(2)]
        cst = at("cst", [P, C_M1])
        vec, svec = at("vec", [P, NV1]), at("svec", [P, NV2])
        ones = at("ones", [P, P])
        epst = at("epst", [P, 1])
        csil, mod, gs = at("csil", [P, KD]), at("mod", [P, 3 * KD]), at("gs", [P, KD])
        mx, nmx, rs, rinv = (at(n, [P, 8]) for n in ("mx", "nmx", "rs", "rinv"))
        sm = at("sm", [P, 24])
        sp = at("sp", [P, 20, NCH])
        spi = at("spi", [P, NCH], I32)
        hbg, ldt = at("hbg", [P, KH]), at("ldt", [P, 2])
        m8 = at("m8", [P, 3, 8])
        ident, diag, bdones = cst[:, C_ID:C_DG], cst[:, C_DG:C_BD], cst[:, C_BD:C_M1]
        A0 = top[0]
        aH, aL = at("aH", [P, KF, S], F32R, A0), at("aL", [P, KF, S], F32R, A0 + 4 * KF * S)
        x_tok, xn_tok = at("x_tok", [P, TB, D], F32, A0), at("xn_tok", [P, TB, D], F32, A0 + 16384)
        row1, row2 = at("row1", [P, P], F32, A0 + 32768), at("row2", [P, P], F32, A0 + 33280)
        names = ["qraw", "kraw", "vT", "u_s", "sqq", "sqk", "rq", "rk", "cv", "yc", "sqc", "yo", "sqa"]
        (qraw, kraw, vT, u_s, sqq, sqk, rq, rk, cv, yc, sqc, yo, sqa) = (
            at(n, [P, S], F32, A0 + 2048 * j) for j, n in enumerate(names))
        cuP = at("cuP", [P, S + 2], F32, A0 + 2048 * 13)
        mixH, mixL = at("mixH", [P, KD, S], F32R, A0 + 32768), at("mixL", [P, KD, S], F32R, A0 + 49152)
        macc = at("macc", [P, 3 * D], F32, A0 + 65536)
        mraw = [at(f"mraw{s}", [P, D], F32, A0 + 77824 + 4096 * s) for s in range(2)]
        ssc, ssa = at("ssc", [P, S], F32, A0 + 86016), at("ssa", [P, S], F32, A0 + 88064)
        rc, ra = at("rc", [P, S], F32, A0), at("ra", [P, S], F32, A0 + 2048)
        nt1, nt2 = at("nt1", [P, S], F32, A0 + 4096), at("nt2", [P, S], F32, A0 + 6144)
        wo1, wo2 = at("wo1", [P, S], F32, A0 + 8192), at("wo2", [P, S], F32, A0 + 10240)
        tga, tgb = at("tga", [P, KD, S], F32, A0), at("tgb", [P, KD, S], F32, A0 + 16384)
        szb, sza = at("szb", [P, KH, S], F32, A0 + 32768), at("sza", [P, KH, S], F32, A0 + 40960)
        ebuf = [at(f"ebuf{s}", [P, 2, S], F32, A0 + 49152 + 4096 * s) for s in range(2)]
        S0 = A0 + 57344
        braw = at("braw", [P, 2, NCH, GP], F32, S0)
        bdg = at("bdg", [P, 2, NCH, 2 * GP], F32, S0 + 2048)
        bbT = at("bbT", [P, 2, KH, P], F32, S0 + 6144)
        craw = at("craw", [P, 2, KH, NST], F32, S0 + 10240)
        cTt = at("cTt", [P, 2, NCH, 2 * GP], F32, S0 + 12288)
        yaH, yaL = at("yaH", [P, KH, S], F32R, A0 + 73728), at("yaL", [P, KH, S], F32R, A0 + 81920)
        y2H, y2L = at("y2H", [P, KH, S], F32R, A0 + 49152), at("y2L", [P, KH, S], F32R, A0 + 57344)
        ybH = at("ybH", [P, KH, S], F32R, A0 + 65536)
        out_tok = at("out_tok", [P, TB, D], F32, A0)
        B0 = A0 + 90112
        L = at("L", [P, 2, CB[4]], F32, B0)
        pT = at("pT", [P, 2, CB[4]], F32, B0 + 10240)
        qn, kn = at("qn", [P, S], F32, B0 + 20480), at("kn", [P, S], F32, B0 + 22528)
        vtok = at("vtok", [P, TB, P], F32, B0 + 24576)
        score, work = at("score", [P, CB[4]], F32, B0 + 26624), at("work", [P, CB[4]], F32, B0 + 31744)
        relu_b = [at(f"relu{s}", [P, S], F32, B0 + 36864 + 2048 * s) for s in range(2)]
        ybL = at("ybL", [P, KH, S], F32R, B0 + 31744)
        r1, gt, ut, sg, a32, sqx = (at(n, [P, S], F32, B0 + 26624 + 2048 * j) for j, n in
                                    enumerate(("r1", "gt", "ut", "sg", "a32", "sqx")))
        ss1 = at("ss1", [P, S], F32, B0 + 38912)
        eb = at("eb", [P, 2, 2, S], F32, B0)
        et = [at(f"et{j}", [P, 2, S // 2], F32, B0 + 8192 + 2048 * j) for j in range(4)]
        bbS, dgS = at("bbS", [P, 2, P], F32, B0 + 24576), at("dgS", [P, P], F32, B0 + 25600)
        cpS = at("cpS", [P, 4, 2, P], F32, B0 + 36864)
        thg = at("thg", [P, S], F32, B0 + 24576)
        k2, yg = at("k2", [P, S], F32, B0 + 40960), at("yg", [P, S], F32, B0 + 40960)
        t1, t2, t3, t4, gr, gi, hr0, hr1, hi0, hi1 = (
            at(n, [P, S], F32, B0 + 2048 * j) for j, n in
            enumerate(("t1", "t2", "t3", "t4", "gr", "gi", "hr0", "hr1", "hi0", "hi1")))
        kvraw, kiraw = at("kvraw", [P, S], F32, B0), at("kiraw", [P, S], F32, B0 + 2048)
        xaS = at("xaS", [P, S], F32, B0 + 20480)
        mask1 = at("mask1", [P, S], F32, B0 + 40960)
        pw = at("pw", [P, 2, LEVELS, NCH], F32, B0 + 43008)
        vt2 = at("vt2", [P, TB, HD], F32, B0 + 43008)
        wtok = at("wtok", [P, TB, 8], F32, B0 + 44032)
        assert B0 + 44160 <= nc.sbuf_usable_end

        x_in, cst_in, mask_in, glu_full, vec_in, s5_in, out_done = (
            sem(n) for n in ("x_in", "cst_in", "mask_in", "glu_full", "vec_in", "s5_in", "out_done"))
        w_full = [sem(f"w_full{s}") for s in range(2)]
        hi_done, lo_done = sem("hi_done"), sem("lo_done")
        slot_used = sem("slot_used")
        gfree = [sem(f"gfree{s}") for s in range(2)]
        m_full = [sem(f"m_full{s}") for s in range(2)]
        m_used = sem("m_used")
        vstep, astep, pstep = sem("vstep"), sem("astep"), sem("pstep")
        pe_pre, pre_done, init_v, init_a = (sem(n) for n in ("pe_pre", "pre_done", "init_v", "init_a"))
        ss0, r0d, xn_done, hin_done, vec_rdy, s5_cv = (
            sem(n) for n in ("ss0", "r0d", "xn_done", "hin_done", "vec_rdy", "s5_cv"))
        ss_mm, ss_rd, rs_rdy, qn_rdy = (sem(n) for n in ("ss_mm", "ss_rd", "rs_rdy", "qn_rdy"))
        vtr, vt_done, ych = sem("vtr"), sem("vt_done"), sem("ych")
        sc_ready, sc_free, nm, ex, pn = (sem(n) for n in ("sc_ready", "sc_free", "nm", "ex", "pn"))
        tr_mm, t_free, pv, o_free, yo_rdy = (sem(n) for n in ("tr_mm", "t_free", "pv", "o_free", "yo_rdy"))
        ssum, ssm, rr, nt_done = (sem(n) for n in ("ssum", "ssm", "rr", "nt_done"))
        x1_rdy, x1h, x1l = sem("x1_rdy"), sem("x1h"), sem("x1l")
        sg_rdy, a32_rdy, ah_rdy, a_done, dn_done = (sem(n) for n in ("sg_rdy", "a32_rdy", "ah_rdy", "a_done", "dn_done"))
        mod_mm, pw_rdy, e_out = sem("mod_mm"), sem("pw_rdy"), sem("e_out")
        sq2_rdy, sq2_used, h2f, h2h, h2_done = (sem(n) for n in ("sq2_rdy", "sq2_used", "h2f", "h2h", "h2_done"))
        trig_a, trig_r = sem("trig_a"), sem("trig_r")
        kdup, bd_rdy, s5_tr, s5_ev, bb_rdy, rot_rdy = (
            sem(n) for n in ("kdup", "bd_rdy", "s5_tr", "s5_ev", "bb_rdy", "rot_rdy"))
        kv_tr, kv_ev, ix_ready, relu_rdy, r_used = (sem(n) for n in ("kv_tr", "kv_ev", "ix_ready", "relu_rdy", "r_used"))
        xa_rdy, bu_done, bu_free, h_rdy, y_mm, y_free, yg_rdy, ya_h, ya_done = (
            sem(n) for n in ("xa_rdy", "bu_done", "bu_free", "h_rdy", "y_mm", "y_free", "yg_rdy", "ya_h", "ya_done"))
        e_full = [sem(f"e_full{s}") for s in range(2)]
        e_used = sem("e_used")
        th_rdy, y2h, y2_done, ybh, yb_done = (
            sem(n) for n in ("th_rdy", "y2h", "y2_done", "ybh", "yb_done"))
        mg_rdy, mgh, mg_done = sem("mg_rdy"), sem("mgh"), sem("mg_done")
        x3_rdy, xf_rdy, xf_tr, ot_done, fin = (sem(n) for n in ("x3_rdy", "xf_rdy", "xf_tr", "ot_done", "fin"))

        def wait(eng, s, v):
            if not (isinstance(v, int) and v <= 0):
                eng.wait_ge(s, v)

        class Slot:

            def __init__(self, first, j=0, per=0, i=0):
                c = first + j
                self.par = c % 2
                self.n = c + per * i if isinstance(i, int) else i * per + c
                self.half = c // 2 + per // 2 * i if isinstance(i, int) else i * (per // 2) + c // 2
                self.gf = self.half - (KF // 2 if c >= N_KV else 0)

            def next(self, k=2):
                s = Slot(0)
                s.par, s.n, s.half, s.gf = self.par, self.n + k, self.half + k // 2, self.gf + k // 2
                return s

        def settled(eng):
            eng.nop(nofuse=True)

        def freed(eng, s):
            eng.wait_ge(gfree[s.par], s.gf + 1)

        def blk(t, k):
            return t[:, k * P:(k + 1) * P]

        block = ctx.enter_context(nc.Block())

        @block.sync
        def _(sp_):
            for t in range(TB):
                sp_.dma_start(x_tok[:, t, :], x[0, t * P:(t + 1) * P, :]).then_inc(x_in, 16)

            def cols(w, c, n=P):
                return w[0].rearrange("(k p) c -> p k c", p=P)[:, :, bass.ds(c, n)]

            def load(s, src, width=P, shape=KD):
                wait(sp_, lo_done, s.n - 1)
                dst = raw[s.par][:].rearrange("p (k c) -> p k c", k=shape)[:, :, 0:width]
                sp_.dma_start(dst, src).then_inc(w_full[s.par], 16)

            for j, z in enumerate((Z_Q, Z_K, Z_V)):
                load(Slot(N_MIX, j), cols(w_in, z))

            def mix(i, last):
                for j, z in enumerate((Z_U, Z_GC, Z_GB)):
                    load(Slot(3, j, 6, i), cols(w_in, i * P + z))
                if not last:
                    for j, z in enumerate((Z_Q, Z_K, Z_V)):
                        load(Slot(3, 3 + j, 6, i), cols(w_in, i * P + (z + P)))
            with sp_.Fori(0, NPAIR - 1) as i:
                mix(i, False)
            mix(NPAIR - 1, True)
            with sp_.Fori(0, KD // 2) as i:
                for s in range(2):
                    load(Slot(N_WO, s, 2, i), cols(w_out, i * (2 * P) + s * P))
            with sp_.Fori(0, KF) as i:
                load(Slot(N_FF, 0, 2, i), cols(w_gate, i * P))
                load(Slot(N_FF, 1, 2, i), cols(w_up, i * P))
            with sp_.Fori(0, KF // 2) as i:
                for s in range(2):
                    load(Slot(N_DN, s, 2, i), w_down[0][bass.ds(i * (2 * P) + s * P, P), :]
                         .rearrange("p (k c) -> p k c", k=KD))
            load(Slot(N_KV, 0), cols(w_in_2, Y_K))
            load(Slot(N_KV, 1), cols(w_in_2, Y_KI, NKI), NKI)
            with sp_.Fori(0, NPAIR) as i:
                load(Slot(N_IX, 0, 2, i), cols(w_in_2, i * P + Y_QI))
                load(Slot(N_IX, 1, 2, i), cols(w_in_2, i * P + Y_ZB))
            load(Slot(N_S5), cols(w_in_2, Y_XA))

            def s5(j, last):
                for k in range(2):
                    load(Slot(N_S5 + 1, 2 * k, 6, j), cols(w_in_2, j * (2 * P) + (k * P + Y_GA)))
                    load(Slot(N_S5 + 1, 2 * k + 1, 6, j), cols(w_in_2, j * (2 * P) + (k * P + Y_GB)))
                if not last:
                    load(Slot(N_S5 + 1, 4, 6, j), cols(w_in_2, j * P + (Y_XA + P)))
                load(Slot(N_S5 + 1, 4 if last else 5, 6, j), cols(w_in_2, j * P + Y_ZA))
            with sp_.Fori(0, KH - 1) as j:
                s5(j, False)
            s5(KH - 1, True)
            load(Slot(N_AT), cols(w_in_2, Y_Q))

            def at_(i, last):
                s = Slot(N_AT + 1, 0, 2, i)
                wait(sp_, lo_done, s.n - 1)
                for e in range(2):
                    dst = raw[s.par][:].rearrange("p (k e c) -> p k e c", k=KH, e=2)[:, :, e, :]
                    src = w_glu_2[0].rearrange("(k p) c -> p k c", p=P)[:, :, bass.ds(i * P + e * HALF, P)]
                    sp_.dma_start(dst, src).then_inc(glu_full if e else w_full[s.par], 16)
                if not last:
                    load(Slot(N_AT + 1, 1, 2, i), cols(w_in_2, i * P + (Y_Q + P)))
            with sp_.Fori(0, NPAIR - 1) as i:
                at_(i, False)
            at_(NPAIR - 1, True)
            with sp_.Fori(0, KD // 2) as i:
                load(Slot(N_AB, 0, 2, i), cols(w_a_o_2, i * (2 * P), 2 * P), 2 * P, KH)
                load(Slot(N_AB, 1, 2, i), cols(w_b_o_2, i * (2 * P), 2 * P), 2 * P, KH)
            with sp_.Fori(0, KD // 2) as i:
                for s in range(2):
                    load(Slot(N_O2, s, 2, i), cols(w_out_2, i * (2 * P) + s * P))
            for t in range(TB):
                sp_.wait_ge(fin, t + 1)
                sp_.dma_start(out[0, t * P:(t + 1) * P, :], out_tok[:, t, :]).then_inc(out_done, 16)
            sp_.wait_ge(out_done, 16 * TB)

        @block.gpsimd
        def _(pool):
            g = nc.gpsimd
            pool.dma_start(cst[:], consts[:, 0:C_M1]).then_inc(cst_in, 16)
            pool.dma_start(mask1[:], consts[:, C_M1:C_END]).then_inc(mask_in, 16)
            rows = [(g_mix, V_GMIX, 8), (g_conv_out, V_GCONV, 4), (g_attn_out, V_GATT, 4), (g_ffn, V_GFFN, 8),
                    (c_2, V_C, 8), (norm_g_2, V_NG, 8), (b_mod_2, V_BMOD, 24), (b_glu_2, V_BGLU, 8),
                    (d_skip_2, V_DSK, 4)]
            for v, r, n in rows:
                pool.dma_start(row1[r:r + n, :], v.rearrange("a (n p) -> (a n) p", p=P)).then_inc(vec_in, 16)
            pool.dma_start(row1[V_CONV:V_CONV + 12, :],
                           conv_w.rearrange("a w (n p) -> (a w n) p", p=P)).then_inc(vec_in, 16)
            pool.dma_start(row1[V_FG:V_FG + 8, :], final_g_2.rearrange("(n p) -> n p", p=P)).then_inc(vec_in, 16)
            for r, v in ((V_GQ, g_q), (V_GK, g_k)):
                for e in range(2):
                    pool.dma_start(row1[r:r + 1, e * HD:(e + 1) * HD], v).then_inc(vec_in, 16)
            for r, v in ((W_ARE, a_re_2), (W_AIM, a_im_2)):
                pool.dma_start(row2[r:r + NCH, :], v[0].rearrange("(s g) n -> s (g n)", g=2)).then_inc(vec_in, 16)
            pool.dma_start(ldt[W_LDT:W_LDT + NCH, :], log_dt_2[0].rearrange("(s g) -> s g", g=2)).then_inc(vec_in, 16)

            with pool.Fori(0, NPAIR) as i:
                for m in range(6):
                    pool.wait_ge(m_used, i * 6 + (m + 2))
                    pool.dma_start(mraw[m % 2][:], w_mod_2[0][bass.ds(i * (2 * P) + (m // 3) * P, P),
                                                             (m % 3) * D:(m % 3 + 1) * D]).then_inc(m_full[m % 2], 16)

            pool.wait_ge(pw_rdy, 1)
            pool.wait_ge(pv, 2 * NPAIR)
            st = Steps(pool, pstep)
            with pool.Fori(0, NCH // 2) as i:
                st.enter(i, 1 + 6 * LEVELS)
                g.memset(eb[:, :, 0, 0:1], 1.0)
                st.mark(g.memset(eb[:, :, 1, 0:1], 0.0))
                for k in range(LEVELS):
                    n = 1 << k
                    st.need()
                    c, s = eb[:, :, 0, 0:n], eb[:, :, 1, 0:n]
                    wc, ws = (pw[:, e, k, bass.ds(i * 2, 2)].unsqueeze(2).broadcast_to([P, 2, n]) for e in range(2))
                    m = [t[:, :, 0:n] for t in et]
                    st.mark(g.tensor_tensor(m[0], c, wc, ALU.mult))
                    st.mark(g.tensor_tensor(m[1], s, ws, ALU.mult))
                    st.mark(g.tensor_tensor(m[2], c, ws, ALU.mult))
                    last = st.mark(g.tensor_tensor(m[3], s, wc, ALU.mult))
                    st.need(last - 2)
                    st.mark(g.tensor_tensor(eb[:, :, 0, n:2 * n], m[0], m[1], ALU.subtract))
                    st.need(last)
                    st.mark(g.tensor_tensor(eb[:, :, 1, n:2 * n], m[2], m[3], ALU.add))
                st.need()
                for c in range(2):
                    pool.dma_start(e_dram[bass.ds(i * 2 + c, 1)].rearrange("a p e t -> (a p) e t"),
                                   eb[:, c]).then_inc(e_out, 16)
                pool.wait_ge(e_out, i * 32 + 32)
                st.leave(NCH // 2)

            pool.wait_ge(slot_used, N_DN + KF)
            for e, (b, c) in enumerate(((b_re_2, c_re_2), (b_im_2, c_im_2))):
                pool.dma_start(braw[:, e], b[0].rearrange("(s g) n p -> (g n) s p", g=2)).then_inc(s5_in, 16)
                pool.dma_start(craw[:, e], c[0].rearrange("(k g) p n -> (g p) k n", g=8)).then_inc(s5_in, 16)
            pool.wait_ge(s5_ev, 2)
            pool.wait_ge(s5_cv, 1)
            pool.wait_ge(r_used, 6 * NPAIR + 3)
            st.mark(g.memset(cpS[:], 0.0))
            st.need()

            def input_matrix(j):
                g.tensor_copy(bbS[:], dynj(bbT, j)).then_inc(bb_rdy, 1)

            def dynj(t, j):
                return t[:, :, j, :] if isinstance(j, int) else t[:, :, bass.ds(j, 1), :].rearrange("p e j n -> p e (j n)")

            def rotations(c, i):
                pool.wait_ge(e_used, i * 4 + (c + 1))
                src = e_dram[bass.ds(i * 4 + c, 1)] if not isinstance(i, int) else e_dram[i * 4 + c:i * 4 + c + 1]
                pool.dma_start(ebuf[c % 2][:], src.rearrange("a p e t -> (a p) e t")).then_inc(e_full[c % 2], 16)

            def s5(j, last):
                for c in range(4):
                    q = j * 4 + c
                    if not (last and c == 3):
                        rotations(c + 1, j)
                    pool.wait_ge(bu_free, q + 3)
                    g.tensor_tensor(t1[:], t1[:], t2[:], ALU.add).then_inc(rot_rdy, 1)
                    g.tensor_tensor(t3[:], t3[:], t4[:], ALU.subtract).then_inc(rot_rdy, 1)
                    if c == 3 and not last:
                        pool.wait_ge(bu_done, q + 1)
                        input_matrix(j + 1)
                    pool.wait_ge(y_mm, q + 1)
                    if c == 0:
                        dsk = vec[:, j + V_DSK:j + V_DSK + 1] if isinstance(j, int) else vec[:, bass.ds(j + V_DSK, 1)]
                        g.tensor_tensor(dgS[:], ident, dsk.broadcast_to([P, P]), ALU.mult)
                    g.tensor_copy(cpS[:, c, :, 32 * c:32 * c + 32], dynj(cTt, q))
                    pool.wait_ge(e_used, q + 3)
                    g.tensor_tensor((hr0, hr1)[c % 2][:], t1[:], t2[:], ALU.subtract)
                    g.tensor_tensor((hi0, hi1)[c % 2][:], t3[:], t4[:], ALU.add).then_inc(h_rdy, 1)
            input_matrix(0)
            rotations(0, 0)
            with pool.Fori(0, KH - 1) as j:
                s5(j, False)
            s5(KH - 1, True)

        @block.tensor
        def _(pe):
            mm = nc.tensor.matmul

            def transposes(dst, srcs, idn=ident):
                for t, src in enumerate(srcs):
                    m, kk = src.shape[1], src.shape[0]
                    ins = nc.tensor.transpose(dst[0:m, t * P:t * P + kk], src, idn[0:kk, 0:kk])
                return ins

            def products(s, terms):
                pe.wait_ge(lo_done, s.n + 1)
                for k, rh, rl, o, a, z in terms:
                    mm(o, blk(wH[s.par], k), rh, start=a, stop=False)
                    mm(o, blk(wH[s.par], k), rl, start=False, stop=False)
                    ins = mm(o, blk(wL[s.par], k), rh, start=False, stop=z)
                ins.then_inc(slot_used, 1)

            def project(s, m=P, each=None):
                wait(pe, gfree[s.par], s.gf)
                pe.wait_ge(lo_done, s.n + 1)
                o = PB[s.par][0:m, :]
                for k in range(KD):
                    a, b = wH[s.par][:, k * P:k * P + m], wL[s.par][:, k * P:k * P + m]
                    if each is not None:
                        pe.wait_ge(each, k + 1)
                    mm(o, a, hH[:, k, :], start=(k == 0), stop=False)
                    mm(o, a, hL[:, k, :], start=False, stop=False)
                    ins = mm(o, b, hH[:, k, :], start=False, stop=(k == KD - 1))
                ins.then_inc(slot_used, 1)

            def scores(a, q, k):
                for hh in range(2):
                    r = slice(HD * hh, HD * hh + HD)
                    for b in range(TB):
                        u = 4 * hh + b
                        pe.wait_ge(sc_free, a * 8 + (u + 1))
                        mm(SB[u % 2][:, 0:P * (b + 1)], q[r, blkc(b)], k[r, 0:P * (b + 1)],
                           start=True, stop=True).then_inc(sc_ready, 1)

            def blkc(b):
                return slice(b * P, (b + 1) * P)

            def attend(a, v, vcol):
                for hh in range(2):
                    pe.wait_ge(pn, a * 2 + (hh + 1))
                    for kb in range(TB):
                        pe.wait_ge(t_free, a * 8 + (4 * hh + kb + 1))
                        transposes(TBANK[kb % 2], [L[:, hh, CB[b] + P * kb:CB[b] + P * kb + P] for b in range(kb, TB)]
                                   ).then_inc(tr_mm, 1)
                wait(pe, o_free, a + 1)
                for hh in range(2):
                    r = slice(HD * hh, HD * hh + HD)
                    pe.wait_ge(t_free, a * 8 + (4 * hh + 4 + 2))
                    for kb in range(TB):
                        ins = mm(OB[r, P * kb:S], v[:, kb, vcol(hh)], pT[:, hh, OFF[kb]:OFF[kb + 1]],
                                 start=(kb == 0), stop=(kb == TB - 1), skip_group_check=True)
                    ins.then_inc(pv, 1)

            for s in (y_mm, y_mm, ix_ready, xf_tr):
                pe.nop().then_inc(s, 1)
            pe.wait_ge(cst_in, 16)
            pe.wait_ge(vec_in, 16 * 18)
            pe.wait_ge(r0d, 1)
            nc.tensor.transpose(PB[6][:, 0:NV1], row1[0:NV1, :], ident[0:NV1, 0:NV1]).then_inc(pe_pre, 1)
            nc.tensor.transpose(PB[7][:, 0:NV2], row2[0:NV2, :], ident[0:NV2, 0:NV2]).then_inc(pe_pre, 1)
            for f in range(2 * KD):
                src = xn_tok if f < KD else x_tok
                if f == 0:
                    pe.wait_ge(xn_done, 1)
                wait(pe, pre_done, f - 1)
                transposes(PB[f % 2], [src[:, t, (f % KD) * P:(f % KD) * P + P] for t in range(TB)]).then_inc(pe_pre, 1)
            pe.wait_ge(pre_done, 2 * KD)

            def qkv(first, i):
                for j in range(3):
                    project(Slot(first, j, 6, i))

            def head_sums(a, ks):
                freed(pe, ks)
                pe.wait_ge(sc_free, a * 8 + 2)
                for e, sq in enumerate((sqq, sqk)):
                    mm(SB[e][:], bdones, sq[:], start=True, stop=True).then_inc(ss_mm, 1)

            def mix(i, last):
                for j in range(3):
                    project(Slot(3, j, 6, i))
                freed(pe, Slot(2, 0, 6, i))
                transposes(PB[3], [vT[:, blkc(b)] for b in range(TB)]).then_inc(vtr, 1)
                pe.wait_ge(ss_rd, i * 2 + 2)
                pe.wait_ge(qn_rdy, i + 1)
                scores(i, qn, kn)
                if not last:
                    qkv(6, i)
                pe.wait_ge(vt_done, i + 1)
                attend(i, vtok, lambda hh: slice(HD * hh, HD * hh + HD))
                if not last:
                    head_sums(i + 1, Slot(7, 0, 6, i))

            qkv(0, 0)
            freed(pe, Slot(0, 2))
            head_sums(0, Slot(1))
            with pe.Fori(0, NPAIR - 1) as i:
                mix(i, False)
            mix(NPAIR - 1, True)

            pe.wait_ge(ssum, 1)
            mm(PB[4][:], ones[:], ssc[:], start=True, stop=True).then_inc(ssm, 1)
            pe.wait_ge(ssum, 2)
            mm(PB[5][:], ones[:], ssa[:], start=True, stop=True).then_inc(ssm, 1)
            for c in range(3 * KD):
                ins = mm(PB[6][:, c:c + 1], macc[:, blkc(c)], ones[:, 0:1], start=True, stop=True)
            ins.then_inc(mod_mm, 1)
            with pe.Fori(0, KD // 2) as i:
                for s in range(2):
                    sl = Slot(N_WO, s, 2, i)
                    pe.wait_ge(gfree[s], sl.gf)
                    products(sl, [(k, mixH[:, k, :], mixL[:, k, :], PB[s if k < KH else 2 + s][:], k % KH == 0,
                                   k % KH == KH - 1) for k in range(KD)])

            project(Slot(N_FF), each=x1l)
            pe.wait_ge(ssum, 3)
            mm(PB[4][:], ones[:], ss1[:], start=True, stop=True).then_inc(ssm, 1)
            project(Slot(N_FF, 1))
            with pe.Fori(1, KF) as i:
                for s in range(2):
                    project(Slot(N_FF, s, 2, i))

            def down(i, first, last):
                for s in range(2):
                    sl = Slot(N_DN, s, 2, i)
                    pe.wait_ge(lo_done, sl.n + 1)
                    kf = i * 2 + s
                    rh, rl = (t[:, bass.ds(kf, 1), :].rearrange("p k t -> p (k t)") if not isinstance(i, int)
                              else t[:, kf, :] for t in (aH, aL))
                    if first:
                        pe.wait_ge(a_done, kf + 1)
                    for d in (range(KD) if not first or s else (2, 3, 4, 5, 6, 7, 0, 1)):
                        a, z = first and s == 0, last and s == 1
                        if a and d == 0:
                            pe.wait_ge(a_done, KF)
                        mm(PB[d][:], blk(wH[s], d), rh, start=a, stop=False, skip_group_check=True)
                        mm(PB[d][:], blk(wH[s], d), rl, start=False, stop=False, skip_group_check=True)
                        ins = mm(PB[d][:], blk(wL[s], d), rh, start=False, stop=z, skip_group_check=True)
                        if z and d < KD - 1:
                            ins.then_inc(dn_done, 1)
                    ins.then_inc(slot_used, 1)
            down(0, True, False)
            with pe.Fori(1, KF // 2 - 1) as i:
                down(i, False, False)
            down(KF // 2 - 1, False, True)

            for d in range(KD):
                pe.wait_ge(sq2_rdy, d + 1)
                mm(PB[0][:], ones[:], (sqx, a32)[d % 2][:], start=(d == 0), stop=(d == KD - 1),
                   skip_group_check=True).then_inc(sq2_used, 1)
            project(Slot(N_KV, 0), each=h2_done)
            project(Slot(N_KV, 1), NKI)
            pe.wait_ge(bd_rdy, 1)
            for e in range(2):
                transposes(PB[6 + e], [bdg[:, e, 4 * j:4 * j + 4, :].rearrange("p s q -> p (s q)") for j in range(KH)]
                           ).then_inc(s5_tr, 1)
            for e in range(2):
                transposes(PB[4 + e], [craw[:, e, k, :] for k in range(KH)]).then_inc(s5_tr, 1)
            freed(pe, Slot(N_KV, 0))
            transposes(PB[3], [kvraw[:, blkc(b)] for b in range(TB)]).then_inc(kv_tr, 1)
            freed(pe, Slot(N_KV, 1))
            transposes(PB[2], [kiraw[0:NKI, blkc(b)] for b in range(TB)]).then_inc(kv_tr, 1)
            pe.wait_ge(s5_cv, 1)
            pe.wait_ge(kdup, 2)

            with pe.Fori(0, NPAIR) as i:
                project(Slot(N_IX, 0, 2, i))
                project(Slot(N_IX, 1, 2, i))
                freed(pe, Slot(N_IX, 0, 2, i))
                for hh in range(2):
                    r = slice(HD * hh, HD * hh + HD)
                    for b in range(1, TB):
                        u = 3 * hh + b - 1
                        pe.wait_ge(relu_rdy, i * 6 + (u + 1))
                        mm(SB[u % 2][:, 0:P * (b + 1)], qn[r, blkc(b)], k2[r, 0:P * (b + 1)],
                           start=True, stop=True).then_inc(ix_ready, 1)

            project(Slot(N_S5))
            freed(pe, Slot(N_S5))
            pe.wait_ge(kv_ev, 2)
            pe.wait_ge(relu_rdy, 6 * NPAIR + 2)

            def y_out(j, c):
                pe.wait_ge(h_rdy, j * 4 + (c + 2))
                if c == 0:
                    pe.wait_ge(y_free, j + 1)
                    mm(OB[:], dgS[:], xaS[:], start=True, stop=False, skip_group_check=True)
                for e, h in enumerate(((hr0, hr1)[c % 2], (hi0, hi1)[c % 2])):
                    ins = mm(OB[:], cpS[:, c, e, :], h[:], start=False, stop=(c == 3 and e == 1), skip_group_check=True)
                ins.then_inc(y_mm, 1)

            def s5(j, last):
                pe.wait_ge(bb_rdy, j + 1)
                pe.wait_ge(xa_rdy, j + 1)
                for c in range(4):
                    pe.wait_ge(bu_free, j * 4 + (c + 1))
                    r = slice(32 * c, 32 * c + 32)
                    for e in range(2):
                        ins = mm((SB if c % 2 == 0 else TBANK)[e][:], bbS[r, e, :], xaS[r, :], start=True, stop=True)
                    ins.then_inc(bu_done, 1)
                    project(Slot(N_S5 + 1, c, 6, j))
                    if c:
                        y_out(j, c - 1)
                if not last:
                    project(Slot(N_S5 + 1, 4, 6, j))
                project(Slot(N_S5 + 1, 4 if last else 5, 6, j))
                y_out(j, 3)
            with pe.Fori(0, KH - 1) as j:
                s5(j, False)
            s5(KH - 1, True)

            project(Slot(N_AT))
            freed(pe, Slot(N_AT))
            pe.wait_ge(bu_free, NCH + 2)
            pe.wait_ge(y_free, KH + 1)
            scores(NPAIR, qn, kn)
            pe.wait_ge(ya_done, KH + 1)

            def att(i, last):
                sl = Slot(N_AT + 1, 0, 2, i)
                pe.wait_ge(gfree[1], sl.gf)
                products(sl, [(2 * k + e, yaH[:, k, :], yaL[:, k, :], PB[1 + 2 * e][:], k == 0, k == KH - 1)
                              for e in range(2) for k in range(KH)])
                if not last:
                    project(Slot(N_AT + 1, 1, 2, i))
                attend(i + NPAIR, vt2, lambda hh: slice(0, HD))
                if not last:
                    freed(pe, Slot(N_AT + 1, 1, 2, i))
                    scores(i + (NPAIR + 1), qn, kn)
            with pe.Fori(0, NPAIR - 1) as i:
                att(i, False)
            att(NPAIR - 1, True)

            pe.wait_ge(y2_done, KH)
            pe.wait_ge(yb_done, KH)
            with pe.Fori(0, KD // 2) as i:
                for s, (rh, rl) in enumerate(((y2H, y2L), (ybH, ybL))):
                    sl = Slot(N_AB, s, 2, i)
                    pe.wait_ge(gfree[s], sl.gf)
                    products(sl, [(2 * k + e, rh[:, k, :], rl[:, k, :], PB[s + 2 * e][:], k == 0, k == KH - 1)
                                  for e in range(2) for k in range(KH)])
            def to_tokens(i):
                for s in range(2):
                    pe.wait_ge(xf_rdy, i * 2 + (s + 1))
                    wait(pe, ot_done, i * 2 + 1)
                    transposes(TBANK[s], [(t3, t4)[s][:, blkc(b)] for b in range(TB)]).then_inc(xf_tr, 1)

            project(Slot(N_O2, 0), each=mg_done)
            project(Slot(N_O2, 1))
            with pe.Fori(0, KD // 2 - 1) as i:
                project(Slot(N_O2, 2, 2, i))
                to_tokens(i)
                project(Slot(N_O2, 3, 2, i))
            to_tokens(KD // 2 - 1)
            pe.wait_ge(ssum, 4)
            for t in range(TB):
                ins = mm(PB[4][:, t:t + 1], gr[:, blkc(t)], ones[:, 0:1], start=True, stop=True)
            ins.then_inc(ssm, 1)

        @block.scalar
        def _(act):
            A = nc.scalar.activation

            def copy(o, i_, scale=1.0):
                return A(o, i_, ACT.Copy, scale=scale)

            def split_hi(s):
                act.wait_ge(w_full[s.par], s.half * 16 + 16)
                wait(act, slot_used, s.n - 1)
                copy(wH[s.par][:], raw[s.par][:]).then_inc(hi_done, 1)

            def used(s):
                act.wait_ge(slot_used, s.n + 1)

            def rsqrt(o, ps, scale, k, done):
                act.wait_ge(ssm, k)
                A(o, ps, ACT.Ln, bias=epst[:, 0:1], scale=scale).then_inc(astep, 1)
                a_n[0] += 1
                act.wait_ge(astep, a_n[0])
                A(o, o, ACT.Exp, scale=-0.5).then_inc(done, 1)
            a_n = [0]

            def load_set(n):
                nc.scalar.add_instruction(mybir.InstLoadActFuncSet(
                    name=nc.get_next_instruction_name(), act_func_set_id=n, ins=[], outs=[]))

            act.wait_ge(init_v, 1)
            act.wait_ge(x_in, 16 * TB)
            for t in range(TB):
                ins = A(xn_tok[:, t, :], x_tok[:, t, :], ACT.Square, accum_out=sm[:, t:t + 1])
            ins.then_inc(astep, 1)
            a_n[0] += 1
            act.wait_ge(astep, a_n[0])
            A(sm[:, 4:8], sm[:, 0:4], ACT.Ln, bias=epst[:, 0:1], scale=1.0 / D).then_inc(astep, 1)
            a_n[0] += 1
            act.wait_ge(astep, a_n[0])
            A(sm[:, 8:12], sm[:, 4:8], ACT.Exp, scale=-0.5).then_inc(ss0, 1)
            split_hi(Slot(0))
            split_hi(Slot(1))
            act.wait_ge(vec_rdy, 1)
            for k in range(KD):
                act.wait_ge(pe_pre, 2 + k + 1)
                A(hH[:, k, :], PB[k % 2][:], ACT.Identity, scale=vec[:, V_GMIX + k:V_GMIX + k + 1]).then_inc(hin_done, 1)
            A(csil[:], vec[:, V_C:V_C + KD], ACT.Silu).then_inc(trig_a, 1)
            act.wait_ge(trig_r, 1)
            A(sp[:, 6:8, :], sp[:, 4:6, :], ACT.Sin).then_inc(trig_a, 1)

            def qkv(first, i, a):
                s = [Slot(first, j, 6, i) for j in range(3)]
                wait(act, qn_rdy, a)
                wait(act, ss_mm, a * 2)
                for sl, dst, sq in ((s[0], qraw, sqq), (s[1], kraw, sqk)):
                    used(sl)
                    copy(dst[:], PB[sl.par][:])
                    A(sq[:], PB[sl.par][:], ACT.Square).then_inc(gfree[sl.par], 1)
                    split_hi(sl.next())
                used(s[2])
                wait(act, vtr, a)
                copy(vT[:], PB[s[2].par][:]).then_inc(gfree[s[2].par], 1)

            def head_rsqrt(a):
                for e, r in enumerate((rq, rk)):
                    act.wait_ge(ss_mm, a * 2 + (e + 1))
                    A(r[:], SB[e][:], ACT.Ln, bias=epst[:, 0:1], scale=1.0 / HD).then_inc(ss_rd, 1)
                    act.wait_ge(ss_rd, a * 2 + (e + 1))
                    A(r[:], r[:], ACT.Exp, scale=-0.5).then_inc(rs_rdy, 1)

            def softmax(a):
                for hh in range(2):
                    act.wait_ge(nm, a * 2 + (hh + 1))
                    for b in range(TB):
                        c = 4 * hh + b
                        l = L[:, hh, CB[b]:CB[b + 1]]
                        ins = A(l, l, ACT.Exp, bias=nmx[:, c:c + 1], accum_out=rs[:, c:c + 1])
                    ins.then_inc(ex, 1)

            def p_evac(a):
                for hh in range(2):
                    for kb in range(TB):
                        act.wait_ge(tr_mm, a * 8 + (4 * hh + kb + 1))
                        n = S - P * kb
                        copy(pT[:, hh, OFF[kb]:OFF[kb + 1]], TBANK[kb % 2][:, 0:n]).then_inc(t_free, 1)

            def mix(i, last):
                head_rsqrt(i)
                u, gc, gb = (Slot(3, j, 6, i) for j in range(3))
                used(u)
                if not (isinstance(i, int) and i == 0):
                    wait(act, ych, i + 1)
                copy(u_s[:], PB[u.par][:]).then_inc(gfree[u.par], 1)
                split_hi(u.next())
                used(gc)
                split_hi(gc.next())
                used(gb)
                split_hi(gb.next())
                freed(act, gb)
                A(sqc[:], yc[:], ACT.Square)
                A(dyn(mixH, i), yc[:], ACT.Identity, scale=vec[:, bass.ds(i + V_GCONV, 1)]).then_inc(ych, 1)
                act.wait_ge(vtr, i + 1)
                copy(vtok[:].rearrange("p b n -> p (b n)"), PB[3][:]).then_inc(vt_done, 1)
                softmax(i)
                if not last:
                    qkv(6, i, i + 1)
                p_evac(i)
                if not last:
                    split_hi(Slot(6, 2, 6, i).next())
                act.wait_ge(pv, i * 2 + 2)
                copy(yo[:], OB[:])
                A(sqa[:], OB[:], ACT.Square)
                A(dyn(mixH, i + KH), OB[:], ACT.Identity, scale=vec[:, bass.ds(i + V_GATT, 1)]).then_inc(o_free, 1)

            def dyn(t, k):
                return t[:, k, :] if isinstance(k, int) else t[:, bass.ds(k, 1), :].rearrange("p k t -> p (k t)")

            for s, n in ((t_free, 2), (ych, 1), (y_free, 1), (o_free, 1)):
                for _ in range(n):
                    act.nop().then_inc(s, 1)
            qkv(0, 0, 0)
            split_hi(Slot(0, 2).next())
            load_set(6)
            with act.Fori(0, NPAIR - 1) as i:
                mix(i, False)
            mix(NPAIR - 1, True)

            rsqrt(rc[:], PB[4][:], 1.0 / HALF, 1, rr)
            rsqrt(ra[:], PB[5][:], 1.0 / HALF, 2, rr)
            with act.Fori(0, KD // 2) as i:
                for s in range(2):
                    sl, d = Slot(N_WO, s, 2, i), i * 2 + s
                    used(sl)
                    split_hi(sl.next())
                    act.wait_ge(x1_rdy, d + 1)
                    A(sqx[:], dyn(xT, d), ACT.Square)
                    A(dyn(hH, d), dyn(xT, d), ACT.Identity, scale=vec[:, bass.ds(d + V_GFFN, 1)]).then_inc(x1h, 1)

            rsqrt(r1[:], PB[4][:], 1.0 / D, 3, rr)
            with act.Fori(0, KF) as i:
                g_, u_ = Slot(N_FF, 0, 2, i), Slot(N_FF, 1, 2, i)
                used(g_)
                split_hi(g_.next())
                freed(act, g_)
                A(sg[:], gt[:], ACT.Silu).then_inc(sg_rdy, 1)
                used(u_)
                split_hi(u_.next())
                act.wait_ge(a32_rdy, i + 1)
                copy(dyn(aH, i), a32[:]).then_inc(ah_rdy, 1)
            with act.Fori(0, KF // 2) as i:
                for s in range(2):
                    sl = Slot(N_DN, s, 2, i)
                    used(sl)
                    split_hi(sl.next())

            for d in range(KD):
                act.wait_ge(x1_rdy, KD + d + 1)
                wait(act, sq2_used, d - 1)
                A((sqx, a32)[d % 2][:], xT[:, d, :], ACT.Square).then_inc(sq2_rdy, 1)
            act.wait_ge(sq2_used, KD)
            rsqrt(r1[:], PB[0][:], 1.0 / D, 3, rr)
            for d in range(KD):
                act.wait_ge(h2f, d + 1)
                A(hH[:, d, :], (sg, a32)[d % 2][:], ACT.Identity, bias=mod[:, d:d + 1]).then_inc(h2h, 1)
            kv, ki = Slot(N_KV, 0), Slot(N_KV, 1)
            used(kv)
            act.wait_ge(e_out, 16 * NCH)
            copy(kvraw[:], PB[0][:]).then_inc(gfree[0], 1)
            split_hi(kv.next())
            used(ki)
            copy(kiraw[0:NKI, :], PB[1][0:NKI, :]).then_inc(gfree[1], 1)
            split_hi(ki.next())
            for e in range(2):
                act.wait_ge(s5_tr, e + 1)
                copy(bbT[:, e].rearrange("p k n -> p (k n)"), PB[6 + e][:]).then_inc(s5_ev, 1)
            act.wait_ge(kv_tr, 1)
            copy(vt2[:], PB[3][:].rearrange("p (b n) -> p b n", b=TB)[:, :, HD:2 * HD]).then_inc(kv_ev, 1)
            act.wait_ge(kv_tr, 2)
            copy(wtok[:], PB[2][:].rearrange("p (b n) -> p b n", b=TB)[:, :, HD:HD + 8]).then_inc(kv_ev, 1)

            act.nop().then_inc(relu_rdy, 1)
            act.nop().then_inc(relu_rdy, 1)
            with act.Fori(0, NPAIR) as i:
                q, z = Slot(N_IX, 0, 2, i), Slot(N_IX, 1, 2, i)
                used(q)
                wait(act, ix_ready, i * 6 + 1)
                copy(qn[:], PB[0][:]).then_inc(gfree[0], 1)
                split_hi(q.next())
                used(z)
                for hh in range(2):
                    for b in range(1, TB):
                        u = 3 * hh + b - 1
                        act.wait_ge(ix_ready, i * 6 + (u + 2))
                        act.wait_ge(r_used, i * 6 + (u + 2))
                        A(relu_b[u % 2][:, 0:P * (b + 1)], SB[u % 2][:, 0:P * (b + 1)], ACT.Relu,
                          scale=IDX_SCALE).then_inc(relu_rdy, 1)
                A(dyn(szb, i), PB[1][:], ACT.Silu).then_inc(gfree[1], 1)
                split_hi(z.next())

            xa = Slot(N_S5)
            used(xa)
            copy(xaS[:], PB[xa.par][:]).then_inc(xa_rdy, 1)
            act.wait_ge(xa_rdy, 1)
            act.nop().then_inc(gfree[xa.par], 1)
            split_hi(xa.next())

            def s5(j, last):
                for c in range(4):
                    s = Slot(N_S5 + 1, c, 6, j)
                    used(s)
                    A(dyn((tga, tgb)[c % 2], j * 2 + c // 2), PB[s.par][:], ACT.Tanh, scale=0.5).then_inc(gfree[s.par], 1)
                    split_hi(s.next())
                if not last:
                    s = Slot(N_S5 + 1, 4, 6, j)
                    used(s)
                    copy(xaS[:], PB[s.par][:]).then_inc(xa_rdy, 1)
                    act.wait_ge(xa_rdy, j + 2)
                    act.nop().then_inc(gfree[s.par], 1)
                    split_hi(s.next())
                s = Slot(N_S5 + 1, 4 if last else 5, 6, j)
                used(s)
                A(dyn(sza, j), PB[s.par][:], ACT.Silu).then_inc(gfree[s.par], 1)
                if last:
                    act.wait_ge(glu_full, 16)
                split_hi(s.next())
                act.wait_ge(y_mm, j * 4 + 6)
                wait(act, ya_done, j + 1)
                A(yg[:], OB[:], ACT.Gelu_apprx_tanh).then_inc(y_free, 1)
                act.wait_ge(y_free, j + 2)
                copy(dyn(yaH, j), yg[:]).then_inc(ya_h, 1)
            with act.Fori(0, KH - 1) as j:
                s5(j, False)
            s5(KH - 1, True)

            q = Slot(N_AT)
            used(q)
            copy(qn[:], PB[0][:], HD ** -0.5).then_inc(gfree[0], 1)
            split_hi(q.next())

            def att(i, last):
                softmax(i + NPAIR)
                s = Slot(N_AT + 1, 0, 2, i)
                used(s)
                if not last:
                    act.wait_ge(glu_full, i * 16 + 32)
                split_hi(s.next())
                A(thg[:], PB[3][:], ACT.Tanh, bias=hbg[:, bass.ds(i, 1)], scale=0.5).then_inc(th_rdy, 1)
                freed(act, s)
                copy(dyn(y2H, i), dyn(sza, i), 0.5).then_inc(y2h, 1)
                if not last:
                    s = Slot(N_AT + 1, 1, 2, i)
                    used(s)
                    copy(qn[:], PB[0][:], HD ** -0.5).then_inc(gfree[0], 1)
                p_evac(i + NPAIR)
                if not last:
                    split_hi(s.next())
                act.wait_ge(o_free, i + (NPAIR + 1) + 1)
                copy(dyn(ybH, i), dyn(szb, i)).then_inc(ybh, 1)
            with act.Fori(0, NPAIR - 1) as i:
                att(i, False)
            att(NPAIR - 1, True)

            with act.Fori(0, KD // 2) as i:
                for s in range(2):
                    sl = Slot(N_AB, s, 2, i)
                    used(sl)
                    split_hi(sl.next())
                for e in range(2):
                    act.wait_ge(mg_rdy, i * 2 + (e + 1))
                    copy(dyn(hH, i * 2 + e), dyn(tga, i * 2 + e), 0.5).then_inc(mgh, 1)

            def out2(i, last):
                for s in range(2):
                    sl, d = Slot(N_O2, s, 2, i), i * 2 + s
                    if not last:
                        used(sl)
                        split_hi(sl.next())
                    act.wait_ge(x3_rdy, d + 1)
                    act.wait_ge(ot_done, i * 2 + 1)
                    A((t1, t2)[s][:], dyn(xT, d), ACT.Square)
                    A((t3, t4)[s][:], dyn(xT, d), ACT.Identity, scale=vec[:, bass.ds(d + V_FG, 1)]).then_inc(xf_rdy, 1)
            with act.Fori(0, KD // 2 - 1) as i:
                out2(i, False)
            out2(KD // 2 - 1, True)
            act.wait_ge(ssm, 4)
            A(sm[:, 12:16], PB[4][:, 0:4], ACT.Ln, bias=epst[:, 0:1], scale=1.0 / D).then_inc(astep, 1)
            a_n[0] += 1
            act.wait_ge(astep, a_n[0])
            A(sm[:, 16:20], sm[:, 12:16], ACT.Exp, scale=-0.5).then_inc(rr, 1)

        @block.vector
        def _(dve):
            v = nc.vector
            TT, TS, STT = v.tensor_tensor, v.tensor_scalar, v.scalar_tensor_tensor
            MU, AD, SU = ALU.mult, ALU.add, ALU.subtract
            st = Steps(dve, vstep)
            mark, need = st.mark, st.need

            def dyn(t, k):
                return t[:, k, :] if isinstance(k, int) else t[:, bass.ds(k, 1), :].rearrange("p k t -> p (k t)")

            def col(t, k):
                return t[:, bass.ds(k, 1)] if not isinstance(k, int) else t[:, k:k + 1]

            def split_lo(s):
                dve.wait_ge(hi_done, s.n + 1)
                TT(wL[s.par][:], raw[s.par][:], wH[s.par][:].bitcast(F32), SU).then_inc(lo_done, 1)

            def used(s):
                dve.wait_ge(slot_used, s.n + 1)

            def newton(r, ss, scale, ta, tb):
                mark(TS(ta, ss, scale, EPS, MU, AD))
                mark(TT(tb, r, r, MU))
                need()
                mark(TT(tb, tb, ta, MU))
                need()
                mark(TS(tb, tb, -0.5, 1.5, MU, AD))
                need()
                return mark(TT(r, r, tb, MU))

            for s, n in ((sc_free, 2), (m_used, 3), (r_used, 3), (bu_free, 2), (e_used, 2), (h_rdy, 1), (ot_done, 1), (ya_done, 1)):
                for _ in range(n):
                    dve.nop().then_inc(s, 1)
            v.memset(epst[:], EPS).then_inc(init_v, 1)
            v.memset(ones[:], 1.0)
            v.memset(macc[:], 0.0)
            v.memset(ssc[:], 0.0)
            m_init = mark(v.memset(ssa[:], 0.0))
            dve.wait_ge(vec_in, 16 * 18)
            for e in range(2):
                ins = v.tensor_copy(row2[32:48, e * HD:(e + 1) * HD], ldt[32:48, e:e + 1].broadcast_to([NCH, HD]))
            ins.then_inc(r0d, 1)
            dve.wait_ge(ss0, 1)
            need(newton(sm[:, 8:12], sm[:, 0:4], 1.0 / D, sm[:, 12:16], sm[:, 16:20]))
            for t in range(TB):
                ins = TS(xn_tok[:, t, :], x_tok[:, t, :], sm[:, 8 + t:9 + t], None, MU)
            ins.then_inc(xn_done, 1)
            dve.wait_ge(pe_pre, 2)
            v.tensor_copy(vec[:], PB[6][:, 0:NV1])
            ins = v.tensor_copy(svec[:], PB[7][:, 0:NV2])
            mark(ins)
            need()
            mark(TS(hbg[:], vec[:, V_BGLU + KH:V_BGLU + 2 * KH], 0.5, None, MU))
            TS(vec[:, V_GQ:V_GQ + 1], vec[:, V_GQ:V_GQ + 1], HD ** -0.5, None, MU).then_inc(vec_rdy, 1)
            split_lo(Slot(0))
            for k in range(KD):
                dve.wait_ge(pe_pre, 2 + k + 1)
                dve.wait_ge(hin_done, k + 1)
                STT(hL[:, k, :], PB[k % 2][:], vec[:, V_GMIX + k:V_GMIX + k + 1], hH[:, k, :].bitcast(F32),
                    MU, SU).then_inc(pre_done, 1)
            for k in range(KD):
                dve.wait_ge(pe_pre, 2 + KD + k + 1)
                v.tensor_copy(xT[:, k, :], PB[k % 2][:]).then_inc(pre_done, 1)
            split_lo(Slot(1))
            mark(v.memset(cuP[:, 0:2], 0.0))

            def par(k):
                return sp[:, k, :]

            def seq(*fs):
                for f in fs:
                    need()
                    mark(f())

            MAGIC, PI, TWO_PI = 12582912.0, 3.1415925, 6.283185307179586
            LN2H, LN2L = 0.693359375, -2.12194440e-4

            def exp(dst, src):
                z, n, r, p = par(8), par(9), par(10), par(11)
                seq(lambda: TS(z, src, -87.0, 88.0, ALU.max, ALU.min),
                    lambda: TS(n, z, 1.4426950408889634, MAGIC, MU, AD),
                    lambda: TS(n, n, MAGIC, None, SU),
                    lambda: STT(r, n, -LN2H, z, MU, AD),
                    lambda: STT(r, n, -LN2L, r, MU, AD),
                    lambda: TS(p, r, 1 / 5040, None, MU))
                for c in (1 / 720, 1 / 120, 1 / 24, 1 / 6, 1 / 2, 1.0):
                    seq(lambda: STT(p, p, c, r, AD, MU))
                seq(lambda: TS(n, n, 127.0, None, AD),
                    lambda: v.tensor_copy(spi[:], n),
                    lambda: TS(spi[:], spi[:], 23, None, ALU.logical_shift_left),
                    lambda: STT(dst, p, 1.0, spi[:].bitcast(F32), AD, MU))

            are, aim = svec[:, 0:NCH], svec[:, NCH:2 * NCH]
            exp(par(0), svec[:, 2 * NCH:3 * NCH])
            seq(lambda: TT(par(12), are, par(0), MU))
            exp(par(1), par(12))
            C1, C2 = 6.28125, 1.93500518798828125e-3
            C3 = TWO_PI - C1 - C2
            th, n, r, t = par(2), par(9), par(4), par(10)
            seq(lambda: TT(th, aim, par(0), MU),
                lambda: TS(n, th, 1 / TWO_PI, MAGIC, MU, AD),
                lambda: TS(n, n, MAGIC, None, SU),
                lambda: STT(th, n, -C1, th, MU, AD),
                lambda: STT(th, n, -C2, th, MU, AD),
                lambda: STT(th, n, -C3, th, MU, AD),
                lambda: TS(r, th, PI, -PI, ALU.min, ALU.max),
                lambda: TS(par(5), th, TWO_PI / 4, None, AD),
                lambda: TS(t, par(5), PI, -TWO_PI, ALU.is_gt, MU),
                lambda: TT(par(5), par(5), t, AD),
                lambda: TS(par(5), par(5), PI, -PI, ALU.min, ALU.max))
            need()
            v.tensor_copy(par(3), par(5)).then_inc(trig_r, 1)
            dve.wait_ge(trig_a, 2)
            sn, cs = par(6), par(7)
            nr, ni, den, rd, crr, cri = (par(k) for k in (12, 13, 14, 8, 15, 16))
            seq(lambda: TT(nr, par(1), cs, MU),
                lambda: TS(nr, nr, -1.0, None, AD),
                lambda: TT(ni, par(1), sn, MU),
                lambda: TT(den, are, are, MU),
                lambda: TT(t, aim, aim, MU),
                lambda: TT(den, den, t, AD),
                lambda: v.reciprocal(rd, den),
                lambda: TT(crr, nr, are, MU),
                lambda: TT(t, ni, aim, MU),
                lambda: TT(crr, crr, t, AD),
                lambda: TT(crr, crr, rd, MU),
                lambda: TT(cri, ni, are, MU),
                lambda: TT(t, nr, aim, MU),
                lambda: TT(cri, cri, t, SU),
                lambda: TT(cri, cri, rd, MU))
            mark(v.tensor_copy(pw[:, 0, 0, :], cs))
            mark(v.tensor_copy(pw[:, 1, 0, :], sn))
            for k in range(LEVELS - 1):
                c, s = pw[:, 0, k, :], pw[:, 1, k, :]
                need()
                mark(TT(par(9), c, s, SU))
                mark(TT(par(10), c, s, AD))
                need()
                mark(STT(pw[:, 1, k + 1, :], c, 2.0, s, MU, MU))
                mark(TT(pw[:, 0, k + 1, :], par(9), par(10), MU))
            need()
            v.tensor_copy(par(17), par(9)).then_inc(pw_rdy, 1)

            def qk_norm(a):
                dve.wait_ge(rs_rdy, a * 2 + 1)
                STT(qn[:], qraw[:], vec[:, V_GQ:V_GQ + 1], rq[:], MU, MU)
                dve.wait_ge(rs_rdy, a * 2 + 2)
                STT(kn[:], kraw[:], vec[:, V_GK:V_GK + 1], rk[:], MU, MU).then_inc(qn_rdy, 1)

            def score_max(a, masks):
                for hh in range(2):
                    for b in range(TB):
                        u, c = 4 * hh + b, 4 * hh + b
                        dve.wait_ge(sc_ready, a * 8 + (u + 1))
                        settled(dve)
                        v.tensor_tensor_reduce(L[:, hh, CB[b]:CB[b + 1]], SB[u % 2][:, 0:P * (b + 1)], masks[b], 1.0,
                                               GONE, AD, ALU.max, mx[:, c:c + 1]).then_inc(sc_free, 1)
                    dve.wait_ge(sc_free, a * 8 + (4 * hh + 4 + 2))
                    TS(nmx[:, 4 * hh:4 * hh + 4], mx[:, 4 * hh:4 * hh + 4], -1.0, None, MU).then_inc(nm, 1)

            def normalise(a):
                for hh in range(2):
                    dve.wait_ge(ex, a * 2 + (hh + 1))
                    mark(v.reciprocal(rinv[:, 4 * hh:4 * hh + 4], rs[:, 4 * hh:4 * hh + 4]))
                    need()
                    for b in range(TB):
                        l = L[:, hh, CB[b]:CB[b + 1]]
                        ins = TS(l, l, rinv[:, 4 * hh + b:4 * hh + b + 1], None, MU)
                    ins.then_inc(pn, 1)

            def mod_rows(i, ms):
                for m in ms:
                    dve.wait_ge(m_full[m % 2], i * 48 + 16 * (m // 2 + 1))
                    wait(dve, m_used, i * 6 + m + 1)
                    o = macc[:, (m % 3) * D:(m % 3 + 1) * D]
                    STT(o, mraw[m % 2][:], col(csil, i * 2 + m // 3), o, MU, AD).then_inc(m_used, 1)

            def mix(i, last):
                qk_norm(i)
                u, gc, gb = (Slot(3, j, 6, i) for j in range(3))
                split_lo(u.next())
                used(gc)
                freed(dve, u)
                mark(TT(cuP[:, 2:S + 2], PB[gc.par][:], u_s[:], MU))
                need()
                TS(cv[:], cuP[:, 2:S + 2], col(vec, i + (V_CONV + 8)), None, MU).then_inc(gfree[gc.par], 1)
                split_lo(gc.next())
                freed(dve, gc)
                mark(STT(cv[:], cuP[:, 1:S + 1], col(vec, i + (V_CONV + 4)), cv[:], MU, AD))
                need()
                mark(STT(cv[:], cuP[:, 0:S], col(vec, i + V_CONV), cv[:], MU, AD))
                used(gb)
                need()
                wait(dve, ych, i + 1)
                TT(yc[:], PB[gb.par][:], cv[:], MU).then_inc(gfree[gb.par], 1)
                score_max(i, [mask1[:, S - P * (b + 1):S] for b in range(TB)])
                split_lo(gb.next())
                dve.wait_ge(ych, i + 2)
                mark(TT(ssc[:], ssc[:], sqc[:], AD))
                mark(STT(dyn(mixL, i), yc[:], col(vec, i + V_GCONV), dyn(mixH, i).bitcast(F32), MU, SU))
                mod_rows(i, range(0, 2))
                normalise(i)
                if not last:
                    split_lo(Slot(3, 3, 6, i).next())
                    mod_rows(i, range(2, 4))
                    split_lo(Slot(3, 4, 6, i).next())
                    mod_rows(i, range(4, 6))
                    split_lo(Slot(3, 5, 6, i).next())
                else:
                    mod_rows(i, range(2, 6))
                dve.wait_ge(o_free, i + 2)
                mark(TT(ssa[:], ssa[:], sqa[:], AD))
                mark(STT(dyn(mixL, i + KH), yo[:], col(vec, i + V_GATT), dyn(mixH, i + KH).bitcast(F32), MU, SU))

            need(m_init)
            dve.wait_ge(trig_a, 1)
            for j in range(3):
                split_lo(Slot(0, j).next())
            with dve.Fori(0, NPAIR - 1) as i:
                st.enter(i, MIX_STEPS)
                mix(i, False)
                st.leave(NPAIR - 1)
            mix(NPAIR - 1, True)
            need()
            v.memset(ss1[:], 0.0).then_inc(ssum, 1)
            v.memset(nt1[:], 0.0).then_inc(ssum, 1)

            dve.wait_ge(mod_mm, 1)
            mark(TT(mod[:], PB[6][:, 0:3 * KD], vec[:, V_BMOD:V_BMOD + 3 * KD], AD))
            need()
            mark(STT(gs[:], mod[:, KD:2 * KD], 1.0, vec[:, V_NG:V_NG + KD], AD, MU))
            dve.wait_ge(rr, 1)
            need(newton(rc[:], PB[4][:], 1.0 / HALF, nt1[:], nt2[:]))
            dve.wait_ge(rr, 2)
            need(newton(ra[:], PB[5][:], 1.0 / HALF, nt1[:], nt2[:]))
            with dve.Fori(0, KD // 2) as i:
                st.enter(i, 8)
                for s in range(2):
                    sl, d = Slot(N_WO, s, 2, i), i * 2 + s
                    used(sl)
                    mark(TT(wo1[:], PB[s][:], rc[:], MU))
                    TT(wo2[:], PB[2 + s][:], ra[:], MU).then_inc(gfree[s], 1)
                    need()
                    mark(TT(dyn(xT, d), dyn(xT, d), wo1[:], AD))
                    freed(dve, sl)
                    need()
                    TT(dyn(xT, d), dyn(xT, d), wo2[:], AD).then_inc(x1_rdy, 1)
                    split_lo(sl.next())
                    dve.wait_ge(x1h, d + 1)
                    mark(TT(ss1[:], ss1[:], sqx[:], AD))
                    STT(dyn(hL, d), dyn(xT, d), col(vec, d + V_GFFN), dyn(hH, d).bitcast(F32), MU, SU).then_inc(x1l, 1)
                    need()
                    mark(v.memset(m8[:, 0, 0:1], 0.0))
                st.leave(KD // 2)
            need()
            v.memset(m8[:, 0, 0:1], 0.0).then_inc(ssum, 1)

            dve.wait_ge(rr, 3)
            need(newton(r1[:], PB[4][:], 1.0 / D, gt[:], ut[:]))
            with dve.Fori(0, KF) as i:
                st.enter(i, 1)
                g_, u_ = Slot(N_FF, 0, 2, i), Slot(N_FF, 1, 2, i)
                used(g_)
                TT(gt[:], PB[0][:], r1[:], MU).then_inc(gfree[0], 1)
                split_lo(g_.next())
                used(u_)
                TT(ut[:], PB[1][:], r1[:], MU).then_inc(gfree[1], 1)
                split_lo(u_.next())
                dve.wait_ge(sg_rdy, i + 1)
                freed(dve, u_)
                TT(a32[:], sg[:], ut[:], MU).then_inc(a32_rdy, 1)
                dve.wait_ge(ah_rdy, i + 1)
                TT(dyn(aL, i), a32[:], dyn(aH, i).bitcast(F32), SU).then_inc(a_done, 1)
                mark(v.memset(m8[:, 0, 0:1], 0.0))
                st.leave(KF)
            with dve.Fori(0, KF // 2) as i:
                for s in range(2):
                    split_lo(Slot(N_DN, s, 2, i).next())

            for d in range(KD):
                if d < KD - 1:
                    dve.wait_ge(dn_done, d + 1)
                else:
                    dve.wait_ge(slot_used, N_DN + KF)
                TT(xT[:, d, :], xT[:, d, :], PB[d][:], AD).then_inc(x1_rdy, 1)
            v.memset(cTt[:], 0.0)
            mark(v.memset(bdg[:], 0.0))
            dve.wait_ge(rr, 4)
            need(newton(r1[:], PB[0][:], 1.0 / D, gt[:], ut[:]))

            def h2_low(d):
                dve.wait_ge(h2h, d + 1)
                STT(hL[:, d, :], (sg, a32)[d % 2][:], mod[:, d:d + 1], hH[:, d, :].bitcast(F32), AD, SU
                    ).then_inc(h2_done, 1)
            for d in range(KD):
                wait(dve, h2_done, d - 1)
                STT((sg, a32)[d % 2][:], xT[:, d, :], gs[:, d:d + 1], r1[:], MU, MU).then_inc(h2f, 1)
                if d:
                    h2_low(d - 1)
            h2_low(KD - 1)

            dve.wait_ge(s5_in, 64)
            dve.wait_ge(e_out, 16 * NCH)

            def over(k):
                return par(k).unsqueeze(2).broadcast_to([P, NCH, GP])
            tb_ = [t[:, 0:NCH * GP].rearrange("p (s q) -> p s q", q=GP) for t in (t3, t4, gr, gi)]
            mark(TT(tb_[0], braw[:, 0], over(15), MU))
            mark(TT(tb_[1], braw[:, 1], over(16), MU))
            mark(TT(tb_[2], braw[:, 1], over(15), MU))
            mark(TT(tb_[3], braw[:, 0], over(16), MU))
            need()
            for g2 in range(2):
                r = slice(HD * g2, HD * g2 + HD)
                mark(TT(bdg[r, 0, :, GP * g2:GP * g2 + GP], tb_[0][r], tb_[1][r], SU))
                ins = TT(bdg[r, 1, :, GP * g2:GP * g2 + GP], tb_[2][r], tb_[3][r], AD)
            ins.then_inc(bd_rdy, 1)
            for k, (raw_, dst) in enumerate(((kvraw, kn), (kiraw, k2))):
                freed(dve, Slot(N_KV, k))
                v.tensor_copy(dst[0:HD, :], raw_[0:HD, :])
                v.tensor_copy(dst[HD:P, :], raw_[0:HD, :]).then_inc(kdup, 1)
                split_lo(Slot(N_KV, k).next())
            for e in range(2):
                dve.wait_ge(s5_tr, 3 + e)
                for g2 in range(2):
                    src = PB[4 + e][0:HD, :].rearrange("n (s g q) -> n s g q", g=2, q=GP)[:, :, g2, :]
                    ins = TS(cTt[HD * g2:HD * g2 + HD, e, :, GP * g2:GP * g2 + GP], src, (1.0, -1.0)[e], None, MU)
            ins.then_inc(s5_cv, 1)

            m_s = mark(v.memset(score[:], 0.0))
            dve.wait_ge(kv_ev, 2)
            need(m_s)
            with dve.Fori(0, NPAIR) as i:
                q, z = Slot(N_IX, 0, 2, i), Slot(N_IX, 1, 2, i)
                split_lo(q.next())
                for hh in range(2):
                    for b in range(1, TB):
                        u = 3 * hh + b - 1
                        dve.wait_ge(relu_rdy, i * 6 + (u + 1 + 2))
                        wait(dve, r_used, i * 6 + u + 1)
                        sc = score[:, CB[b]:CB[b + 1]]
                        STT(sc, relu_b[u % 2][:, 0:P * (b + 1)], wtok[:, b, bass.ds(i * 2 + hh, 1)], sc, MU, AD
                            ).then_inc(r_used, 1)
                split_lo(z.next())
            dve.wait_ge(r_used, 6 * NPAIR + 3)
            for b in range(1, TB):
                mark(STT(score[:, CB[b + 1] - P:CB[b + 1]], diag, GONE, score[:, CB[b + 1] - P:CB[b + 1]], MU, AD))
            need()
            mark(v.tensor_copy(work[:, P:CB[4]], score[:, P:CB[4]]))

            def best8():
                need()
                settled(dve)
                for b in range(3):
                    mark(v.max(m8[:, b, :], work[:, CB[b + 1]:CB[b + 2]]))

            def take8(m):
                need(m)
                settled(dve)
                for b in range(3):
                    w = work[:, CB[b + 1]:CB[b + 2]]
                    mark(v.match_replace(w, m8[:, b, :], w, GONE))

            def gelu_low(j):
                dve.wait_ge(ya_h, j + 1)
                STT(dyn(yaL, j), yg[:], 1.0, dyn(yaH, j).bitcast(F32), MU, SU).then_inc(ya_done, 1)

            def s5(j, last):
                for c in range(4):
                    split_lo(Slot(N_S5 + 1, c, 6, j).next())
                    q = j * 4 + c
                    br, bi = (b[:] for b in (SB if c % 2 == 0 else TBANK))
                    co, si = ebuf[c % 2][:, 0, :], ebuf[c % 2][:, 1, :]
                    dve.wait_ge(bu_done, q + 1)
                    dve.wait_ge(e_full[c % 2], j * 32 + 16 * (c // 2 + 1))
                    dve.wait_ge(h_rdy, q + 1)
                    TT(t1[:], br, co, MU)
                    TT(t2[:], bi, si, MU)
                    TT(t3[:], bi, co, MU)
                    TT(t4[:], br, si, MU).then_inc(bu_free, 1)
                    best8()
                    m = st.k
                    if c == 0 and not (isinstance(j, int) and j == 0):
                        gelu_low(j - 1)
                    mg = par(1)[:, bass.ds(q, 1)] if not isinstance(q, int) else par(1)[:, q:q + 1]
                    dve.wait_ge(rot_rdy, q * 2 + 1)
                    settled(dve)
                    a = mark(v.tensor_tensor_scan(gr[:], mg.broadcast_to([P, S]), t1[:], 0.0, MU, AD))
                    dve.wait_ge(rot_rdy, q * 2 + 2)
                    settled(dve)
                    mark(v.tensor_tensor_scan(gi[:], mg.broadcast_to([P, S]), t3[:], 0.0, MU, AD))
                    need(a)
                    TT(t1[:], gr[:], co, MU)
                    need()
                    TT(t2[:], gi[:], si, MU)
                    TT(t3[:], gr[:], si, MU)
                    TT(t4[:], gi[:], co, MU).then_inc(e_used, 1)
                    if c == 3 and not last:
                        split_lo(Slot(N_S5 + 1, 4, 6, j).next())
                    take8(m)
                split_lo(Slot(N_S5 + 1, 4 if last else 5, 6, j).next())

            split_lo(Slot(N_S5).next())
            s5(0, False)
            with dve.Fori(1, KH - 1) as j:
                st.enter(j - 1, S5_STEPS)
                s5(j, False)
                st.leave(KH - 2)
            s5(KH - 1, True)
            gelu_low(KH - 1)
            need()
            mark(TT(work[:, P:CB[4]], work[:, P:CB[4]], score[:, P:CB[4]], ALU.is_lt))
            need()
            mark(TS(score[:, P:CB[4]], work[:, P:CB[4]], -1.0, -NEG, AD, MU))
            mark(TS(score[:, 0:P], diag, NEG, None, MU))
            need()

            masks = [score[:, CB[b]:CB[b + 1]] for b in range(TB)]
            split_lo(Slot(N_AT).next())
            score_max(NPAIR, masks)

            def att(i, last):
                normalise(i + NPAIR)
                s = Slot(N_AT + 1, 0, 2, i)
                used(s)
                mark(STT(dyn(sza, i), PB[1][:], col(vec, i + V_BGLU), dyn(sza, i), AD, MU))
                split_lo(s.next())
                need()
                dve.wait_ge(th_rdy, i + 1)
                STT(dyn(sza, i), thg[:], 1.0, dyn(sza, i), AD, MU).then_inc(gfree[1], 1)
                dve.wait_ge(y2h, i + 1)
                STT(dyn(y2L, i), dyn(sza, i), 0.5, dyn(y2H, i).bitcast(F32), MU, SU).then_inc(y2_done, 1)
                dve.wait_ge(pv, (i + NPAIR) * 2 + 2)
                TT(dyn(szb, i), OB[:], dyn(szb, i), MU).then_inc(o_free, 1)
                if not last:
                    score_max(i + (NPAIR + 1), masks)
                    split_lo(Slot(N_AT + 1, 1, 2, i).next())
                dve.wait_ge(o_free, i + (NPAIR + 1) + 1)
                dve.wait_ge(ybh, i + 1)
                STT(dyn(ybL, i), dyn(szb, i), 1.0, dyn(ybH, i).bitcast(F32), MU, SU).then_inc(yb_done, 1)
            with dve.Fori(0, NPAIR - 1) as i:
                st.enter(i, 3)
                att(i, False)
                st.leave(NPAIR - 1)
            att(NPAIR - 1, True)

            with dve.Fori(0, KD // 2) as i:
                st.enter(i, 3)
                for s, tg in enumerate((tga, tgb)):
                    sl = Slot(N_AB, s, 2, i)
                    used(sl)
                    t0 = mark(STT(dyn(tg, i * 2), dyn(tg, i * 2), 1.0, PB[s][:], AD, MU))
                    STT(dyn(tg, i * 2 + 1), dyn(tg, i * 2 + 1), 1.0, PB[s + 2][:], AD, MU).then_inc(gfree[s], 1)
                    split_lo(sl.next())
                need()
                freed(dve, sl)
                for e in range(2):
                    d = i * 2 + e
                    TT(dyn(tga, d), dyn(tga, d), dyn(tgb, d), AD).then_inc(mg_rdy, 1)
                for e in range(2):
                    d = i * 2 + e
                    dve.wait_ge(mgh, d + 1)
                    STT(dyn(hL, d), dyn(tga, d), 0.5, dyn(hH, d).bitcast(F32), MU, SU).then_inc(mg_done, 1)
                mark(v.memset(m8[:, 0, 0:1], 0.0))
                st.leave(KD // 2)

            mark(v.memset(gr[:], 0.0))
            need()

            def residual(i, j, last=False):
                sl, d, s = Slot(N_O2, j, 2, i), i * 2 + j, j % 2
                used(sl)
                STT(dyn(xT, d), PB[s][:], col(mod, d + 2 * KD), dyn(xT, d), MU, AD).then_inc(x3_rdy, 1)
                if not last:
                    dve.wait_ge(x3_rdy, d + 1)
                    v.memset(m8[:, 1, 0:1], 0.0).then_inc(gfree[s], 1)
                    split_lo(sl.next())

            def tokens(i):
                for s in range(2):
                    d = i * 2 + s
                    dve.wait_ge(xf_rdy, d + 1)
                    mark(TT(gr[:], gr[:], (t1, t2)[s][:], AD))
                    dve.wait_ge(xf_tr, d + 2)
                    v.tensor_copy(out_tok[:, :, bass.ds(d * P, P)], TBANK[s][:].rearrange("p (b n) -> p b n", b=TB)
                                  ).then_inc(ot_done, 1)
                    need()
            residual(0, 0)
            residual(0, 1)
            with dve.Fori(0, KD // 2 - 2) as i:
                st.enter(i, 2)
                residual(i, 2)
                tokens(i)
                residual(i, 3)
                st.leave(KD // 2 - 2)
            residual(KD // 2 - 1, 0, True)
            tokens(KD // 2 - 2)
            residual(KD // 2 - 1, 1, True)
            tokens(KD // 2 - 1)
            v.memset(m8[:, 0, 0:1], 0.0).then_inc(ssum, 1)
            dve.wait_ge(rr, 5)
            dve.wait_ge(ot_done, KD + 1)
            need(newton(sm[:, 16:20], PB[4][:, 0:4], 1.0 / D, sm[:, 12:16], sm[:, 8:12]))
            for t in range(TB):
                TS(out_tok[:, t, :], out_tok[:, t, :], sm[:, 16 + t:17 + t], None, MU).then_inc(fin, 1)


_INS = ["x", "g_mix", "w_in", "conv_w", "g_q", "g_k", "g_conv_out", "g_attn_out", "w_out", "g_ffn", "w_gate", "w_up",
        "w_down", "c_2", "norm_g_2", "w_mod_2", "b_mod_2", "w_in_2", "a_re_2", "a_im_2", "b_re_2", "b_im_2", "c_re_2",
        "c_im_2", "d_skip_2", "log_dt_2", "w_glu_2", "b_glu_2", "w_a_o_2", "w_b_o_2", "w_out_2", "final_g_2"]


def kernel(**inputs):
    import concourse.bacc as _bacc
    from concourse.bass_utils import run_bass_kernel_spmd as _run

    nc = _bacc.Bacc("TRN2", target_bir_lowering=False, num_devices=1)
    arrays, args = {}, []
    for name in _INS + ["constants"]:
        a = constants() if name == "constants" else np.ascontiguousarray(inputs[name])
        arrays[f"in_{name}_dram"] = a
        args.append(nc.dram_tensor(f"in_{name}_dram", a.shape, mybir.dt.from_np(a.dtype), kind="ExternalInput").ap())
    args.append(nc.dram_tensor("out_0_dram", (1, S, D), F32, kind="ExternalOutput").ap())
    program(nc, args)
    r = _run(nc, [arrays], core_ids=[0])
    return r.results[0]["out_0_dram"]
```

```python
import concourse.bass as bass
from concourse import mybir
from contextlib import ExitStack
import numpy as np

F32 = mybir.dt.float32
F32R = mybir.dt.float32r
I32 = mybir.dt.int32
ALU = mybir.AluOpType
ACT = mybir.ActivationFunctionType
AX = mybir.AxisListType

P = 128
S = 512
TB = S // P
D = 1024
KD = D // P
HALF = D // 2
KH = HALF // P
HD = 64
NPAIR = 4
FF = ((-(-8 * D // 3) + 255) // 256) * 256
KF = FF // P
EPS = 1e-6
NEG = -1e30
GONE = -3e38
TOPK = min(256, S // 4)
ROUNDS = TOPK // 8
IDX_SCALE = float((8 * 64) ** -0.5)
G2, NST, GP = 32, 64, 16
NCH = G2 * NST // P
LEVELS = 9
MIX_STEPS, S5_STEPS = 9, 32

Z_U, Z_GB, Z_GC, Z_Q, Z_K, Z_V = (j * HALF for j in range(6))
Y_XA, Y_ZA, Y_Q, Y_K, Y_ZB, Y_QI, Y_KI, Y_WI = 0, 512, 1024, 1536, 1664, 2176, 2688, 2752
Y_GA, Y_GB = 2760, 3784
NKI = Y_GA - Y_KI

N_MIX = 0
N_WO = N_MIX + 24
N_FF = N_WO + KD
N_DN = N_FF + 2 * KF
N_KV = N_DN + KF
N_IX = N_KV + 2
N_S5 = N_IX + 2 * NPAIR
N_AT = N_S5 + 24
N_AB = N_AT + 8
N_O2 = N_AB + 8
N_END = N_O2 + KD

MOD_AT = 8
GATE, ZA, XA = (0, 1, 3, 4), 2, 5

CB = [0, 128, 384, 768, 1280]
OFF = [0, 512, 896, 1152, 1280]

V_GMIX, V_CONV, V_GCONV, V_GATT, V_GFFN, V_C, V_NG, V_BMOD, V_BGLU, V_DSK, V_FG, V_GQ, V_GK = \
    0, 8, 20, 24, 28, 36, 44, 52, 76, 84, 88, 96, 97
NV1 = 98
W_ARE, W_AIM, W_LDT = 0, 16, 32
NV2 = 48

C_ID, C_DG, C_BD, C_M1, C_END = 0, 128, 256, 384, 896


def constants():
    i = np.arange(P)[:, None]
    d = i - np.arange(S)[None, :] + (S - P)
    c = ((d >= 0) & (d <= 128)) * 1 + ((d >= 0) & (d % 4 == 0)) + ((d >= 0) & (d % 16 == 0))
    m1 = np.where(c > 0, np.log(np.maximum(c, 1)), NEG)
    j = np.arange(P)[None, :]
    dg = np.where(j <= i, 0.0, 1.0)
    bd = (i // HD == j // HD) * 1.0
    return np.concatenate([np.eye(P), dg, bd, m1], 1).astype(np.float32)


def gfree_count(n):
    return n // 2 - (KF // 2 if n >= N_KV else 0)


class Steps:

    def __init__(self, eng, sem):
        self.eng, self.sem, self.base, self.k, self.i, self.per = eng, sem, 0, 0, None, 0

    def mark(self, ins):
        ins.then_inc(self.sem, 1)
        self.k += 1
        return self.k

    def need(self, k=None):
        k = self.k if k is None else k
        self.eng.wait_ge(self.sem, self.base + k if self.i is None else self.i * self.per + (self.base + k))

    def enter(self, i, per):
        self.base, self.k, self.i, self.per = self.base + self.k, 0, i, per

    def leave(self, times):
        assert self.k == self.per, ("steps in the loop's body", self.k)
        self.base, self.k, self.i = self.base + self.per * times, 0, None


def program(nc, io):
    (x, g_mix, w_in, conv_w, g_q, g_k, g_conv_out, g_attn_out, w_out, g_ffn, w_gate, w_up, w_down,
     c_2, norm_g_2, w_mod_2, b_mod_2, w_in_2, a_re_2, a_im_2, b_re_2, b_im_2, c_re_2, c_im_2,
     d_skip_2, log_dt_2, w_glu_2, b_glu_2, w_a_o_2, w_b_o_2, w_out_2, final_g_2, consts) = io[:-1]
    out = io[-1]
    e_dram = nc.dram_tensor("rotations", [NCH, P, 2, S], F32, kind="Internal").ap()

    with ExitStack() as ctx:
        base = (nc.sbuf_base + 63) // 64 * 64
        top = [base]

        def at(name, shape, dt=F32, off=None):
            size = 4 * int(np.prod(shape[1:]))
            if off is None:
                off = top[0]
                top[0] += (size + 31) // 32 * 32
            return nc.alloc_sbuf_tensor_at(name, shape, dt, offset=off)

        def sem(name):
            return ctx.enter_context(nc.semaphore(name))

        PB = [ctx.enter_context(nc.psum_tensor(f"bank{b}", [P, S], F32)) for b in range(8)]
        SB, TBANK, OB = (PB[4], PB[5], PB[6], PB[2]), (PB[6], PB[2], PB[4], PB[5]), PB[7]
        AB = ((PB[0], PB[3]), (PB[1], PB[2]))

        xT = at("xT", [P, KD, S])
        hH, hL = at("hH", [P, KD, S], F32R), at("hL", [P, KD, S], F32R)
        raw = [at(f"raw{s}", [P, 1024]) for s in range(2)]
        wH = [at(f"wH{s}", [P, 1024], F32R) for s in range(2)]
        wL = [at(f"wL{s}", [P, 1024], F32R) for s in range(2)]
        cst = at("cst", [P, C_M1])
        vec, svec = at("vec", [P, NV1]), at("svec", [P, NV2])
        ones = at("ones", [P, P])
        epst = at("epst", [P, 1])
        csil, mod, gs = at("csil", [P, KD]), at("mod", [P, 3 * KD]), at("gs", [P, KD])
        mx, nmx, rs, rinv = (at(n, [P, 8]) for n in ("mx", "nmx", "rs", "rinv"))
        sm = at("sm", [P, 24])
        sp = at("sp", [P, 20, NCH])
        spi = at("spi", [P, NCH], I32)
        hbg, ldt = at("hbg", [P, KH]), at("ldt", [P, 2])
        m8 = at("m8", [P, 3, 8])
        ident, diag, bdones = cst[:, C_ID:C_DG], cst[:, C_DG:C_BD], cst[:, C_BD:C_M1]
        A0 = top[0]
        aH, aL = at("aH", [P, KF, S], F32R, A0), at("aL", [P, KF, S], F32R, A0 + 4 * KF * S)
        x_tok = at("x_tok", [P, TB, D], F32, A0)
        row1, row2 = at("row1", [P, P], F32, A0 + 32768), at("row2", [P, P], F32, A0 + 33280)
        names = ["qraw", "kraw", "vT", "u_s", "sqq", "sqk", "rq", "rk", "cv", "yc", "sqc", "yo", "sqa"]
        (qraw, kraw, vT, u_s, sqq, sqk, rq, rk, cv, yc, sqc, yo, sqa) = (
            at(n, [P, S], F32, A0 + 2048 * j) for j, n in enumerate(names))
        cuP = at("cuP", [P, S + 2], F32, A0 + 2048 * 13)
        mixH, mixL = at("mixH", [P, KD, S], F32R, A0 + 32768), at("mixL", [P, KD, S], F32R, A0 + 49152)
        macc = at("macc", [P, 3 * D], F32, A0 + 65536)
        mraw = [at(f"mraw{s}", [P, D], F32, A0 + 77824 + 4096 * s) for s in range(2)]
        ssc, ssa = at("ssc", [P, S], F32, A0 + 86016), at("ssa", [P, S], F32, A0 + 88064)
        rc, ra = at("rc", [P, S], F32, A0), at("ra", [P, S], F32, A0 + 2048)
        nt1, nt2 = at("nt1", [P, S], F32, A0 + 4096), at("nt2", [P, S], F32, A0 + 6144)
        wo1, wo2 = at("wo1", [P, S], F32, A0 + 8192), at("wo2", [P, S], F32, A0 + 10240)
        tga, tgb = at("tga", [P, KD, S], F32, A0), at("tgb", [P, KD, S], F32, A0 + 16384)
        szb, sza = at("szb", [P, KH, S], F32, A0 + 32768), at("sza", [P, KH, S], F32, A0 + 40960)
        ebuf = [at(f"ebuf{s}", [P, 2, S], F32, A0 + 49152 + 4096 * s) for s in range(2)]
        S0 = A0 + 57344
        braw = at("braw", [P, 2, NCH, GP], F32, S0)
        bdg = at("bdg", [P, 2, NCH, 2 * GP], F32, S0 + 2048)
        bbT = at("bbT", [P, 2, KH, P], F32, S0 + 6144)
        craw = at("craw", [P, 2, KH, NST], F32, S0 + 10240)
        cTt = at("cTt", [P, 2, NCH, 2 * GP], F32, S0 + 12288)
        yaH, yaL = at("yaH", [P, KH, S], F32R, A0 + 73728), at("yaL", [P, KH, S], F32R, A0 + 81920)
        y2H, y2L = at("y2H", [P, KH, S], F32R, A0 + 49152), at("y2L", [P, KH, S], F32R, A0 + 57344)
        ybH = at("ybH", [P, KH, S], F32R, A0 + 65536)
        out_tok = at("out_tok", [P, TB, D], F32, A0)
        B0 = A0 + 90112
        L = at("L", [P, 2, CB[4]], F32, B0)
        pT = at("pT", [P, 2, CB[4]], F32, B0 + 10240)
        qn, kn = at("qn", [P, S], F32, B0 + 20480), at("kn", [P, S], F32, B0 + 22528)
        vtok = at("vtok", [P, TB, P], F32, B0 + 24576)
        score, work = at("score", [P, CB[4]], F32, B0 + 26624), at("work", [P, CB[4]], F32, B0 + 31744)
        relu_b = [at(f"relu{s}", [P, S], F32, B0 + 36864 + 2048 * s) for s in range(2)]
        ybL = at("ybL", [P, KH, S], F32R, B0 + 31744)
        r1, gt, ut, sg, a32, sqx = (at(n, [P, S], F32, B0 + 26624 + 2048 * j) for j, n in
                                    enumerate(("r1", "gt", "ut", "sg", "a32", "sqx")))
        ss1 = at("ss1", [P, S], F32, B0 + 38912)
        q1 = [at(f"q1{e}", [P, S], F32R, B0 + 26624 + 2048 * e) for e in range(2)]
        k1 = [at(f"k1{e}", [P, S], F32R, B0 + 30720 + 2048 * e) for e in range(2)]
        k1L = at("k1L", [P, S], F32R, B0 + 34816)
        qx = [at("qx0", [P, S], F32R, B0 + 20480), at("qx1", [P, S], F32R, B0 + 12288)]
        kx, kxL = at("kx", [P, S], F32R, B0 + 14336), at("kxL", [P, S], F32R, B0 + 16384)
        eb = at("eb", [P, 2, 2, S], F32, B0)
        et = [at(f"et{j}", [P, 2, S // 2], F32, B0 + 8192 + 2048 * j) for j in range(4)]
        bbS, dgS = at("bbS", [P, 2, P], F32, B0 + 24576), at("dgS", [P, P], F32, B0 + 25600)
        cpS = at("cpS", [P, 4, 2, P], F32, B0 + 36864)
        thg = at("thg", [P, S], F32, B0 + 24576)
        yg = at("yg", [P, S], F32, B0 + 40960)
        t1, t2, t3, t4, gr, gi, hr0, hr1, hi0, hi1 = (
            at(n, [P, S], F32, B0 + 2048 * j) for j, n in
            enumerate(("t1", "t2", "t3", "t4", "gr", "gi", "hr0", "hr1", "hi0", "hi1")))
        kvraw, kiraw = at("kvraw", [P, S], F32, B0), at("kiraw", [P, S], F32, B0 + 2048)
        xaS = at("xaS", [P, S], F32, B0 + 20480)
        mask1 = at("mask1", [P, S], F32, B0 + 40960)
        pw = at("pw", [P, 2, LEVELS, NCH], F32, B0 + 43008)
        vt2 = at("vt2", [P, TB, HD], F32, B0 + 43008)
        wtok = at("wtok", [P, TB, 8], F32, B0 + 44032)
        assert B0 + 44160 <= nc.sbuf_usable_end

        x_in = [sem(f"x_in{t}") for t in range(TB)]
        cst_in, mask_in, glu_full, vec_in, vecp_in, svec_in, s5_in, out_done = (
            sem(n) for n in ("cst_in", "mask_in", "glu_full", "vec_in", "vecp_in", "svec_in", "s5_in", "out_done"))
        w_full = [sem(f"w_full{s}") for s in range(2)]
        hi_done, lo_done = sem("hi_done"), sem("lo_done")
        slot_used = sem("slot_used")
        gfree = [sem(f"gfree{s}") for s in range(2)]
        m_full = [sem(f"m_full{s}") for s in range(2)]
        m_used = sem("m_used")
        vstep, astep, pstep = sem("vstep"), sem("astep"), sem("pstep")
        pe_pre, vec_cp, init_v, init_p = (sem(n) for n in ("pe_pre", "vec_cp", "init_v", "init_p"))
        r0d, xt_mm, xt_done, sq0_rdy, sq0_used, h1f, h1h, h1_done, vec_rdy, s5_cv = (
            sem(n) for n in ("r0d", "xt_mm", "xt_done", "sq0_rdy", "sq0_used", "h1f", "h1h", "h1_done", "vec_rdy",
                             "s5_cv"))
        ss_mm, ss_rd, rs_rdy, qn_rdy = (sem(n) for n in ("ss_mm", "ss_rd", "rs_rdy", "qn_rdy"))
        q_hi, q_lo, qx_hi, kx_hi = (sem(n) for n in ("q_hi", "q_lo", "qx_hi", "kx_hi"))
        vtr, vt_done, ych = sem("vtr"), sem("vt_done"), sem("ych")
        sc_ready, sc_free, nm, ex, pn = (sem(n) for n in ("sc_ready", "sc_free", "nm", "ex", "pn"))
        tr_mm, t_free, pv, o_free, yo_rdy = (sem(n) for n in ("tr_mm", "t_free", "pv", "o_free", "yo_rdy"))
        ssum, ssm, rr, nt_done = (sem(n) for n in ("ssum", "ssm", "rr", "nt_done"))
        x1_rdy, x1h, x1l = sem("x1_rdy"), sem("x1h"), sem("x1l")
        sg_rdy, a32_rdy, ah_rdy, a_done, dn_done = (sem(n) for n in ("sg_rdy", "a32_rdy", "ah_rdy", "a_done", "dn_done"))
        mod_mm, pw_rdy, e_out = sem("mod_mm"), sem("pw_rdy"), sem("e_out")
        mod_cp = sem("mod_cp")
        cv_split = sem("cv_split")
        sq2_rdy, sq2_used, h2f, h2h, h2_done = (sem(n) for n in ("sq2_rdy", "sq2_used", "h2f", "h2h", "h2_done"))
        trig_a, trig_r = sem("trig_a"), sem("trig_r")
        kdup, bd_rdy, s5_tr, s5_ev, bb_rdy, rot_rdy = (
            sem(n) for n in ("kdup", "bd_rdy", "s5_tr", "s5_ev", "bb_rdy", "rot_rdy"))
        kv_tr, kv_ev, ix_ready, relu_rdy, r_used = (sem(n) for n in ("kv_tr", "kv_ev", "ix_ready", "relu_rdy", "r_used"))
        xa_rdy, bu_done, bu_free, h_rdy, y_mm, y_free, yg_rdy, ya_h, ya_done = (
            sem(n) for n in ("xa_rdy", "bu_done", "bu_free", "h_rdy", "y_mm", "y_free", "yg_rdy", "ya_h", "ya_done"))
        e_full = [sem(f"e_full{s}") for s in range(2)]
        e_used = sem("e_used")
        th_rdy, y2h, y2_done, ybh, yb_done = (
            sem(n) for n in ("th_rdy", "y2h", "y2_done", "ybh", "yb_done"))
        mg_rdy, mgh, mg_done = sem("mg_rdy"), sem("mgh"), sem("mg_done")
        x3_rdy, xf_rdy, xf_tr, ot_done, r_fin = (sem(n) for n in ("x3_rdy", "xf_rdy", "xf_tr", "ot_done", "r_fin"))
        fin = [sem(f"fin{t}") for t in range(TB)]

        def wait(eng, s, v):
            if not (isinstance(v, int) and v <= 0):
                eng.wait_ge(s, v)

        class Slot:

            def __init__(self, first, j=0, per=0, i=0):
                c = first + j
                self.par = c % 2
                self.n = c + per * i if isinstance(i, int) else i * per + c
                self.half = c // 2 + per // 2 * i if isinstance(i, int) else i * (per // 2) + c // 2
                self.gf = self.half - (KF // 2 if c >= N_KV else 0)

            def next(self, k=2):
                s = Slot(0)
                s.par, s.n, s.half, s.gf = self.par, self.n + k, self.half + k // 2, self.gf + k // 2
                return s

        def settled(eng):
            eng.nop(nofuse=True)

        def freed(eng, s):
            eng.wait_ge(gfree[s.par], s.gf + 1)

        def blk(t, k):
            return t[:, k * P:(k + 1) * P]

        block = ctx.enter_context(nc.Block())

        @block.sync
        def _(sp_):
            sp_.dma_start(cst[:], consts[:, 0:C_M1]).then_inc(cst_in, 16)
            for t in range(TB):
                sp_.dma_start(x_tok[:, t, :], x[0, t * P:(t + 1) * P, :]).then_inc(x_in[t], 16)

            def cols(w, c, n=P):
                return w[0].rearrange("(k p) c -> p k c", p=P)[:, :, bass.ds(c, n)]

            def load(s, src, width=P, shape=KD):
                wait(sp_, lo_done, s.n - 1)
                dst = raw[s.par][:].rearrange("p (k c) -> p k c", k=shape)[:, :, 0:width]
                sp_.dma_start(dst, src).then_inc(w_full[s.par], 16)

            for j, z in enumerate((Z_Q, Z_K, Z_V)):
                load(Slot(N_MIX, j), cols(w_in, z))

            def mix(i, last):
                for j, z in enumerate((Z_U, Z_GC, Z_GB)):
                    load(Slot(3, j, 6, i), cols(w_in, i * P + z))
                if not last:
                    for j, z in enumerate((Z_Q, Z_K, Z_V)):
                        load(Slot(3, 3 + j, 6, i), cols(w_in, i * P + (z + P)))
            with sp_.Fori(0, NPAIR - 1) as i:
                mix(i, False)
            mix(NPAIR - 1, True)
            with sp_.Fori(0, KD // 2) as i:
                for s in range(2):
                    load(Slot(N_WO, s, 2, i), cols(w_out, i * (2 * P) + s * P))
            with sp_.Fori(0, KF) as i:
                load(Slot(N_FF, 0, 2, i), cols(w_gate, i * P))
                load(Slot(N_FF, 1, 2, i), cols(w_up, i * P))
            with sp_.Fori(0, KF // 2) as i:
                for s in range(2):
                    load(Slot(N_DN, s, 2, i), w_down[0][bass.ds(i * (2 * P) + s * P, P), :]
                         .rearrange("p (k c) -> p k c", k=KD))
            load(Slot(N_KV, 0), cols(w_in_2, Y_K))
            load(Slot(N_KV, 1), cols(w_in_2, Y_KI, NKI), NKI)
            with sp_.Fori(0, NPAIR) as i:
                load(Slot(N_IX, 0, 2, i), cols(w_in_2, i * P + Y_QI))
                load(Slot(N_IX, 1, 2, i), cols(w_in_2, i * P + Y_ZB))
            load(Slot(N_S5), cols(w_in_2, Y_XA))

            def s5(j, last):
                for c in range(4):
                    if c == 2:
                        load(Slot(N_S5 + 1, ZA, 6, j), cols(w_in_2, j * P + Y_ZA))
                    y = (Y_GA, Y_GB)[c % 2] + c // 2 * P
                    load(Slot(N_S5 + 1, GATE[c], 6, j), cols(w_in_2, j * (2 * P) + y))
                if not last:
                    load(Slot(N_S5 + 1, XA, 6, j), cols(w_in_2, j * P + (Y_XA + P)))
            with sp_.Fori(0, KH - 1) as j:
                s5(j, False)
            s5(KH - 1, True)
            load(Slot(N_AT), cols(w_in_2, Y_Q))

            def at_(i, last):
                s = Slot(N_AT + 1, 0, 2, i)
                wait(sp_, lo_done, s.n - 1)
                for e in range(2):
                    dst = raw[s.par][:].rearrange("p (k e c) -> p k e c", k=KH, e=2)[:, :, e, :]
                    src = w_glu_2[0].rearrange("(k p) c -> p k c", p=P)[:, :, bass.ds(i * P + e * HALF, P)]
                    sp_.dma_start(dst, src).then_inc(glu_full if e else w_full[s.par], 16)
                if not last:
                    load(Slot(N_AT + 1, 1, 2, i), cols(w_in_2, i * P + (Y_Q + P)))
            with sp_.Fori(0, NPAIR - 1) as i:
                at_(i, False)
            at_(NPAIR - 1, True)
            with sp_.Fori(0, KD // 2) as i:
                load(Slot(N_AB, 0, 2, i), cols(w_a_o_2, i * (2 * P), 2 * P), 2 * P, KH)
                load(Slot(N_AB, 1, 2, i), cols(w_b_o_2, i * (2 * P), 2 * P), 2 * P, KH)
            with sp_.Fori(0, KD // 2) as i:
                for s in range(2):
                    load(Slot(N_O2, s, 2, i), cols(w_out_2, i * (2 * P) + s * P))
            for t in range(TB):
                sp_.wait_ge(fin[t], 1)
                sp_.dma_start(out[0, t * P:(t + 1) * P, :], out_tok[:, t, :]).then_inc(out_done, 16)
            sp_.wait_ge(out_done, 16 * TB)

        @block.gpsimd
        def _(pool):
            g = nc.gpsimd
            pool.dma_start(row1[V_CONV:V_CONV + 12, :],
                           conv_w.rearrange("a w (n p) -> (a w n) p", p=P)).then_inc(vecp_in, 16)
            pool.dma_start(row1[V_FG:V_FG + 8, :], final_g_2.rearrange("(n p) -> n p", p=P)).then_inc(vecp_in, 16)
            for r, v in ((V_GQ, g_q), (V_GK, g_k)):
                for e in range(2):
                    pool.dma_start(row1[r:r + 1, e * HD:(e + 1) * HD], v).then_inc(vecp_in, 16)
            pool.dma_start(mask1[:], consts[:, C_M1:C_END]).then_inc(mask_in, 16)
            g.memset(macc[:], 0.0)
            g.memset(ssc[:], 0.0)
            g.memset(ssa[:], 0.0).then_inc(init_p, 1)

            with pool.Fori(0, NPAIR) as i:
                for m in range(6):
                    pool.wait_ge(m_used, i * 6 + (m + 2))
                    pool.dma_start(mraw[m % 2][:], w_mod_2[0][bass.ds(i * (2 * P) + (m // 3) * P, P),
                                                             (m % 3) * D:(m % 3 + 1) * D]).then_inc(m_full[m % 2], 16)

            pool.wait_ge(pw_rdy, 1)
            pool.wait_ge(pv, 2 * NPAIR)
            st = Steps(pool, pstep)
            with pool.Fori(0, NCH // 2) as i:
                st.enter(i, 1 + 6 * LEVELS)
                g.memset(eb[:, :, 0, 0:1], 1.0)
                st.mark(g.memset(eb[:, :, 1, 0:1], 0.0))
                for k in range(LEVELS):
                    n = 1 << k
                    st.need()
                    c, s = eb[:, :, 0, 0:n], eb[:, :, 1, 0:n]
                    wc, ws = (pw[:, e, k, bass.ds(i * 2, 2)].unsqueeze(2).broadcast_to([P, 2, n]) for e in range(2))
                    m = [t[:, :, 0:n] for t in et]
                    st.mark(g.tensor_tensor(m[0], c, wc, ALU.mult))
                    st.mark(g.tensor_tensor(m[1], s, ws, ALU.mult))
                    st.mark(g.tensor_tensor(m[2], c, ws, ALU.mult))
                    last = st.mark(g.tensor_tensor(m[3], s, wc, ALU.mult))
                    st.need(last - 2)
                    st.mark(g.tensor_tensor(eb[:, :, 0, n:2 * n], m[0], m[1], ALU.subtract))
                    st.need(last)
                    st.mark(g.tensor_tensor(eb[:, :, 1, n:2 * n], m[2], m[3], ALU.add))
                st.need()
                for c in range(2):
                    pool.dma_start(e_dram[bass.ds(i * 2 + c, 1)].rearrange("a p e t -> (a p) e t"),
                                   eb[:, c]).then_inc(e_out, 16)
                pool.wait_ge(e_out, i * 32 + 32)
                st.leave(NCH // 2)

            pool.wait_ge(slot_used, N_DN + KF)
            for e, (b, c) in enumerate(((b_re_2, c_re_2), (b_im_2, c_im_2))):
                pool.dma_start(braw[:, e], b[0].rearrange("(s g) n p -> (g n) s p", g=2)).then_inc(s5_in, 16)
                pool.dma_start(craw[:, e], c[0].rearrange("(k g) p n -> (g p) k n", g=8)).then_inc(s5_in, 16)
            pool.wait_ge(s5_ev, 2)
            pool.wait_ge(s5_cv, 1)
            pool.wait_ge(r_used, 6 * NPAIR + 3)
            st.mark(g.memset(cpS[:], 0.0))
            st.need()

            def input_matrix(j):
                g.tensor_copy(bbS[:], dynj(bbT, j)).then_inc(bb_rdy, 1)

            def dynj(t, j):
                return t[:, :, j, :] if isinstance(j, int) else t[:, :, bass.ds(j, 1), :].rearrange("p e j n -> p e (j n)")

            def rotations(c, i):
                pool.wait_ge(e_used, i * 4 + (c + 1))
                src = e_dram[bass.ds(i * 4 + c, 1)] if not isinstance(i, int) else e_dram[i * 4 + c:i * 4 + c + 1]
                pool.dma_start(ebuf[c % 2][:], src.rearrange("a p e t -> (a p) e t")).then_inc(e_full[c % 2], 16)

            def s5(j, last):
                for c in range(4):
                    q = j * 4 + c
                    if not (last and c == 3):
                        rotations(c + 1, j)
                    pool.wait_ge(bu_free, q + 3)
                    g.tensor_tensor(t1[:], t1[:], t2[:], ALU.add).then_inc(rot_rdy, 1)
                    g.tensor_tensor(t3[:], t3[:], t4[:], ALU.subtract).then_inc(rot_rdy, 1)
                    if c == 3 and not last:
                        pool.wait_ge(bu_done, q + 1)
                        input_matrix(j + 1)
                    pool.wait_ge(y_mm, q + 1)
                    if c == 0:
                        dsk = vec[:, j + V_DSK:j + V_DSK + 1] if isinstance(j, int) else vec[:, bass.ds(j + V_DSK, 1)]
                        g.tensor_tensor(dgS[:], ident, dsk.broadcast_to([P, P]), ALU.mult)
                    g.tensor_copy(cpS[:, c, :, 32 * c:32 * c + 32], dynj(cTt, q))
                    pool.wait_ge(e_used, q + 3)
                    g.tensor_tensor((hr0, hr1)[c % 2][:], t1[:], t2[:], ALU.subtract)
                    g.tensor_tensor((hi0, hi1)[c % 2][:], t3[:], t4[:], ALU.add).then_inc(h_rdy, 1)
            input_matrix(0)
            rotations(0, 0)
            with pool.Fori(0, KH - 1) as j:
                s5(j, False)
            s5(KH - 1, True)

        @block.tensor
        def _(pe):
            mm = nc.tensor.matmul

            def transposes(dst, srcs, idn=ident):
                for t, src in enumerate(srcs):
                    m, kk = src.shape[1], src.shape[0]
                    ins = nc.tensor.transpose(dst[0:m, t * P:t * P + kk], src, idn[0:kk, 0:kk])
                return ins

            def products(s, terms):
                pe.wait_ge(lo_done, s.n + 1)
                for k, rh, rl, o, a, z in terms:
                    mm(o, blk(wH[s.par], k), rh, start=a, stop=False)
                    mm(o, blk(wH[s.par], k), rl, start=False, stop=False)
                    ins = mm(o, blk(wL[s.par], k), rh, start=False, stop=z)
                if z:
                    ins.then_inc(slot_used, 1)

            def project(s, m=P, each=None):
                wait(pe, gfree[s.par], s.gf)
                pe.wait_ge(lo_done, s.n + 1)
                o = PB[s.par][0:m, :]
                for k in range(KD):
                    a, b = wH[s.par][:, k * P:k * P + m], wL[s.par][:, k * P:k * P + m]
                    if each is not None:
                        pe.wait_ge(each, k + 1)
                    mm(o, a, hH[:, k, :], start=(k == 0), stop=False)
                    mm(o, a, hL[:, k, :], start=False, stop=False)
                    ins = mm(o, b, hH[:, k, :], start=False, stop=(k == KD - 1))
                ins.then_inc(slot_used, 1)

            def scores(a, q, k):
                for hh in range(2):
                    r = slice(HD * hh, HD * hh + HD)
                    for b in range(TB):
                        u = 4 * hh + b
                        pe.wait_ge(sc_free, a * 8 + (u + 1))
                        mm(SB[b][:, 0:P * (b + 1)], q[r, blkc(b)], k[r, 0:P * (b + 1)],
                           start=True, stop=True).then_inc(sc_ready, 1)

            def split_score(o, hh, b, q, k, kl):
                r, n = slice(HD * hh, HD * hh + HD), P * (b + 1)
                mm(o[:, 0:n], q[:, blkc(b)], k[:, 0:n], start=True, stop=False)
                return mm(o[:, 0:n], q[r, blkc(b)], kl[r, 0:n], start=False, stop=True)

            def split_scores(a):
                for hh in range(2):
                    for b in range(TB):
                        pe.wait_ge(sc_free, a * 8 + (4 * hh + b + 1))
                        split_score(SB[b], hh, b, q1[hh], k1[hh], k1L).then_inc(sc_ready, 1)

            def blkc(b):
                return slice(b * P, (b + 1) * P)

            def attend(a, v, vcol):
                for hh in range(2):
                    pe.wait_ge(pn, a * 2 + (hh + 1))
                    for kb in range(TB):
                        pe.wait_ge(t_free, a * 8 + (4 * hh + kb + 1))
                        transposes(TBANK[kb], [L[:, hh, CB[b] + P * kb:CB[b] + P * kb + P] for b in range(kb, TB)]
                                   ).then_inc(tr_mm, 1)
                wait(pe, o_free, a + 1)
                for hh in range(2):
                    r = slice(HD * hh, HD * hh + HD)
                    pe.wait_ge(t_free, a * 8 + (4 * hh + 4 + 4))
                    for kb in range(TB):
                        ins = mm(OB[r, P * kb:S], v[:, kb, vcol(hh)], pT[:, hh, OFF[kb]:OFF[kb + 1]],
                                 start=(kb == 0), stop=(kb == TB - 1), skip_group_check=True)
                    ins.then_inc(pv, 1)

            for s in (y_mm, y_mm, ix_ready, xf_tr):
                pe.nop().then_inc(s, 1)
            pe.wait_ge(cst_in, 16)
            pe.wait_ge(svec_in, 16 * 3)
            pe.wait_ge(r0d, 1)
            nc.tensor.transpose(PB[7][:, 0:NV2], row2[0:NV2, :], ident[0:NV2, 0:NV2]).then_inc(pe_pre, 1)
            for t in range(TB):
                pe.wait_ge(x_in[t], 16)
                for k in range(KD):
                    if t == 0 and k == KD - 1:
                        pe.wait_ge(vec_cp, 1)
                    ins = transposes(PB[k][:, t * P:(t + 1) * P], [x_tok[:, t, k * P:(k + 1) * P]])
                    if t == TB - 1:
                        ins.then_inc(xt_mm, 1)
            for k in range(KD):
                pe.wait_ge(sq0_rdy, k + 1)
                mm(PB[0][:], ones[:], (sqx, a32)[k % 2][:], start=(k == 0), stop=(k == KD - 1),
                   skip_group_check=True).then_inc(sq0_used, 1)
                if k == 1:
                    pe.wait_ge(vec_in, 16 * 9)
                    pe.wait_ge(vecp_in, 16 * 6)
                    nc.tensor.transpose(PB[1][:, 0:NV1], row1[0:NV1, :], ident[0:NV1, 0:NV1]).then_inc(pe_pre, 1)

            def qkv(first, i):
                for j in range(3):
                    project(Slot(first, j, 6, i))

            def head_sums(a, ks):
                freed(pe, ks)
                pe.wait_ge(sc_free, a * 8 + 4)
                for e, sq in enumerate((sqq, sqk)):
                    mm(SB[e][:], bdones, sq[:], start=True, stop=True).then_inc(ss_mm, 1)

            def mix(i, last):
                for j in range(3):
                    project(Slot(3, j, 6, i))
                freed(pe, Slot(2, 0, 6, i))
                transposes(PB[3], [vT[:, blkc(b)] for b in range(TB)]).then_inc(vtr, 1)
                pe.wait_ge(ss_rd, i * 2 + 2)
                pe.wait_ge(q_lo, i + 1)
                split_scores(i)
                if not last:
                    qkv(6, i)
                if last:
                    for s in range(2):
                        pe.wait_ge(gfree[s], Slot(N_WO, s).gf)
                        out_half(Slot(N_WO, s), 0)
                pe.wait_ge(vt_done, i + 1)
                attend(i, vtok, lambda hh: slice(HD * hh, HD * hh + HD))
                if not last:
                    head_sums(i + 1, Slot(7, 0, 6, i))

            def out_half(sl, half, k0=0, k1=KH):
                pe.wait_ge(lo_done, sl.n + 1)
                o = PB[sl.par + 2 * half]
                for k in range(k0, k1):
                    a, z, f = k == 0, k == KH - 1, k + half * KH
                    if z and not half:
                        pe.wait_ge(cv_split, 1)
                    mm(o[:], blk(wH[sl.par], f), mixH[:, f, :], start=a, stop=False)
                    mm(o[:], blk(wH[sl.par], f), mixL[:, f, :], start=False, stop=False)
                    ins = mm(o[:], blk(wL[sl.par], f), mixH[:, f, :], start=False, stop=z)
                if half and z:
                    ins.then_inc(slot_used, 1)

            project(Slot(0), each=h1_done)
            project(Slot(1))
            project(Slot(2))
            freed(pe, Slot(0, 2))
            head_sums(0, Slot(1))
            with pe.Fori(0, NPAIR - 1) as i:
                mix(i, False)
            mix(NPAIR - 1, True)

            for s in range(2):
                out_half(Slot(N_WO, s), 1, 0, KH - 1)
            pe.wait_ge(ssum, 1)
            mm(PB[4][:], ones[:], ssc[:], start=True, stop=True).then_inc(ssm, 1)
            mm(PB[5][:], ones[:], ssa[:], start=True, stop=True).then_inc(ssm, 1)
            for s in range(2):
                out_half(Slot(N_WO, s), 1, KH - 1)
            with pe.Fori(1, KD // 2) as i:
                for s in range(2):
                    sl = Slot(N_WO, s, 2, i)
                    pe.wait_ge(gfree[s], sl.gf)
                    out_half(sl, 0)
                    out_half(sl, 1)

            project(Slot(N_FF), each=x1l)
            pe.wait_ge(ssum, 2)
            mm(PB[4][:], ones[:], ss1[:], start=True, stop=True).then_inc(ssm, 1)
            project(Slot(N_FF, 1))
            with pe.Fori(1, MOD_AT) as i:
                for s in range(2):
                    project(Slot(N_FF, s, 2, i))
            pe.wait_ge(m_used, 6 * NPAIR + 3)
            for c in range(3 * KD):
                ins = mm(PB[6][:, c:c + 1], macc[:, blkc(c)], ones[:, 0:1], start=True, stop=True)
            ins.then_inc(mod_mm, 1)
            with pe.Fori(MOD_AT, KF) as i:
                for s in range(2):
                    project(Slot(N_FF, s, 2, i))

            def down(i, first, last):
                for s in range(2):
                    sl = Slot(N_DN, s, 2, i)
                    pe.wait_ge(lo_done, sl.n + 1)
                    kf = i * 2 + s
                    rh, rl = (t[:, bass.ds(kf, 1), :].rearrange("p k t -> p (k t)") if not isinstance(i, int)
                              else t[:, kf, :] for t in (aH, aL))
                    if first:
                        pe.wait_ge(a_done, kf + 1)
                    for d in (range(KD) if not first or s else (2, 3, 4, 5, 6, 7, 0, 1)):
                        a, z = first and s == 0, last and s == 1
                        if a and d == 0:
                            pe.wait_ge(a_done, KF)
                        if a and d == 6:
                            pe.wait_ge(mod_cp, 1)
                        mm(PB[d][:], blk(wH[s], d), rh, start=a, stop=False, skip_group_check=True)
                        mm(PB[d][:], blk(wH[s], d), rl, start=False, stop=False, skip_group_check=True)
                        ins = mm(PB[d][:], blk(wL[s], d), rh, start=False, stop=z, skip_group_check=True)
                        if z and d < KD - 1:
                            ins.then_inc(dn_done, 1)
                    ins.then_inc(slot_used, 1)
            down(0, True, False)
            with pe.Fori(1, KF // 2 - 1) as i:
                down(i, False, False)
            down(KF // 2 - 1, False, True)

            for d in range(KD):
                pe.wait_ge(sq2_rdy, d + 1)
                mm(PB[0][:], ones[:], (sqx, a32)[d % 2][:], start=(d == 0), stop=(d == KD - 1),
                   skip_group_check=True).then_inc(sq2_used, 1)
            pe.wait_ge(s5_in, 64)
            for e in range(2):
                transposes(PB[4 + e], [craw[:, e, k, :] for k in range(KH)]).then_inc(s5_tr, 1)
            project(Slot(N_KV, 0), each=h2_done)
            project(Slot(N_KV, 1), NKI)
            pe.wait_ge(bd_rdy, 1)
            for e in range(2):
                transposes(PB[6 + e], [bdg[:, e, 4 * j:4 * j + 4, :].rearrange("p s q -> p (s q)") for j in range(KH)]
                           ).then_inc(s5_tr, 1)
            freed(pe, Slot(N_KV, 0))
            transposes(PB[3], [kvraw[:, blkc(b)] for b in range(TB)]).then_inc(kv_tr, 1)
            freed(pe, Slot(N_KV, 1))
            transposes(PB[2], [kiraw[0:NKI, blkc(b)] for b in range(TB)]).then_inc(kv_tr, 1)

            with pe.Fori(0, NPAIR) as i:
                project(Slot(N_IX, 0, 2, i))
                project(Slot(N_IX, 1, 2, i))
                freed(pe, Slot(N_IX, 0, 2, i))
                pe.wait_ge(s5_cv, 1)
                pe.wait_ge(kdup, 2)
                for hh in range(2):
                    r = slice(HD * hh, HD * hh + HD)
                    for b in range(1, TB):
                        u = 3 * hh + b - 1
                        pe.wait_ge(relu_rdy, i * 6 + (u + 1))
                        split_score(SB[u % 2], hh, b, qx[hh], kx, kxL).then_inc(ix_ready, 1)

            project(Slot(N_S5))
            freed(pe, Slot(N_S5))
            pe.wait_ge(kv_ev, 2)
            pe.wait_ge(relu_rdy, 6 * NPAIR + 2)

            def y_out(j, c):
                pe.wait_ge(h_rdy, j * 4 + (c + 2))
                if c == 0:
                    pe.wait_ge(y_free, j + 1)
                    mm(OB[:], dgS[:], xaS[:], start=True, stop=False, skip_group_check=True)
                for e, h in enumerate(((hr0, hr1)[c % 2], (hi0, hi1)[c % 2])):
                    ins = mm(OB[:], cpS[:, c, e, :], h[:], start=False, stop=(c == 3 and e == 1), skip_group_check=True)
                ins.then_inc(y_mm, 1)

            def b_in(j, c):
                if c == 0:
                    pe.wait_ge(bb_rdy, j + 1)
                    pe.wait_ge(xa_rdy, j + 1)
                pe.wait_ge(bu_free, j * 4 + (c + 1))
                r = slice(32 * c, 32 * c + 32)
                for e in range(2):
                    ins = mm((SB if c % 2 == 0 else TBANK)[e][:], bbS[r, e, :], xaS[r, :], start=True, stop=True)
                ins.then_inc(bu_done, 1)

            def gate(j, c):
                project(Slot(N_S5 + 1, GATE[c], 6, j))

            def s5(j, last):
                gate(j, 0)
                b_in(j, 1)
                gate(j, 1)
                project(Slot(N_S5 + 1, ZA, 6, j))
                y_out(j, 0)
                for c in range(2, 4):
                    b_in(j, c)
                    gate(j, c)
                    y_out(j, c - 1)
                if not last:
                    project(Slot(N_S5 + 1, XA, 6, j))
                    b_in(j + 1, 0)
                else:
                    project(Slot(N_AT))
                y_out(j, 3)
            b_in(0, 0)
            with pe.Fori(0, KH - 1) as j:
                s5(j, False)
            s5(KH - 1, True)

            freed(pe, Slot(N_AT))
            pe.wait_ge(bu_free, NCH + 2)
            pe.wait_ge(y_free, KH + 1)
            scores(NPAIR, qn, kn)
            pe.wait_ge(ya_done, KH + 1)

            def ab_terms(s, e, ks):
                rh, rl = ((y2H, y2L), (ybH, ybL))[s]
                return [(2 * k + e, rh[:, k, :], rl[:, k, :], AB[s][e][:], k == 0, k == KH - 1) for k in ks]

            def att(i, last):
                sl = Slot(N_AT + 1, 0, 2, i)
                pe.wait_ge(gfree[1], sl.gf)
                products(sl, [(2 * k + e, yaH[:, k, :], yaL[:, k, :], PB[1 + 2 * e][:], k == 0, k == KH - 1)
                              for e in range(2) for k in range(KH)])
                if not last:
                    project(Slot(N_AT + 1, 1, 2, i))
                else:
                    pe.wait_ge(gfree[0], Slot(N_AB).gf)
                    pe.wait_ge(y2_done, KH - 1)
                    products(Slot(N_AB), ab_terms(0, 0, range(KH - 1)))
                    pe.wait_ge(th_rdy, KH)
                    products(Slot(N_AB), ab_terms(0, 1, range(KH - 1)))
                attend(i + NPAIR, vt2, lambda hh: slice(0, HD))
                if not last:
                    freed(pe, Slot(N_AT + 1, 1, 2, i))
                    scores(i + (NPAIR + 1), qn, kn)
            with pe.Fori(0, NPAIR - 1) as i:
                att(i, False)
            att(NPAIR - 1, True)

            pe.wait_ge(y2_done, KH)
            products(Slot(N_AB), ab_terms(0, 0, [KH - 1]) + ab_terms(0, 1, [KH - 1]))
            pe.wait_ge(gfree[1], Slot(N_AB, 1).gf)
            pe.wait_ge(yb_done, KH)
            products(Slot(N_AB, 1), ab_terms(1, 0, range(KH)) + ab_terms(1, 1, range(KH)))
            with pe.Fori(1, KD // 2) as i:
                for s in range(2):
                    sl = Slot(N_AB, s, 2, i)
                    pe.wait_ge(gfree[s], sl.gf)
                    products(sl, ab_terms(s, 0, range(KH)) + ab_terms(s, 1, range(KH)))
            def to_tokens(i):
                for s in range(2):
                    pe.wait_ge(xf_rdy, i * 2 + (s + 1))
                    wait(pe, ot_done, i * 2 + 1)
                    transposes(TBANK[s], [(t3, t4)[s][:, blkc(b)] for b in range(TB)]).then_inc(xf_tr, 1)

            project(Slot(N_O2), each=mg_done)
            project(Slot(N_O2, 1))
            with pe.Fori(0, KD // 2 - 1) as i:
                project(Slot(N_O2, 2, 2, i))
                to_tokens(i)
                project(Slot(N_O2, 3, 2, i))
            to_tokens(KD // 2 - 1)
            pe.wait_ge(ssum, 3)
            for t in range(TB):
                ins = mm(PB[4][:, t:t + 1], gr[:, blkc(t)], ones[:, 0:1], start=True, stop=True)
            ins.then_inc(ssm, 1)

        @block.scalar
        def _(act):
            A = nc.scalar.activation

            def copy(o, i_, scale=1.0):
                return A(o, i_, ACT.Copy, scale=scale)

            def split_hi(s):
                act.wait_ge(w_full[s.par], s.half * 16 + 16)
                wait(act, slot_used, s.n - 1)
                copy(wH[s.par][:], raw[s.par][:]).then_inc(hi_done, 1)

            def used(s):
                act.wait_ge(slot_used, s.n + 1)

            def rsqrt(o, ps, scale, k, done):
                act.wait_ge(ssm, k)
                A(o, ps, ACT.Ln, bias=epst[:, 0:1], scale=scale).then_inc(astep, 1)
                a_n[0] += 1
                act.wait_ge(astep, a_n[0])
                A(o, o, ACT.Exp, scale=-0.5).then_inc(done, 1)
            a_n = [0]

            def load_set(n):
                nc.scalar.add_instruction(mybir.InstLoadActFuncSet(
                    name=nc.get_next_instruction_name(), act_func_set_id=n, ins=[], outs=[]))

            for r, v in ((W_ARE, a_re_2), (W_AIM, a_im_2)):
                act.dma_start(row2[r:r + NCH, :], v[0].rearrange("(s g) n -> s (g n)", g=2)).then_inc(svec_in, 16)
            act.dma_start(ldt[W_LDT:W_LDT + NCH, :], log_dt_2[0].rearrange("(s g) -> s g", g=2)).then_inc(svec_in, 16)
            for v, r, n in [(g_mix, V_GMIX, 8), (g_conv_out, V_GCONV, 4), (g_attn_out, V_GATT, 4), (g_ffn, V_GFFN, 8),
                            (c_2, V_C, 8), (norm_g_2, V_NG, 8), (b_mod_2, V_BMOD, 24), (b_glu_2, V_BGLU, 8),
                            (d_skip_2, V_DSK, 4)]:
                act.dma_start(row1[r:r + n, :], v.rearrange("a (n p) -> (a n) p", p=P)).then_inc(vec_in, 16)
            load_set(6)
            for k in range(KD):
                act.wait_ge(xt_done, k + 1)
                wait(act, sq0_used, k - 1)
                A((sqx, a32)[k % 2][:], xT[:, k, :], ACT.Square).then_inc(sq0_rdy, 1)
            split_hi(Slot(0))
            act.wait_ge(init_v, 1)
            act.wait_ge(sq0_used, KD)
            A(r1[:], PB[0][:], ACT.Ln, bias=epst[:, 0:1], scale=1.0 / D).then_inc(astep, 1)
            a_n[0] += 1
            act.wait_ge(astep, a_n[0])
            A(r1[:], r1[:], ACT.Exp, scale=-0.5).then_inc(rr, 1)
            split_hi(Slot(1))
            for k in range(KD):
                act.wait_ge(h1f, k + 1)
                copy(hH[:, k, :], (sg, a32)[k % 2][:]).then_inc(h1h, 1)
            act.wait_ge(vec_rdy, 1)
            A(csil[:], vec[:, V_C:V_C + KD], ACT.Silu).then_inc(trig_a, 1)
            act.wait_ge(trig_r, 1)
            A(sp[:, 6:8, :], sp[:, 4:6, :], ACT.Sin).then_inc(trig_a, 1)

            def qkv(first, i, a):
                s = [Slot(first, j, 6, i) for j in range(3)]
                wait(act, qn_rdy, a)
                wait(act, ss_mm, a * 2)
                for sl, dst, sq in ((s[0], qraw, sqq), (s[1], kraw, sqk)):
                    used(sl)
                    copy(dst[:], PB[sl.par][:])
                    A(sq[:], PB[sl.par][:], ACT.Square).then_inc(gfree[sl.par], 1)
                    split_hi(sl.next())
                used(s[2])
                wait(act, vtr, a)
                copy(vT[:], PB[s[2].par][:]).then_inc(gfree[s[2].par], 1)

            def head_rsqrt(a):
                for e, r in enumerate((rq, rk)):
                    act.wait_ge(ss_mm, a * 2 + (e + 1))
                    A(r[:], SB[e][:], ACT.Ln, bias=epst[:, 0:1], scale=1.0 / HD).then_inc(ss_rd, 1)
                    act.wait_ge(ss_rd, a * 2 + (e + 1))
                    A(r[:], r[:], ACT.Exp, scale=-0.5).then_inc(rs_rdy, 1)

            def softmax(a):
                for hh in range(2):
                    act.wait_ge(nm, a * 2 + (hh + 1))
                    for b in range(TB):
                        c = 4 * hh + b
                        l = L[:, hh, CB[b]:CB[b + 1]]
                        ins = A(l, l, ACT.Exp, bias=nmx[:, c:c + 1], accum_out=rs[:, c:c + 1])
                    ins.then_inc(ex, 1)

            def p_evac(a):
                for hh in range(2):
                    for kb in range(TB):
                        act.wait_ge(tr_mm, a * 8 + (4 * hh + kb + 1))
                        n = S - P * kb
                        copy(pT[:, hh, OFF[kb]:OFF[kb + 1]], TBANK[kb][:, 0:n]).then_inc(t_free, 1)

            def mix(i, last):
                head_rsqrt(i)
                u, gc, gb = (Slot(3, j, 6, i) for j in range(3))
                used(u)
                if not (isinstance(i, int) and i == 0):
                    wait(act, ych, i + 1)
                copy(u_s[:], PB[u.par][:]).then_inc(gfree[u.par], 1)
                split_hi(u.next())
                act.wait_ge(qn_rdy, i + 1)
                copy(q1[0][0:HD, :], qn[0:HD, :])
                copy(q1[1][HD:P, :], qn[HD:P, :])
                for e in range(2):
                    r = slice(HD * e, HD * e + HD)
                    copy(k1[e][0:HD, :], kn[r, :])
                    ins = copy(k1[e][HD:P, :], kn[r, :])
                ins.then_inc(q_hi, 1)
                used(gc)
                split_hi(gc.next())
                used(gb)
                split_hi(gb.next())
                freed(act, gb)
                A(sqc[:], yc[:], ACT.Square)
                A(dyn(mixH, i), yc[:], ACT.Identity, scale=vec[:, bass.ds(i + V_GCONV, 1)]).then_inc(ych, 1)
                act.wait_ge(vtr, i + 1)
                copy(vtok[:].rearrange("p b n -> p (b n)"), PB[3][:]).then_inc(vt_done, 1)
                softmax(i)
                if not last:
                    qkv(6, i, i + 1)
                p_evac(i)
                if not last:
                    split_hi(Slot(6, 2, 6, i).next())
                act.wait_ge(pv, i * 2 + 2)
                copy(yo[:], OB[:])
                A(sqa[:], OB[:], ACT.Square)
                A(dyn(mixH, i + KH), OB[:], ACT.Identity, scale=vec[:, bass.ds(i + V_GATT, 1)]).then_inc(o_free, 1)

            def dyn(t, k):
                return t[:, k, :] if isinstance(k, int) else t[:, bass.ds(k, 1), :].rearrange("p k t -> p (k t)")

            for s, n in ((t_free, 4), (ych, 1), (y_free, 1), (o_free, 1)):
                for _ in range(n):
                    act.nop().then_inc(s, 1)
            qkv(0, 0, 0)
            split_hi(Slot(0, 2).next())
            load_set(6)
            with act.Fori(0, NPAIR - 1) as i:
                mix(i, False)
            mix(NPAIR - 1, True)

            rsqrt(rc[:], PB[4][:], 1.0 / HALF, 1, rr)
            rsqrt(ra[:], PB[5][:], 1.0 / HALF, 2, rr)
            with act.Fori(0, KD // 2) as i:
                for s in range(2):
                    sl, d = Slot(N_WO, s, 2, i), i * 2 + s
                    used(sl)
                    split_hi(sl.next())
                    act.wait_ge(x1_rdy, d + 1)
                    A(sqx[:], dyn(xT, d), ACT.Square)
                    A(dyn(hH, d), dyn(xT, d), ACT.Identity, scale=vec[:, bass.ds(d + V_GFFN, 1)]).then_inc(x1h, 1)

            rsqrt(r1[:], PB[4][:], 1.0 / D, 3, rr)
            load_set(18)
            with act.Fori(0, KF) as i:
                g_, u_ = Slot(N_FF, 0, 2, i), Slot(N_FF, 1, 2, i)
                used(g_)
                split_hi(g_.next())
                freed(act, g_)
                A(sg[:], gt[:], ACT.Silu).then_inc(sg_rdy, 1)
                used(u_)
                split_hi(u_.next())
                act.wait_ge(a32_rdy, i + 1)
                copy(dyn(aH, i), a32[:]).then_inc(ah_rdy, 1)
            with act.Fori(0, KF // 2) as i:
                for s in range(2):
                    sl = Slot(N_DN, s, 2, i)
                    used(sl)
                    split_hi(sl.next())

            load_set(6)
            for d in range(KD):
                act.wait_ge(x1_rdy, KD + d + 1)
                wait(act, sq2_used, d - 1)
                A((sqx, a32)[d % 2][:], xT[:, d, :], ACT.Square).then_inc(sq2_rdy, 1)
            act.wait_ge(sq2_used, KD)
            rsqrt(r1[:], PB[0][:], 1.0 / D, 3, rr)
            for d in range(KD):
                act.wait_ge(h2f, d + 1)
                A(hH[:, d, :], (sg, a32)[d % 2][:], ACT.Identity, bias=mod[:, d:d + 1]).then_inc(h2h, 1)
            kv, ki = Slot(N_KV, 0), Slot(N_KV, 1)
            used(kv)
            act.wait_ge(e_out, 16 * NCH)
            copy(kvraw[:], PB[0][:]).then_inc(gfree[0], 1)
            split_hi(kv.next())
            used(ki)
            copy(kiraw[0:NKI, :], PB[1][0:NKI, :]).then_inc(gfree[1], 1)
            act.wait_ge(gfree[1], Slot(N_KV, 1).gf + 1)
            copy(kx[0:HD, :], kiraw[0:HD, :])
            copy(kx[HD:P, :], kiraw[0:HD, :]).then_inc(kx_hi, 1)
            split_hi(ki.next())
            for e in range(2):
                act.wait_ge(s5_tr, e + 3)
                copy(bbT[:, e].rearrange("p k n -> p (k n)"), PB[6 + e][:]).then_inc(s5_ev, 1)
            act.wait_ge(kv_tr, 1)
            copy(vt2[:], PB[3][:].rearrange("p (b n) -> p b n", b=TB)[:, :, HD:2 * HD]).then_inc(kv_ev, 1)
            act.wait_ge(kv_tr, 2)
            copy(wtok[:], PB[2][:].rearrange("p (b n) -> p b n", b=TB)[:, :, HD:HD + 8]).then_inc(kv_ev, 1)

            load_set(18)
            act.nop().then_inc(relu_rdy, 1)
            act.nop().then_inc(relu_rdy, 1)
            with act.Fori(0, NPAIR) as i:
                q, z = Slot(N_IX, 0, 2, i), Slot(N_IX, 1, 2, i)
                used(q)
                wait(act, ix_ready, i * 6 + 1)
                copy(qx[0][0:HD, :], PB[0][0:HD, :])
                copy(qx[1][HD:P, :], PB[0][HD:P, :]).then_inc(qx_hi, 1)
                split_hi(q.next())
                used(z)
                for hh in range(2):
                    for b in range(1, TB):
                        u = 3 * hh + b - 1
                        act.wait_ge(ix_ready, i * 6 + (u + 2))
                        act.wait_ge(r_used, i * 6 + (u + 2))
                        A(relu_b[u % 2][:, 0:P * (b + 1)], SB[u % 2][:, 0:P * (b + 1)], ACT.Relu,
                          scale=IDX_SCALE).then_inc(relu_rdy, 1)
                A(dyn(szb, i), PB[1][:], ACT.Silu).then_inc(gfree[1], 1)
                split_hi(z.next())

            xa = Slot(N_S5)
            used(xa)
            copy(xaS[:], PB[xa.par][:]).then_inc(xa_rdy, 1)
            act.wait_ge(xa_rdy, 1)
            act.nop().then_inc(gfree[xa.par], 1)
            split_hi(xa.next())

            def s5(j, last):
                for c in range(4):
                    s = Slot(N_S5 + 1, GATE[c], 6, j)
                    used(s)
                    A(dyn((tga, tgb)[c % 2], j * 2 + c // 2), PB[s.par][:], ACT.Tanh, scale=0.5).then_inc(gfree[s.par], 1)
                    if last and c == 3:
                        act.wait_ge(glu_full, 16)
                    split_hi(s.next())
                    if c == 1:
                        s = Slot(N_S5 + 1, ZA, 6, j)
                        used(s)
                        A(dyn(sza, j), PB[s.par][:], ACT.Silu).then_inc(gfree[s.par], 1)
                        split_hi(s.next())
                if not last:
                    s = Slot(N_S5 + 1, XA, 6, j)
                    used(s)
                    copy(xaS[:], PB[s.par][:]).then_inc(xa_rdy, 1)
                    act.wait_ge(xa_rdy, j + 2)
                    act.nop().then_inc(gfree[s.par], 1)
                    split_hi(s.next())
                if last:
                    s = Slot(N_AT)
                    used(s)
                    copy(qn[:], PB[0][:], HD ** -0.5).then_inc(gfree[0], 1)
                    split_hi(s.next())
                act.wait_ge(y_mm, j * 4 + 6)
                wait(act, ya_done, j + 1)
                A(yg[:], OB[:], ACT.Gelu_apprx_tanh).then_inc(y_free, 1)
                act.wait_ge(y_free, j + 2)
                copy(dyn(yaH, j), yg[:]).then_inc(ya_h, 1)
            with act.Fori(0, KH - 1) as j:
                s5(j, False)
            s5(KH - 1, True)

            load_set(0)

            def att(i, last):
                softmax(i + NPAIR)
                s = Slot(N_AT + 1, 0, 2, i)
                used(s)
                if not last:
                    act.wait_ge(glu_full, i * 16 + 32)
                split_hi(s.next())
                A(thg[:], PB[3][:], ACT.Tanh, bias=hbg[:, bass.ds(i, 1)], scale=0.5).then_inc(th_rdy, 1)
                freed(act, s)
                copy(dyn(y2H, i), dyn(sza, i), 0.5).then_inc(y2h, 1)
                if not last:
                    s = Slot(N_AT + 1, 1, 2, i)
                    used(s)
                    copy(qn[:], PB[0][:], HD ** -0.5).then_inc(gfree[0], 1)
                p_evac(i + NPAIR)
                if not last:
                    split_hi(s.next())
                act.wait_ge(o_free, i + (NPAIR + 1) + 1)
                copy(dyn(ybH, i), dyn(szb, i)).then_inc(ybh, 1)
            with act.Fori(0, NPAIR - 1) as i:
                att(i, False)
            att(NPAIR - 1, True)

            with act.Fori(0, KD // 2) as i:
                for s in range(2):
                    sl = Slot(N_AB, s, 2, i)
                    used(sl)
                    split_hi(sl.next())
                for e in range(2):
                    act.wait_ge(mg_rdy, i * 2 + (e + 1))
                    copy(dyn(hH, i * 2 + e), dyn(tga, i * 2 + e), 0.5).then_inc(mgh, 1)

            def out2(i, last):
                for s in range(2):
                    sl, d = Slot(N_O2, s, 2, i), i * 2 + s
                    if not last:
                        used(sl)
                        split_hi(sl.next())
                    act.wait_ge(x3_rdy, d + 1)
                    act.wait_ge(ot_done, i * 2 + 1)
                    A((t1, t2)[s][:], dyn(xT, d), ACT.Square)
                    A((t3, t4)[s][:], dyn(xT, d), ACT.Identity, scale=vec[:, bass.ds(d + V_FG, 1)]).then_inc(xf_rdy, 1)
            with act.Fori(0, KD // 2 - 1) as i:
                out2(i, False)
            out2(KD // 2 - 1, True)
            load_set(6)
            act.wait_ge(ssm, 4)
            A(sm[:, 12:16], PB[4][:, 0:4], ACT.Ln, bias=epst[:, 0:1], scale=1.0 / D).then_inc(astep, 1)
            a_n[0] += 1
            act.wait_ge(astep, a_n[0])
            A(sm[:, 16:20], sm[:, 12:16], ACT.Exp, scale=-0.5).then_inc(rr, 1)
            act.wait_ge(r_fin, 1)
            for t in range(1, TB, 2):
                A(out_tok[:, t, :], out_tok[:, t, :], ACT.Copy, scale=sm[:, 16 + t:17 + t]).then_inc(fin[t], 1)

        @block.vector
        def _(dve):
            v = nc.vector
            TT, TS, STT = v.tensor_tensor, v.tensor_scalar, v.scalar_tensor_tensor
            MU, AD, SU = ALU.mult, ALU.add, ALU.subtract
            st = Steps(dve, vstep)
            mark, need = st.mark, st.need

            def dyn(t, k):
                return t[:, k, :] if isinstance(k, int) else t[:, bass.ds(k, 1), :].rearrange("p k t -> p (k t)")

            def col(t, k):
                return t[:, bass.ds(k, 1)] if not isinstance(k, int) else t[:, k:k + 1]

            def split_lo(s):
                dve.wait_ge(hi_done, s.n + 1)
                TT(wL[s.par][:], raw[s.par][:], wH[s.par][:].bitcast(F32), SU).then_inc(lo_done, 1)

            def used(s):
                dve.wait_ge(slot_used, s.n + 1)

            def newton(r, ss, scale, ta, tb):
                mark(TS(ta, ss, scale, EPS, MU, AD))
                mark(TT(tb, r, r, MU))
                need()
                mark(TT(tb, tb, ta, MU))
                need()
                mark(TS(tb, tb, -0.5, 1.5, MU, AD))
                need()
                return mark(TT(r, r, tb, MU))

            for s, n in ((sc_free, 4), (m_used, 3), (r_used, 3), (bu_free, 2), (e_used, 2), (h_rdy, 1), (ot_done, 1), (ya_done, 1)):
                for _ in range(n):
                    dve.nop().then_inc(s, 1)
            v.memset(epst[:], EPS).then_inc(init_v, 1)
            v.memset(ones[:], 1.0)
            mark(v.memset(cuP[:, 0:2], 0.0))
            dve.wait_ge(svec_in, 16 * 3)
            for e in range(2):
                ins = v.tensor_copy(row2[32:48, e * HD:(e + 1) * HD], ldt[32:48, e:e + 1].broadcast_to([NCH, HD]))
            ins.then_inc(r0d, 1)
            dve.wait_ge(pe_pre, 1)
            v.tensor_copy(svec[:], PB[7][:, 0:NV2]).then_inc(vec_cp, 1)
            dve.wait_ge(vec_cp, 1)

            def par(k):
                return sp[:, k, :]

            def seq(*fs):
                for f in fs:
                    need()
                    mark(f())

            MAGIC, PI, TWO_PI = 12582912.0, 3.1415925, 6.283185307179586
            LN2H, LN2L = 0.693359375, -2.12194440e-4

            def exp(dst, src):
                z, n, r, p = par(8), par(9), par(10), par(11)
                seq(lambda: TS(z, src, -87.0, 88.0, ALU.max, ALU.min),
                    lambda: TS(n, z, 1.4426950408889634, MAGIC, MU, AD),
                    lambda: TS(n, n, MAGIC, None, SU),
                    lambda: STT(r, n, -LN2H, z, MU, AD),
                    lambda: STT(r, n, -LN2L, r, MU, AD),
                    lambda: TS(p, r, 1 / 5040, None, MU))
                for c in (1 / 720, 1 / 120, 1 / 24, 1 / 6, 1 / 2, 1.0):
                    seq(lambda: STT(p, p, c, r, AD, MU))
                seq(lambda: TS(n, n, 127.0, None, AD),
                    lambda: v.tensor_copy(spi[:], n),
                    lambda: TS(spi[:], spi[:], 23, None, ALU.logical_shift_left),
                    lambda: STT(dst, p, 1.0, spi[:].bitcast(F32), AD, MU))

            are, aim = svec[:, 0:NCH], svec[:, NCH:2 * NCH]
            exp(par(0), svec[:, 2 * NCH:3 * NCH])
            C1, C2 = 6.28125, 1.93500518798828125e-3
            C3 = TWO_PI - C1 - C2
            th, n, r, t = par(2), par(9), par(4), par(10)
            seq(lambda: TT(th, aim, par(0), MU),
                lambda: TS(n, th, 1 / TWO_PI, MAGIC, MU, AD),
                lambda: TS(n, n, MAGIC, None, SU),
                lambda: STT(th, n, -C1, th, MU, AD),
                lambda: STT(th, n, -C2, th, MU, AD),
                lambda: STT(th, n, -C3, th, MU, AD),
                lambda: TS(r, th, PI, -PI, ALU.min, ALU.max),
                lambda: TS(par(5), th, TWO_PI / 4, None, AD),
                lambda: TS(t, par(5), PI, -TWO_PI, ALU.is_gt, MU),
                lambda: TT(par(5), par(5), t, AD),
                lambda: TS(par(5), par(5), PI, -PI, ALU.min, ALU.max))
            need()
            v.tensor_copy(par(3), par(5)).then_inc(trig_r, 1)

            for k in range(KD):
                dve.wait_ge(xt_mm, k + 1)
                v.tensor_copy(xT[:, k, :], PB[k][:]).then_inc(xt_done, 1)
            dve.wait_ge(pe_pre, 2)
            mark(v.tensor_copy(vec[:], PB[1][:, 0:NV1]))
            need()
            mark(TS(hbg[:], vec[:, V_BGLU + KH:V_BGLU + 2 * KH], 0.5, None, MU))
            TS(vec[:, V_GQ:V_GQ + 1], vec[:, V_GQ:V_GQ + 1], HD ** -0.5, None, MU).then_inc(vec_rdy, 1)
            split_lo(Slot(0))
            dve.wait_ge(rr, 1)
            need(newton(r1[:], PB[0][:], 1.0 / D, gt[:], ut[:]))

            def h1_low(k):
                dve.wait_ge(h1h, k + 1)
                TT(hL[:, k, :], (sg, a32)[k % 2][:], hH[:, k, :].bitcast(F32), SU).then_inc(h1_done, 1)
            for k in range(KD):
                wait(dve, h1_done, k - 1)
                STT((sg, a32)[k % 2][:], xT[:, k, :], vec[:, V_GMIX + k:V_GMIX + k + 1], r1[:], MU, MU).then_inc(h1f, 1)
                if k:
                    h1_low(k - 1)
            h1_low(KD - 1)
            split_lo(Slot(1))


            def qk_norm(a):
                dve.wait_ge(rs_rdy, a * 2 + 1)
                STT(qn[:], qraw[:], vec[:, V_GQ:V_GQ + 1], rq[:], MU, MU)
                dve.wait_ge(rs_rdy, a * 2 + 2)
                STT(kn[:], kraw[:], vec[:, V_GK:V_GK + 1], rk[:], MU, MU).then_inc(qn_rdy, 1)

            def score_max(a, masks):
                for hh in range(2):
                    for b in range(TB):
                        u, c = 4 * hh + b, 4 * hh + b
                        dve.wait_ge(sc_ready, a * 8 + (u + 1))
                        settled(dve)
                        v.tensor_tensor_reduce(L[:, hh, CB[b]:CB[b + 1]], SB[b][:, 0:P * (b + 1)], masks[b], 1.0,
                                               GONE, AD, ALU.max, mx[:, c:c + 1]).then_inc(sc_free, 1)
                    dve.wait_ge(sc_free, a * 8 + (4 * hh + 4 + 4))
                    TS(nmx[:, 4 * hh:4 * hh + 4], mx[:, 4 * hh:4 * hh + 4], -1.0, None, MU).then_inc(nm, 1)

            def normalise(a):
                for hh in range(2):
                    dve.wait_ge(ex, a * 2 + (hh + 1))
                    mark(v.reciprocal(rinv[:, 4 * hh:4 * hh + 4], rs[:, 4 * hh:4 * hh + 4]))
                    need()
                    for b in range(TB):
                        l = L[:, hh, CB[b]:CB[b + 1]]
                        ins = TS(l, l, rinv[:, 4 * hh + b:4 * hh + b + 1], None, MU)
                    ins.then_inc(pn, 1)

            def mod_rows(i, ms):
                for m in ms:
                    dve.wait_ge(m_full[m % 2], i * 48 + 16 * (m // 2 + 1))
                    wait(dve, m_used, i * 6 + m + 1)
                    o = macc[:, (m % 3) * D:(m % 3 + 1) * D]
                    STT(o, mraw[m % 2][:], col(csil, i * 2 + m // 3), o, MU, AD).then_inc(m_used, 1)

            def mix(i, last):
                qk_norm(i)
                u, gc, gb = (Slot(3, j, 6, i) for j in range(3))
                split_lo(u.next())
                used(gc)
                freed(dve, u)
                mark(TT(cuP[:, 2:S + 2], PB[gc.par][:], u_s[:], MU))
                need()
                TS(cv[:], cuP[:, 2:S + 2], col(vec, i + (V_CONV + 8)), None, MU).then_inc(gfree[gc.par], 1)
                split_lo(gc.next())
                dve.wait_ge(q_hi, i + 1)
                TT(q1[0][HD:P, :], qn[0:HD, :], q1[0][0:HD, :].bitcast(F32), SU)
                TT(q1[1][0:HD, :], qn[HD:P, :], q1[1][HD:P, :].bitcast(F32), SU)
                TT(k1L[0:HD, :], kn[0:HD, :], k1[0][0:HD, :].bitcast(F32), SU)
                TT(k1L[HD:P, :], kn[HD:P, :], k1[1][HD:P, :].bitcast(F32), SU).then_inc(q_lo, 1)
                freed(dve, gc)
                mark(STT(cv[:], cuP[:, 1:S + 1], col(vec, i + (V_CONV + 4)), cv[:], MU, AD))
                need()
                mark(STT(cv[:], cuP[:, 0:S], col(vec, i + V_CONV), cv[:], MU, AD))
                used(gb)
                need()
                wait(dve, ych, i + 1)
                TT(yc[:], PB[gb.par][:], cv[:], MU).then_inc(gfree[gb.par], 1)
                score_max(i, [mask1[:, S - P * (b + 1):S] for b in range(TB)])
                split_lo(gb.next())
                dve.wait_ge(ych, i + 2)
                mark(TT(ssc[:], ssc[:], sqc[:], AD))
                mark(STT(dyn(mixL, i), yc[:], col(vec, i + V_GCONV), dyn(mixH, i).bitcast(F32), MU, SU))
                if last:
                    need()
                    dve.nop().then_inc(cv_split, 1)
                mod_rows(i, range(0, 2))
                normalise(i)
                if not last:
                    split_lo(Slot(3, 3, 6, i).next())
                    mod_rows(i, range(2, 4))
                    split_lo(Slot(3, 4, 6, i).next())
                    mod_rows(i, range(4, 6))
                    split_lo(Slot(3, 5, 6, i).next())
                dve.wait_ge(o_free, i + 2)
                mark(TT(ssa[:], ssa[:], sqa[:], AD))
                mark(STT(dyn(mixL, i + KH), yo[:], col(vec, i + V_GATT), dyn(mixH, i + KH).bitcast(F32), MU, SU))

            dve.wait_ge(init_p, 1)
            dve.wait_ge(mask_in, 16)
            for j in range(3):
                split_lo(Slot(0, j).next())
            with dve.Fori(0, NPAIR - 1) as i:
                st.enter(i, MIX_STEPS)
                mix(i, False)
                st.leave(NPAIR - 1)
            mix(NPAIR - 1, True)
            need()
            v.memset(ss1[:], 0.0).then_inc(ssum, 1)

            dve.wait_ge(rr, 2)
            need(newton(rc[:], PB[4][:], 1.0 / HALF, nt1[:], nt2[:]))
            split_lo(Slot(N_WO).next())
            dve.wait_ge(rr, 3)
            need(newton(ra[:], PB[5][:], 1.0 / HALF, nt1[:], nt2[:]))
            def out_block(i, first=False):
                for s in range(2):
                    sl, d = Slot(N_WO, s, 2, i), i * 2 + s
                    used(sl)
                    mark(TT(wo1[:], PB[s][:], rc[:], MU))
                    TT(wo2[:], PB[2 + s][:], ra[:], MU).then_inc(gfree[s], 1)
                    need()
                    mark(TT(dyn(xT, d), dyn(xT, d), wo1[:], AD))
                    freed(dve, sl)
                    need()
                    TT(dyn(xT, d), dyn(xT, d), wo2[:], AD).then_inc(x1_rdy, 1)
                    if s or not first:
                        split_lo(sl.next())
                    dve.wait_ge(x1h, d + 1)
                    mark(TT(ss1[:], ss1[:], sqx[:], AD))
                    STT(dyn(hL, d), dyn(xT, d), col(vec, d + V_GFFN), dyn(hH, d).bitcast(F32), MU, SU).then_inc(x1l, 1)
                    need()
                    mark(v.memset(m8[:, 0, 0:1], 0.0))
            out_block(0, True)
            with dve.Fori(1, KD // 2) as i:
                st.enter(i - 1, 8)
                out_block(i)
                st.leave(KD // 2 - 1)
            need()
            v.memset(m8[:, 0, 0:1], 0.0).then_inc(ssum, 1)

            dve.wait_ge(rr, 4)
            need(newton(r1[:], PB[4][:], 1.0 / D, gt[:], ut[:]))
            def gate(i):
                g_, u_ = Slot(N_FF, 0, 2, i), Slot(N_FF, 1, 2, i)
                used(g_)
                TT(gt[:], PB[0][:], r1[:], MU).then_inc(gfree[0], 1)
                split_lo(g_.next())
                used(u_)
                TT(ut[:], PB[1][:], r1[:], MU).then_inc(gfree[1], 1)
                split_lo(u_.next())
                dve.wait_ge(sg_rdy, i + 1)
                freed(dve, u_)
                TT(a32[:], sg[:], ut[:], MU).then_inc(a32_rdy, 1)
                dve.wait_ge(ah_rdy, i + 1)
                TT(dyn(aL, i), a32[:], dyn(aH, i).bitcast(F32), SU).then_inc(a_done, 1)

            sn, cs = par(6), par(7)
            nr, ni, den, rd, crr, cri, t = (par(k) for k in (12, 13, 14, 8, 15, 16, 10))

            def decay():
                seq(lambda: TT(par(12), are, par(0), MU))
                exp(par(1), par(12))

            def gains_1():
                seq(lambda: TT(nr, par(1), cs, MU),
                    lambda: TS(nr, nr, -1.0, None, AD),
                    lambda: TT(ni, par(1), sn, MU),
                    lambda: TT(den, are, are, MU),
                    lambda: TT(t, aim, aim, MU),
                    lambda: TT(den, den, t, AD),
                    lambda: v.reciprocal(rd, den),
                    lambda: TT(crr, nr, are, MU))

            def gains_2():
                seq(lambda: TT(t, ni, aim, MU),
                    lambda: TT(crr, crr, t, AD),
                    lambda: TT(crr, crr, rd, MU),
                    lambda: TT(cri, ni, are, MU),
                    lambda: TT(t, nr, aim, MU),
                    lambda: TT(cri, cri, t, SU),
                    lambda: TT(cri, cri, rd, MU))

            def powers(k0, k1):
                if k0 == 0:
                    mark(v.tensor_copy(pw[:, 0, 0, :], cs))
                    mark(v.tensor_copy(pw[:, 1, 0, :], sn))
                for k in range(k0, k1):
                    c, s = pw[:, 0, k, :], pw[:, 1, k, :]
                    need()
                    mark(TT(par(9), c, s, SU))
                    mark(TT(par(10), c, s, AD))
                    need()
                    mark(STT(pw[:, 1, k + 1, :], c, 2.0, s, MU, MU))
                    mark(TT(pw[:, 0, k + 1, :], par(9), par(10), MU))

            def modulation():
                dve.wait_ge(mod_mm, 1)
                mark(TT(mod[:], PB[6][:, 0:3 * KD], vec[:, V_BMOD:V_BMOD + 3 * KD], AD))
                need()
                dve.nop().then_inc(mod_cp, 1)
                mark(STT(gs[:], mod[:, KD:2 * KD], 1.0, vec[:, V_NG:V_NG + KD], AD, MU))

            dve.wait_ge(trig_a, 2)
            pieces = (decay, gains_1, gains_2, lambda: powers(0, 4), lambda: powers(4, LEVELS - 1),
                      lambda: mod_rows(NPAIR - 1, (2, 3)), lambda: mod_rows(NPAIR - 1, (4, 5)), lambda: None, modulation)
            assert len(pieces) == MOD_AT + 1
            for i, piece in enumerate(pieces):
                gate(i)
                piece()
            need()
            v.tensor_copy(par(17), par(9)).then_inc(pw_rdy, 1)
            with dve.Fori(len(pieces), KF) as i:
                gate(i)
            with dve.Fori(0, KF // 2) as i:
                for s in range(2):
                    split_lo(Slot(N_DN, s, 2, i).next())

            for d in range(KD):
                if d < KD - 1:
                    dve.wait_ge(dn_done, d + 1)
                else:
                    dve.wait_ge(slot_used, N_DN + KF)
                TT(xT[:, d, :], xT[:, d, :], PB[d][:], AD).then_inc(x1_rdy, 1)
            v.memset(cTt[:], 0.0)
            mark(v.memset(bdg[:], 0.0))
            dve.wait_ge(rr, 5)
            need(newton(r1[:], PB[0][:], 1.0 / D, gt[:], ut[:]))

            def h2_low(d):
                dve.wait_ge(h2h, d + 1)
                STT(hL[:, d, :], (sg, a32)[d % 2][:], mod[:, d:d + 1], hH[:, d, :].bitcast(F32), AD, SU
                    ).then_inc(h2_done, 1)
            for d in range(KD):
                wait(dve, h2_done, d - 1)
                STT((sg, a32)[d % 2][:], xT[:, d, :], gs[:, d:d + 1], r1[:], MU, MU).then_inc(h2f, 1)
                if d:
                    h2_low(d - 1)
            h2_low(KD - 1)

            dve.wait_ge(s5_in, 64)
            dve.wait_ge(e_out, 16 * NCH)

            def over(k):
                return par(k).unsqueeze(2).broadcast_to([P, NCH, GP])
            tb_ = [t[:, 0:NCH * GP].rearrange("p (s q) -> p s q", q=GP) for t in (t3, t4, gr, gi)]
            mark(TT(tb_[0], braw[:, 0], over(15), MU))
            mark(TT(tb_[1], braw[:, 1], over(16), MU))
            mark(TT(tb_[2], braw[:, 1], over(15), MU))
            mark(TT(tb_[3], braw[:, 0], over(16), MU))
            need()
            for g2 in range(2):
                r = slice(HD * g2, HD * g2 + HD)
                mark(TT(bdg[r, 0, :, GP * g2:GP * g2 + GP], tb_[0][r], tb_[1][r], SU))
                ins = TT(bdg[r, 1, :, GP * g2:GP * g2 + GP], tb_[2][r], tb_[3][r], AD)
            ins.then_inc(bd_rdy, 1)
            split_lo(Slot(N_KV, 0).next())
            freed(dve, Slot(N_KV, 0))
            v.tensor_copy(kn[0:HD, :], kvraw[0:HD, :])
            v.tensor_copy(kn[HD:P, :], kvraw[0:HD, :]).then_inc(kdup, 1)
            split_lo(Slot(N_KV, 1).next())
            dve.wait_ge(kx_hi, 1)
            TT(kxL[0:HD, :], kiraw[0:HD, :], kx[0:HD, :].bitcast(F32), SU)
            TT(kxL[HD:P, :], kiraw[0:HD, :], kx[0:HD, :].bitcast(F32), SU).then_inc(kdup, 1)
            for e in range(2):
                dve.wait_ge(s5_tr, 1 + e)
                for g2 in range(2):
                    src = PB[4 + e][0:HD, :].rearrange("n (s g q) -> n s g q", g=2, q=GP)[:, :, g2, :]
                    ins = TS(cTt[HD * g2:HD * g2 + HD, e, :, GP * g2:GP * g2 + GP], src, (1.0, -1.0)[e], None, MU)
            ins.then_inc(s5_cv, 1)

            m_s = mark(v.memset(score[:], 0.0))
            dve.wait_ge(kv_ev, 2)
            need(m_s)
            with dve.Fori(0, NPAIR) as i:
                q, z = Slot(N_IX, 0, 2, i), Slot(N_IX, 1, 2, i)
                dve.wait_ge(qx_hi, i + 1)
                TT(qx[0][HD:P, :], PB[0][0:HD, :], qx[0][0:HD, :].bitcast(F32), SU)
                TT(qx[1][0:HD, :], PB[0][HD:P, :], qx[1][HD:P, :].bitcast(F32), SU).then_inc(gfree[0], 1)
                split_lo(q.next())
                for hh in range(2):
                    for b in range(1, TB):
                        u = 3 * hh + b - 1
                        dve.wait_ge(relu_rdy, i * 6 + (u + 1 + 2))
                        wait(dve, r_used, i * 6 + u + 1)
                        sc = score[:, CB[b]:CB[b + 1]]
                        STT(sc, relu_b[u % 2][:, 0:P * (b + 1)], wtok[:, b, bass.ds(i * 2 + hh, 1)], sc, MU, AD
                            ).then_inc(r_used, 1)
                split_lo(z.next())
            dve.wait_ge(r_used, 6 * NPAIR + 3)
            for b in range(1, TB):
                mark(STT(score[:, CB[b + 1] - P:CB[b + 1]], diag, GONE, score[:, CB[b + 1] - P:CB[b + 1]], MU, AD))
            need()
            mark(v.tensor_copy(work[:, P:CB[4]], score[:, P:CB[4]]))

            def best8():
                need()
                settled(dve)
                for b in range(3):
                    mark(v.max(m8[:, b, :], work[:, CB[b + 1]:CB[b + 2]]))

            def take8(m):
                need(m)
                settled(dve)
                for b in range(3):
                    w = work[:, CB[b + 1]:CB[b + 2]]
                    mark(v.match_replace(w, m8[:, b, :], w, GONE))

            def gelu_low(j):
                dve.wait_ge(ya_h, j + 1)
                STT(dyn(yaL, j), yg[:], 1.0, dyn(yaH, j).bitcast(F32), MU, SU).then_inc(ya_done, 1)

            def s5(j, last):
                for c in range(4):
                    q = j * 4 + c
                    br, bi = (b[:] for b in (SB if c % 2 == 0 else TBANK)[0:2])
                    co, si = ebuf[c % 2][:, 0, :], ebuf[c % 2][:, 1, :]
                    dve.wait_ge(bu_done, q + 1)
                    dve.wait_ge(e_full[c % 2], j * 32 + 16 * (c // 2 + 1))
                    dve.wait_ge(h_rdy, q + 1)
                    TT(t1[:], br, co, MU)
                    TT(t2[:], bi, si, MU)
                    TT(t3[:], bi, co, MU)
                    TT(t4[:], br, si, MU).then_inc(bu_free, 1)
                    best8()
                    m = st.k
                    if c == 0 and not (isinstance(j, int) and j == 0):
                        gelu_low(j - 1)
                    mg = par(1)[:, bass.ds(q, 1)] if not isinstance(q, int) else par(1)[:, q:q + 1]
                    dve.wait_ge(rot_rdy, q * 2 + 1)
                    settled(dve)
                    a = mark(v.tensor_tensor_scan(gr[:], mg.broadcast_to([P, S]), t1[:], 0.0, MU, AD))
                    dve.wait_ge(rot_rdy, q * 2 + 2)
                    settled(dve)
                    mark(v.tensor_tensor_scan(gi[:], mg.broadcast_to([P, S]), t3[:], 0.0, MU, AD))
                    need(a)
                    TT(t1[:], gr[:], co, MU)
                    need()
                    TT(t2[:], gi[:], si, MU)
                    TT(t3[:], gr[:], si, MU)
                    TT(t4[:], gi[:], co, MU).then_inc(e_used, 1)
                    split_lo(Slot(N_S5 + 1, GATE[c], 6, j).next())
                    if c == 1:
                        split_lo(Slot(N_S5 + 1, ZA, 6, j).next())
                    take8(m)
                if not last:
                    split_lo(Slot(N_S5 + 1, XA, 6, j).next())

            split_lo(Slot(N_S5).next())
            s5(0, False)
            with dve.Fori(1, KH - 1) as j:
                st.enter(j - 1, S5_STEPS)
                s5(j, False)
                st.leave(KH - 2)
            s5(KH - 1, True)
            gelu_low(KH - 1)
            need()
            mark(TT(work[:, P:CB[4]], work[:, P:CB[4]], score[:, P:CB[4]], ALU.is_lt))
            need()
            mark(TS(score[:, P:CB[4]], work[:, P:CB[4]], -1.0, -NEG, AD, MU))
            mark(TS(score[:, 0:P], diag, NEG, None, MU))
            need()

            masks = [score[:, CB[b]:CB[b + 1]] for b in range(TB)]
            split_lo(Slot(N_AT).next())
            score_max(NPAIR, masks)

            def att(i, last):
                normalise(i + NPAIR)
                s = Slot(N_AT + 1, 0, 2, i)
                used(s)
                mark(STT(dyn(sza, i), PB[1][:], col(vec, i + V_BGLU), dyn(sza, i), AD, MU))
                split_lo(s.next())
                need()
                dve.wait_ge(th_rdy, i + 1)
                STT(dyn(sza, i), thg[:], 1.0, dyn(sza, i), AD, MU).then_inc(gfree[1], 1)
                dve.wait_ge(y2h, i + 1)
                STT(dyn(y2L, i), dyn(sza, i), 0.5, dyn(y2H, i).bitcast(F32), MU, SU).then_inc(y2_done, 1)
                dve.wait_ge(pv, (i + NPAIR) * 2 + 2)
                TT(dyn(szb, i), OB[:], dyn(szb, i), MU).then_inc(o_free, 1)
                if not last:
                    score_max(i + (NPAIR + 1), masks)
                    split_lo(Slot(N_AT + 1, 1, 2, i).next())
                dve.wait_ge(o_free, i + (NPAIR + 1) + 1)
                dve.wait_ge(ybh, i + 1)
                STT(dyn(ybL, i), dyn(szb, i), 1.0, dyn(ybH, i).bitcast(F32), MU, SU).then_inc(yb_done, 1)
            with dve.Fori(0, NPAIR - 1) as i:
                st.enter(i, 3)
                att(i, False)
                st.leave(NPAIR - 1)
            att(NPAIR - 1, True)

            with dve.Fori(0, KD // 2) as i:
                st.enter(i, 3)
                for s, tg in enumerate((tga, tgb)):
                    sl = Slot(N_AB, s, 2, i)
                    used(sl)
                    t0 = mark(STT(dyn(tg, i * 2), dyn(tg, i * 2), 1.0, AB[s][0][:], AD, MU))
                    STT(dyn(tg, i * 2 + 1), dyn(tg, i * 2 + 1), 1.0, AB[s][1][:], AD, MU).then_inc(gfree[s], 1)
                    split_lo(sl.next())
                need()
                freed(dve, sl)
                for e in range(2):
                    d = i * 2 + e
                    TT(dyn(tga, d), dyn(tga, d), dyn(tgb, d), AD).then_inc(mg_rdy, 1)
                for e in range(2):
                    d = i * 2 + e
                    dve.wait_ge(mgh, d + 1)
                    STT(dyn(hL, d), dyn(tga, d), 0.5, dyn(hH, d).bitcast(F32), MU, SU).then_inc(mg_done, 1)
                mark(v.memset(m8[:, 0, 0:1], 0.0))
                st.leave(KD // 2)

            mark(v.memset(gr[:], 0.0))
            need()

            def residual(i, j, last=False):
                sl, d, s = Slot(N_O2, j, 2, i), i * 2 + j, j % 2
                used(sl)
                STT(dyn(xT, d), PB[s][:], col(mod, d + 2 * KD), dyn(xT, d), MU, AD).then_inc(x3_rdy, 1)
                if not last:
                    dve.wait_ge(x3_rdy, d + 1)
                    v.memset(m8[:, 1, 0:1], 0.0).then_inc(gfree[s], 1)
                    split_lo(sl.next())

            def tokens(i):
                for s in range(2):
                    d = i * 2 + s
                    dve.wait_ge(xf_rdy, d + 1)
                    mark(TT(gr[:], gr[:], (t1, t2)[s][:], AD))
                    dve.wait_ge(xf_tr, d + 2)
                    v.tensor_copy(out_tok[:, :, bass.ds(d * P, P)], TBANK[s][:].rearrange("p (b n) -> p b n", b=TB)
                                  ).then_inc(ot_done, 1)
                    need()
            residual(0, 0)
            residual(0, 1)
            with dve.Fori(0, KD // 2 - 2) as i:
                st.enter(i, 2)
                residual(i, 2)
                tokens(i)
                residual(i, 3)
                st.leave(KD // 2 - 2)
            residual(KD // 2 - 1, 0, True)
            tokens(KD // 2 - 2)
            residual(KD // 2 - 1, 1, True)
            tokens(KD // 2 - 1)
            v.memset(m8[:, 0, 0:1], 0.0).then_inc(ssum, 1)
            dve.wait_ge(rr, 6)
            dve.wait_ge(ot_done, KD + 1)
            need(newton(sm[:, 16:20], PB[4][:, 0:4], 1.0 / D, sm[:, 12:16], sm[:, 8:12]))
            dve.nop().then_inc(r_fin, 1)
            for t in range(0, TB, 2):
                TS(out_tok[:, t, :], out_tok[:, t, :], sm[:, 16 + t:17 + t], None, MU).then_inc(fin[t], 1)


_INS = ["x", "g_mix", "w_in", "conv_w", "g_q", "g_k", "g_conv_out", "g_attn_out", "w_out", "g_ffn", "w_gate", "w_up",
        "w_down", "c_2", "norm_g_2", "w_mod_2", "b_mod_2", "w_in_2", "a_re_2", "a_im_2", "b_re_2", "b_im_2", "c_re_2",
        "c_im_2", "d_skip_2", "log_dt_2", "w_glu_2", "b_glu_2", "w_a_o_2", "w_b_o_2", "w_out_2", "final_g_2"]


def kernel(**inputs):
    import concourse.bacc as _bacc
    from concourse.bass_utils import run_bass_kernel_spmd as _run

    nc = _bacc.Bacc("TRN2", target_bir_lowering=False, num_devices=1)
    arrays, args = {}, []
    for name in _INS + ["constants"]:
        a = constants() if name == "constants" else np.ascontiguousarray(inputs[name])
        arrays[f"in_{name}_dram"] = a
        args.append(nc.dram_tensor(f"in_{name}_dram", a.shape, mybir.dt.from_np(a.dtype), kind="ExternalInput").ap())
    args.append(nc.dram_tensor("out_0_dram", (1, S, D), F32, kind="ExternalOutput").ap())
    program(nc, args)
    r = _run(nc, [arrays], core_ids=[0])
    return r.results[0]["out_0_dram"]
```
